# Optimizing a Trainium2 kernel written in Bass

```python
import math
import jax, jax.numpy as jnp
from jax import lax
import numpy as np

D_MODEL = 2048
BATCH = 1
SEQ = 256
DEPTH = 1

N_MEM = 256
NORM_EPS = 1e-6

SSD_WIDTH = D_MODEL // 2
SSD_HEAD_DIM = 64
SSD_HEADS = SSD_WIDTH // SSD_HEAD_DIM
SSD_GROUPS = 2
SSD_HEADS_PER_GROUP = SSD_HEADS // SSD_GROUPS
SSD_STATE = 128
SSD_CONV = 4
SSD_CHUNK = 128
SSD_CONV_DIM = SSD_WIDTH + 2 * SSD_GROUPS * SSD_STATE
SSD_IN = SSD_WIDTH + SSD_CONV_DIM + SSD_HEADS

RWKV_WIDTH = D_MODEL - SSD_WIDTH
RWKV_HEAD_DIM = 64
RWKV_HEADS = RWKV_WIDTH // RWKV_HEAD_DIM
RWKV_DECAY_RANK = 96
RWKV_AAA_RANK = 96
RWKV_GATE_RANK = 256
RWKV_IN = 3 * RWKV_WIDTH + RWKV_DECAY_RANK + RWKV_AAA_RANK + RWKV_GATE_RANK
RWKV_LN_EPS = 64e-5

MIX_WIDTH = SSD_WIDTH + RWKV_WIDTH
D_IN = SSD_IN + RWKV_IN

XATTN_HEADS = 4
XATTN_HEAD_DIM = D_MODEL // XATTN_HEADS

D_FF = 4 * D_MODEL


def rms_norm(x, g, eps=NORM_EPS):
    xf = x.astype(jnp.float32)
    y = xf * lax.rsqrt(jnp.mean(xf * xf, axis=-1, keepdims=True) + eps)
    return (y * g).astype(x.dtype)

def causal_depthwise_conv(u, w, b):
    y = lax.conv_general_dilated(
        u, w, window_strides=(1,), padding=[(w.shape[0] - 1, 0)],
        dimension_numbers=("NWC", "WIO", "NWC"), feature_group_count=u.shape[-1])
    return y + b

def ssd_mixer(u, conv_w, conv_b, dt_bias, a_log, d_skip, norm_g):
    f32 = jnp.float32
    bsz, seq, _ = u.shape
    G, E, P, N, Q = SSD_GROUPS, SSD_HEADS_PER_GROUP, SSD_HEAD_DIM, SSD_STATE, SSD_CHUNK
    nc = seq // Q
    z, xbc, dt = jnp.split(u, [SSD_WIDTH, SSD_WIDTH + SSD_CONV_DIM], axis=-1)
    xbc = jax.nn.silu(causal_depthwise_conv(xbc, conv_w, conv_b))
    xs, bm, cm = jnp.split(xbc, [SSD_WIDTH, SSD_WIDTH + G * N], axis=-1)
    xs = xs.astype(f32).reshape(bsz, nc, Q, G, E, P)
    bm = bm.astype(f32).reshape(bsz, nc, Q, G, N)
    cm = cm.astype(f32).reshape(bsz, nc, Q, G, N)
    dt = jax.nn.softplus(dt.astype(f32) + dt_bias.astype(f32))
    a = -jnp.exp(a_log.astype(f32))
    dt_c = dt.reshape(bsz, nc, Q, G, E)
    xdt = xs * dt_c[..., None]
    da = jnp.transpose(dt_c * a.reshape(G, E), (0, 1, 3, 4, 2))
    cs = jnp.cumsum(da, axis=-1)
    causal = jnp.tril(jnp.ones((Q, Q), dtype=bool))
    seg = cs[..., :, None] - cs[..., None, :]
    lmat = jnp.where(causal, jnp.exp(jnp.where(causal, seg, 0.0)), 0.0)
    cb = jnp.einsum('bclgn,bcsgn->bcgls', cm, bm)
    y_diag = jnp.einsum('bcgls,bcgels,bcsgep->bclgep', cb, lmat, xdt)
    decay_to_end = jnp.exp(cs[..., -1:] - cs)
    chunk_states = jnp.einsum('bcsgn,bcges,bcsgep->bcgepn', bm, decay_to_end, xdt)
    chunk_decay = jnp.exp(cs[..., -1])

    def carry_state(h, inp):
        st, dec = inp
        return h * dec[..., None, None] + st, h

    h0 = jnp.zeros((bsz, G, E, P, N), f32)
    _, start_states = lax.scan(carry_state, h0,
                               (jnp.moveaxis(chunk_states, 1, 0), jnp.moveaxis(chunk_decay, 1, 0)))
    start_states = jnp.moveaxis(start_states, 0, 1)
    y_off = jnp.einsum('bclgn,bcgepn,bcgel->bclgep', cm, start_states, jnp.exp(cs))
    y = y_diag + y_off + xs * d_skip.astype(f32).reshape(G, E, 1)
    y = y.reshape(bsz, seq, SSD_WIDTH) * jax.nn.silu(z.astype(f32))
    yg = y.reshape(bsz, seq, G, SSD_WIDTH // G)
    yg = yg * lax.rsqrt(jnp.mean(yg * yg, axis=-1, keepdims=True) + NORM_EPS)
    y = yg.reshape(bsz, seq, SSD_WIDTH) * norm_g
    return y.astype(u.dtype)

def rwkv7_mixer(u, mu, w0, w2, a0, a2, g2, k_k, k_a, r_k, ln_w, ln_b):
    f32 = jnp.float32
    bsz, seq, _ = u.shape
    H, N, W = RWKV_HEADS, RWKV_HEAD_DIM, RWKV_WIDTH
    uf = u.astype(f32)
    u_prev = jnp.pad(uf, ((0, 0), (1, 0), (0, 0)))[:, :-1]
    uf = uf + (u_prev - uf) * mu
    r, k, v, pw, pa, pg = jnp.split(
        uf, [W, 2 * W, 3 * W, 3 * W + RWKV_DECAY_RANK,
             3 * W + RWKV_DECAY_RANK + RWKV_AAA_RANK], axis=-1)
    w_log = -jax.nn.softplus(-(w0 + jnp.tanh(pw) @ w2)) - 0.5
    decay = jnp.exp(-jnp.exp(w_log))
    iclr = jax.nn.sigmoid(a0 + pa @ a2)
    gate = jax.nn.sigmoid(pg) @ g2
    heads = lambda t: t.reshape(bsz, seq, H, N)
    kk = heads(k * k_k)
    kk = kk / jnp.maximum(jnp.sqrt(jnp.sum(kk * kk, axis=-1, keepdims=True)), 1e-12)
    k = k * (1.0 + (iclr - 1.0) * k_a)
    r, k, v, decay, iclr = heads(r), heads(k), heads(v), heads(decay), heads(iclr)

    def step(state, inp):
        r_t, w_t, k_t, v_t, kk_t, a_t = inp
        sa = jnp.einsum('bhij,bhj->bhi', state, -kk_t)
        state = (state * w_t[:, :, None, :]
                 + sa[..., None] * (kk_t * a_t)[:, :, None, :]
                 + v_t[..., None] * k_t[:, :, None, :])
        return state, jnp.einsum('bhij,bhj->bhi', state, r_t)

    seq_first = lambda t: jnp.moveaxis(t, 1, 0)
    s0 = jnp.zeros((bsz, H, N, N), f32)
    _, y = lax.scan(step, s0, (seq_first(r), seq_first(decay), seq_first(k),
                               seq_first(v), seq_first(kk), seq_first(iclr)))
    y = jnp.moveaxis(y, 0, 1)
    mean = jnp.mean(y, axis=-1, keepdims=True)
    var = jnp.mean(jnp.square(y - mean), axis=-1, keepdims=True)
    y = ((y - mean) * lax.rsqrt(var + RWKV_LN_EPS)).reshape(bsz, seq, W) * ln_w + ln_b
    bonus = jnp.sum(r * k * r_k, axis=-1, keepdims=True) * v
    y = (y + bonus.reshape(bsz, seq, W)) * gate
    return y.astype(u.dtype)

def memory_cross_attention(h, m, wq, wk, wv, wo):
    bsz, seq, _ = h.shape
    q = (h @ wq).reshape(bsz, seq, XATTN_HEADS, XATTN_HEAD_DIM)
    k = (m @ wk).reshape(bsz, m.shape[1], XATTN_HEADS, XATTN_HEAD_DIM)
    v = (m @ wv).reshape(bsz, m.shape[1], XATTN_HEADS, XATTN_HEAD_DIM)
    scores = jnp.einsum('bshd,bmhd->bhsm', q, k).astype(jnp.float32) * (XATTN_HEAD_DIM ** -0.5)
    p = jax.nn.softmax(scores, axis=-1).astype(v.dtype)
    o = jnp.einsum('bhsm,bmhd->bshd', p, v).reshape(bsz, seq, D_MODEL)
    return o @ wo

def first_inputs(seed: int = 0) -> dict:
    key = jax.random.key(seed)
    ks = iter(jax.random.split(key, 40))
    nrm = lambda shape, scale: jax.random.normal(next(ks), shape, jnp.float32) * scale
    uni = lambda shape, lo, hi: jax.random.uniform(next(ks), shape, jnp.float32, lo, hi)
    L = DEPTH
    dt0 = jnp.exp(uni((L, SSD_HEADS), math.log(1e-3), math.log(1e-1)))
    return {
        "x": nrm((BATCH, SEQ, D_MODEL), 1.0),
        "mem": nrm((BATCH, N_MEM, D_MODEL), 1.0),
        "norm_mix_g": 1.0 + nrm((L, D_MODEL), 0.02),
        "w_in": nrm((L, D_MODEL, D_IN), D_MODEL ** -0.5),
        "ssd_conv_w": nrm((L, SSD_CONV, 1, SSD_CONV_DIM), SSD_CONV ** -0.5),
        "ssd_conv_b": nrm((L, SSD_CONV_DIM), 0.01),
        "ssd_dt_bias": dt0 + jnp.log(-jnp.expm1(-dt0)),
        "ssd_a_log": jnp.log(uni((L, SSD_HEADS), 1.0, 16.0)),
        "ssd_d": 1.0 + nrm((L, SSD_HEADS), 0.1),
        "ssd_norm_g": 1.0 + nrm((L, SSD_WIDTH), 0.02),
        "rwkv_mu": uni((L, RWKV_IN), 0.0, 1.0),
        "rwkv_w0": uni((L, RWKV_WIDTH), -6.0, -1.0),
        "rwkv_w2": nrm((L, RWKV_DECAY_RANK, RWKV_WIDTH), 0.5 * RWKV_DECAY_RANK ** -0.5),
        "rwkv_a0": nrm((L, RWKV_WIDTH), 0.1),
        "rwkv_a2": nrm((L, RWKV_AAA_RANK, RWKV_WIDTH), RWKV_AAA_RANK ** -0.5),
        "rwkv_g2": nrm((L, RWKV_GATE_RANK, RWKV_WIDTH), RWKV_GATE_RANK ** -0.5),
        "rwkv_k_k": 0.85 + nrm((L, RWKV_WIDTH), 0.05),
        "rwkv_k_a": 1.0 + nrm((L, RWKV_WIDTH), 0.05),
        "rwkv_r_k": nrm((L, RWKV_HEADS, RWKV_HEAD_DIM), 0.1),
        "rwkv_ln_w": 1.0 + nrm((L, RWKV_WIDTH), 0.02),
        "rwkv_ln_b": nrm((L, RWKV_WIDTH), 0.01),
        "w_out": nrm((L, MIX_WIDTH, D_MODEL), MIX_WIDTH ** -0.5),
        "norm_x_g": 1.0 + nrm((L, D_MODEL), 0.02),
        "norm_mem_g": 1.0 + nrm((L, D_MODEL), 0.02),
        "xattn_wq": nrm((L, D_MODEL, D_MODEL), D_MODEL ** -0.5),
        "xattn_wk": nrm((L, D_MODEL, D_MODEL), D_MODEL ** -0.5),
        "xattn_wv": nrm((L, D_MODEL, D_MODEL), D_MODEL ** -0.5),
        "xattn_wo": nrm((L, D_MODEL, D_MODEL), D_MODEL ** -0.5),
        "norm_ffn_g": 1.0 + nrm((L, D_MODEL), 0.02),
        "ffn_w1": nrm((L, D_MODEL, D_FF), D_MODEL ** -0.5),
        "ffn_w2": nrm((L, D_FF, D_MODEL), D_FF ** -0.5),
        "final_norm_g": 1.0 + nrm((D_MODEL,), 0.02),
    }

def first_block(x, mem, norm_mix_g, w_in, ssd_conv_w, ssd_conv_b, ssd_dt_bias, ssd_a_log,
              ssd_d, ssd_norm_g, rwkv_mu, rwkv_w0, rwkv_w2, rwkv_a0, rwkv_a2, rwkv_g2,
              rwkv_k_k, rwkv_k_a, rwkv_r_k, rwkv_ln_w, rwkv_ln_b, w_out, norm_x_g,
              norm_mem_g, xattn_wq, xattn_wk, xattn_wv, xattn_wo, norm_ffn_g, ffn_w1,
              ffn_w2, final_norm_g):
    for l in range(DEPTH):
        h = rms_norm(x, norm_mix_g[l])
        u = h @ w_in[l]
        y_ssd = ssd_mixer(u[..., :SSD_IN], ssd_conv_w[l], ssd_conv_b[l], ssd_dt_bias[l],
                          ssd_a_log[l], ssd_d[l], ssd_norm_g[l])
        y_rwkv = rwkv7_mixer(u[..., SSD_IN:], rwkv_mu[l], rwkv_w0[l], rwkv_w2[l], rwkv_a0[l],
                             rwkv_a2[l], rwkv_g2[l], rwkv_k_k[l], rwkv_k_a[l], rwkv_r_k[l],
                             rwkv_ln_w[l], rwkv_ln_b[l])
        x = x + jnp.concatenate([y_ssd, y_rwkv], axis=-1) @ w_out[l]
        h = rms_norm(x, norm_x_g[l])
        m = rms_norm(mem, norm_mem_g[l])
        x = x + memory_cross_attention(h, m, xattn_wq[l], xattn_wk[l], xattn_wv[l], xattn_wo[l])
        h = rms_norm(x, norm_ffn_g[l])
        x = x + jnp.square(jax.nn.relu(h @ ffn_w1[l])) @ ffn_w2[l]
    return rms_norm(x, final_norm_g)


CHUNK = 64
Q_BLOCK = 128
D_MIX = D_MODEL
HGRN_WIDTH = D_MIX // 2
HGRN_DK = 128
HGRN_HEADS = HGRN_WIDTH // HGRN_DK
HGRN_DV = HGRN_WIDTH // HGRN_HEADS
FOX_WIDTH = D_MIX - HGRN_WIDTH
FOX_HEAD_DIM = 128
FOX_HEADS = FOX_WIDTH // FOX_HEAD_DIM
D_FF_2 = ((8 * D_MODEL // 3 + 255) // 256) * 256
CONV_WIDTH = 3
EPS = 1e-6
FOX_GATE_BIAS_OFFSET = 2.0
IN_SIZES = (HGRN_HEADS * HGRN_DK, HGRN_HEADS * HGRN_DK, HGRN_WIDTH, HGRN_WIDTH,
            FOX_WIDTH, FOX_WIDTH, FOX_WIDTH, FOX_HEADS)
D_IN_2 = sum(IN_SIZES)


def rmsnorm(x, gain):
    x32 = x.astype(jnp.float32)
    y = x32 * lax.rsqrt(jnp.mean(x32 * x32, axis=-1, keepdims=True) + EPS) * gain.astype(jnp.float32)
    return y.astype(x.dtype)

def gla_chunkwise(q, k, v, logf):
    B, H, L, DK = q.shape
    DV = v.shape[-1]
    N = L // CHUNK
    r = lambda t: t.reshape(B, H, N, CHUNK, t.shape[-1])
    q, k, v, logf = r(q), r(k), r(v), r(logf)
    b = jnp.cumsum(logf, axis=-2)
    b_last = b[..., -1:, :]
    q_dec = q * jnp.exp(b)
    k_dec = k * jnp.exp(-b)
    k_end = k * jnp.exp(b_last - b)
    mask = jnp.tril(jnp.ones((CHUNK, CHUNK), dtype=bool))
    attn = jnp.einsum('bhnck,bhnsk->bhncs', q_dec, k_dec)
    attn = jnp.where(mask, attn, 0.0)
    o_intra = jnp.einsum('bhncs,bhnsv->bhncv', attn, v)
    chunk_decay = jnp.exp(b_last[..., 0, :])

    def step(S, xs):
        qd, ke, vv, dc = xs
        o = jnp.einsum('bhck,bhkv->bhcv', qd, S)
        S = dc[..., None] * S + jnp.einsum('bhck,bhcv->bhkv', ke, vv)
        return S, o

    xs = (jnp.moveaxis(q_dec, 2, 0), jnp.moveaxis(k_end, 2, 0),
          jnp.moveaxis(v, 2, 0), jnp.moveaxis(chunk_decay, 2, 0))
    S0 = jnp.zeros((B, H, DK, DV), jnp.float32)
    _, o_inter = lax.scan(step, S0, xs)
    o = o_intra + jnp.moveaxis(o_inter, 0, 2)
    return o.reshape(B, H, L, DV)

def hgrn2_mixer(q, f_logit, inp, g, lb, norm_gain):
    B, L, _ = q.shape
    dt = q.dtype
    heads = lambda t, d: t.reshape(B, L, HGRN_HEADS, d).transpose(0, 2, 1, 3).astype(jnp.float32)
    qh = heads(q, HGRN_DK) * (HGRN_DK ** -0.5)
    zh = heads(f_logit, HGRN_DK)
    vh = heads(inp, HGRN_DV)
    lbh = lb.astype(jnp.float32).reshape(HGRN_HEADS, HGRN_DK)[None, :, None, :]
    f = lbh + (1.0 - lbh) * jax.nn.sigmoid(zh)
    kh = 1.0 - f
    o = gla_chunkwise(qh, kh, vh, jnp.log(f))
    o = o * lax.rsqrt(jnp.mean(o * o, axis=-1, keepdims=True) + EPS) * norm_gain.astype(jnp.float32)
    o = o * jax.nn.silu(heads(g, HGRN_DV))
    return o.transpose(0, 2, 1, 3).reshape(B, L, HGRN_WIDTH).astype(dt)

def fox_mixer(q, k, v, f_logit, gate_bias):
    B, L, _ = q.shape
    dt = q.dtype
    heads = lambda t: t.reshape(B, L, FOX_HEADS, FOX_HEAD_DIM).transpose(0, 2, 1, 3)
    qh, kh, vh = heads(q), heads(k), heads(v)
    logf = jax.nn.log_sigmoid(f_logit.astype(jnp.float32) + gate_bias.astype(jnp.float32))
    c = jnp.cumsum(logf, axis=1).transpose(0, 2, 1)
    scale = FOX_HEAD_DIM ** -0.5
    kpos = jnp.arange(L)

    def one_block(blk):
        start = blk * Q_BLOCK
        qb = lax.dynamic_slice_in_dim(qh, start, Q_BLOCK, axis=2)
        cb = lax.dynamic_slice_in_dim(c, start, Q_BLOCK, axis=2)
        s = jnp.einsum('bhqd,bhkd->bhqk', qb, kh).astype(jnp.float32) * scale
        s = s + cb[..., :, None] - c[..., None, :]
        qpos = start + jnp.arange(Q_BLOCK)
        s = jnp.where(kpos[None, :] <= qpos[:, None], s, -jnp.inf)
        p = jax.nn.softmax(s, axis=-1)
        return jnp.einsum('bhqk,bhkd->bhqd', p.astype(vh.dtype), vh)

    out = lax.map(one_block, jnp.arange(L // Q_BLOCK))
    out = out.transpose(1, 0, 3, 2, 4).reshape(B, L, FOX_WIDTH)
    return out.astype(dt)

def conv_ffn(h, w_gate, w_up, conv_w, conv_b, w_down):
    L = h.shape[1]
    a = h @ w_gate
    a_pad = jnp.pad(a, ((0, 0), (CONV_WIDTH - 1, 0), (0, 0)))
    a = sum(conv_w[j] * a_pad[:, j:j + L] for j in range(CONV_WIDTH)) + conv_b
    return (jax.nn.silu(a) * (h @ w_up)) @ w_down

def second_inputs(seed: int = 0) -> dict:
    key = jax.random.key(seed)
    ks = jax.random.split(key, 16)
    nrm = lambda k, shape, s: jax.random.normal(k, shape, jnp.float32) * s
    return {
        'x': nrm(ks[0], (BATCH, SEQ, D_MODEL), 1.0),
        'norm1_gain': 1.0 + nrm(ks[1], (DEPTH, D_MODEL), 0.02),
        'w_in': nrm(ks[2], (DEPTH, D_MODEL, D_IN_2), D_MODEL ** -0.5),
        'hgrn_lb_param': nrm(ks[3], (DEPTH + 1, HGRN_HEADS * HGRN_DK), 0.5),
        'hgrn_norm_gain': 1.0 + nrm(ks[4], (DEPTH, HGRN_DV), 0.02),
        'fox_gate_bias': FOX_GATE_BIAS_OFFSET + nrm(ks[5], (DEPTH, FOX_HEADS), 0.1),
        'w_out': nrm(ks[6], (DEPTH, D_MIX, D_MODEL), D_MIX ** -0.5),
        'norm2_gain': 1.0 + nrm(ks[7], (DEPTH, D_MODEL), 0.02),
        'w_ffn_gate': nrm(ks[8], (DEPTH, D_MODEL, D_FF_2), D_MODEL ** -0.5),
        'w_ffn_up': nrm(ks[9], (DEPTH, D_MODEL, D_FF_2), D_MODEL ** -0.5),
        'ffn_conv_w': nrm(ks[10], (DEPTH, CONV_WIDTH, D_FF_2), CONV_WIDTH ** -0.5),
        'ffn_conv_b': nrm(ks[11], (DEPTH, D_FF_2), 0.02),
        'w_ffn_down': nrm(ks[12], (DEPTH, D_FF_2, D_MODEL), D_FF_2 ** -0.5),
        'final_norm_gain': 1.0 + nrm(ks[13], (D_MODEL,), 0.02),
    }

def second_block(x, norm1_gain, w_in, hgrn_lb_param, hgrn_norm_gain, fox_gate_bias, w_out,
              norm2_gain, w_ffn_gate, w_ffn_up, ffn_conv_w, ffn_conv_b, w_ffn_down,
              final_norm_gain):
    split_points = [int(v) for v in np.cumsum(IN_SIZES)[:-1]]
    lb_all = jnp.cumsum(jax.nn.softmax(hgrn_lb_param.astype(jnp.float32), axis=0), axis=0)
    for l in range(DEPTH):
        h = rmsnorm(x, norm1_gain[l])
        proj = h @ w_in[l]
        q_a, f_a, i_a, g_a, q_b, k_b, v_b, f_b = jnp.split(proj, split_points, axis=-1)
        o_a = hgrn2_mixer(q_a, f_a, i_a, g_a, lb_all[l], hgrn_norm_gain[l])
        o_b = fox_mixer(q_b, k_b, v_b, f_b, fox_gate_bias[l])
        x = x + jnp.concatenate([o_a, o_b], axis=-1) @ w_out[l]
        h = rmsnorm(x, norm2_gain[l])
        x = x + conv_ffn(h, w_ffn_gate[l], w_ffn_up[l], ffn_conv_w[l], ffn_conv_b[l], w_ffn_down[l])
    return rmsnorm(x, final_norm_gain)


def setup_inputs(seed=0):
    out = dict(first_inputs(seed))
    for name, value in second_inputs(seed + 1).items():
        if name != "x":
            out[name + "_2"] = value
    return out


def reference(
    x, mem, norm_mix_g, w_in, ssd_conv_w, ssd_conv_b, ssd_dt_bias, ssd_a_log, ssd_d, ssd_norm_g,
    rwkv_mu, rwkv_w0, rwkv_w2, rwkv_a0, rwkv_a2, rwkv_g2, rwkv_k_k, rwkv_k_a, rwkv_r_k,
    rwkv_ln_w, rwkv_ln_b, w_out, norm_x_g, norm_mem_g, xattn_wq, xattn_wk, xattn_wv, xattn_wo,
    norm_ffn_g, ffn_w1, ffn_w2, final_norm_g, norm1_gain_2, w_in_2, hgrn_lb_param_2,
    hgrn_norm_gain_2, fox_gate_bias_2, w_out_2, norm2_gain_2, w_ffn_gate_2, w_ffn_up_2,
    ffn_conv_w_2, ffn_conv_b_2, w_ffn_down_2, final_norm_gain_2,
):
    x = first_block(
        x, mem, norm_mix_g, w_in, ssd_conv_w, ssd_conv_b, ssd_dt_bias, ssd_a_log, ssd_d,
        ssd_norm_g, rwkv_mu, rwkv_w0, rwkv_w2, rwkv_a0, rwkv_a2, rwkv_g2, rwkv_k_k, rwkv_k_a,
        rwkv_r_k, rwkv_ln_w, rwkv_ln_b, w_out, norm_x_g, norm_mem_g, xattn_wq, xattn_wk,
        xattn_wv, xattn_wo, norm_ffn_g, ffn_w1, ffn_w2, final_norm_g,
    )
    return second_block(
        x, norm1_gain_2, w_in_2, hgrn_lb_param_2, hgrn_norm_gain_2, fox_gate_bias_2, w_out_2,
        norm2_gain_2, w_ffn_gate_2, w_ffn_up_2, ffn_conv_w_2, ffn_conv_b_2, w_ffn_down_2,
        final_norm_gain_2,
    )


_drawn_inputs = setup_inputs


def setup_inputs(seed=0):
    import zlib

    import numpy as np

    out = dict(_drawn_inputs(seed))
    spreads = {}
    factors = {'ssd_conv_b': 4.887,
     'ssd_norm_g': 3.593,
     'rwkv_w2': 5.312,
     'rwkv_a0': 2.731,
     'rwkv_k_k': 3.321,
     'rwkv_ln_w': 5.076,
     'rwkv_ln_b': 8.0,
     'norm_x_g': 8.0,
     'norm_mem_g': 8.0,
     'hgrn_norm_gain_2': 7.808,
     'fox_gate_bias_2': 25.328,
     'norm2_gain_2': 4.166,
     'ffn_conv_b_2': 6.182,
     'final_norm_gain_2': 7.732,
     'norm_ffn_g': 5.724}
    for name, (base, spread) in spreads.items():
        noise = np.random.default_rng([zlib.crc32(name.encode()), seed]).standard_normal(out[name].shape)
        drawn = base * np.exp(spread * noise) if base else spread * noise
        out[name] = __import__('jax').numpy.asarray(drawn.astype(out[name].dtype))
    for name, factor in factors.items():
        out[name] = (out[name] * factor).astype(out[name].dtype)
    return out
```

```python
from contextlib import ExitStack

import concourse.bass as bass
from concourse import mybir

F32 = mybir.dt.float32
F32R = mybir.dt.float32r
ALU = mybir.AluOpType
ACT = mybir.ActivationFunctionType
AX = mybir.AxisListType
ds = bass.ds

P = 128
SEQ = 256
NT = SEQ // P
D = 2048
KD = D // P
EPS = 1e-6
NEG = -1e30

SSD_W, SSD_H, SSD_G, SSD_N, SSD_CONV = 1024, 16, 2, 128, 4
XBC = SSD_W + 2 * SSD_G * SSD_N
RW = 1024
RP = RW // P
RC = 64
NRC = SEQ // RC
LORA = 96
LN_EPS = 64e-5
XH_, XD = 4, 512
FF1, FF2 = 8192, 5632
GH = 8
HCH = 64

CREDIT = 64

STEPS = {
    "w_in_rkv": (0, 6, 0, 0),
    "rwkv_chunks": (232, 21, 13, 2),
    "xattn_heads": (20, 6, 5, 1),
    "ffn1_up0": (0, 4, 2, 0),
    "ffn1_up1": (0, 4, 2, 0),
    "ffn1_up2": (0, 4, 2, 0),
    "ffn1_up3": (0, 4, 2, 0),
    "hgrn_heads": (14, 9, 8, 3),
    "fox_heads": (11, 6, 5, 2),
    "ffn2_up0": (0, 8, 2, 0),
    "ffn2_up1": (0, 8, 2, 0),
    "ffn2_up2": (0, 8, 2, 0),
}


class Lane:

    def __init__(self, eng, sem, key):
        self.eng, self.sem, self.key = eng, sem, key
        self.const, self.terms = CREDIT, []

    def value(self):
        v = self.const
        for i, per in self.terms:
            v = i * per + v
        return v

    def tok(self):
        return (self.sem, self.value())

    def __call__(self, ins):
        ins.then_inc(self.sem, 1)
        self.const += 1
        return self.tok()

    def wait(self, *toks):
        for sem, v in toks:
            self.eng.wait_ge(sem, v)

    def seq(self, ins):
        t = self(ins)
        self.wait(t)
        return t


class Prog:
    def __init__(self, nc, ctx, ins, out):
        self.nc, self.ctx, self.i, self.out = nc, ctx, ins, out
        sem = lambda n: ctx.enter_context(nc.semaphore(n))
        self.newsem = sem
        self.T = Lane(nc.tensor, sem("tensor_done"), "T")
        self.V = Lane(nc.vector, sem("vector_done"), "V")
        self.S = Lane(nc.scalar, sem("scalar_done"), "S")
        self.G = Lane(nc.gpsimd, sem("gpsimd_done"), "G")
        self.lanes = [self.T, self.V, self.S, self.G]
        self.ring_full = [sem(f"ring_full{q}") for q in range(4)]
        self.s_hi, self.s_lo = sem("weights_hi"), sem("weights_lo")
        self.s_mm, self.s_evac = sem("half_multiplied"), sem("block_evacuated")
        self.tile_const, self.tile_terms = 0, []
        self.blk_const, self.blk_terms = 0, []
        self.s_par = [sem(f"params{k}") for k in range(12)]
        self.par_n = [0] * 12
        for s, e in ((self.T.sem, nc.tensor), (self.s_mm, nc.tensor), (self.V.sem, nc.vector),
                     (self.s_lo, nc.vector), (self.S.sem, nc.scalar), (self.s_hi, nc.scalar),
                     (self.s_evac, nc.vector), (self.G.sem, nc.gpsimd)):
            e.sem_inc(s, CREDIT)
        sb = lambda n, s, d=F32: ctx.enter_context(nc.sbuf_tensor(n, s, d))
        self.sb = sb
        self.raw = sb("raw", [P, 4, 4, 512])
        self.whi = sb("whi", [P, 4, 2, 512], F32R)
        self.wlo = sb("wlo", [P, 4, 2, 512], F32R)
        self.XH = sb("XH", [P, KD, SEQ], F32R)
        self.XL = sb("XL", [P, KD, SEQ], F32R)
        self.PS = ctx.enter_context(nc.psum_tensor("PS", [P, 8, 512], F32))

    def loop(self, n, name, tiles=0, blks=0):
        return LoopScope(self, n, name, tiles, blks)

    def view(self, off, *shape):
        n = 1
        for s in shape:
            n *= s
        assert off + n <= self.arena_words, (off + n, self.arena_words)
        v = self.arena[:, off:off + n]
        if len(shape) == 2:
            v = v.rearrange("p (a b) -> p a b", a=shape[0])
        if len(shape) == 3:
            v = v.rearrange("p (a b c) -> p a b c", a=shape[0], b=shape[1])
        return v

    def join(self, *extra):
        toks = [l.tok() for l in self.lanes] + [(self.s_evac, CREDIT + self.blk_const),
                                                (self.s_mm, CREDIT + 2 * self.tile_const)] + list(extra)
        for l in self.lanes:
            for t in toks:
                if t[0] is not l.sem:
                    l.wait(t)
            l.wait(l.tok())

    def load(self, k, dst, src, eng=None):
        (eng or self.nc.scalar).dma_start(dst, src).then_inc(self.s_par[k], 16)
        self.par_n[k] += 16
        return (self.s_par[k], self.par_n[k])

    def tile(self):
        v = self.tile_const
        for i, per in self.tile_terms:
            v = i * per + v
        return v

    def blk(self):
        v = self.blk_const
        for i, per in self.blk_terms:
            v = i * per + v
        return v

    def block(self, spec, g, par, prev):
        nc, T, V, S = self.nc, self.T, self.V, self.S
        w, k0, kt, xh, xl, mode, col, widths = (spec[k] for k in
                                                ("w", "k0", "kt", "xh", "xl", "mode", "col", "widths"))
        c0 = col(g)
        ncol = sum(widths)
        nq = (kt + 3) // 4
        ps = self.PS[:, 2 * par:2 * par + 2, :]
        b = self.blk()
        for q in range(nq):
            t = self.tile()
            slot = self.tile_const % 4
            nc.sync.wait_ge(self.s_lo, 2 * t - 6 + CREDIT)
            nc.sync.dma_start(self.raw[:, slot, :, 0:ncol],
                              w[k0 + 512 * q:k0 + 512 * q + 512, ds(c0, ncol)]
                              .rearrange("(a p) n -> p a n", p=P)).then_inc(self.ring_full[slot], 16)
            for u in range(2):
                h = 2 * t + u
                hs = (2 * self.tile_const + u) % 4
                raw = self.raw[:, slot, 2 * u:2 * u + 2, 0:ncol]
                hi, lo = self.whi[:, hs, :, 0:ncol], self.wlo[:, hs, :, 0:ncol]
                nc.scalar.wait_ge(self.ring_full[slot], 4 * (t - slot) + 16)
                nc.scalar.wait_ge(self.s_mm, h - 3 + CREDIT)
                nc.scalar.activation(hi, raw, ACT.Copy).then_inc(self.s_hi, 1)
                nc.vector.wait_ge(self.s_hi, h + 1 + CREDIT)
                nc.vector.tensor_tensor(lo, raw, hi.bitcast(F32), ALU.subtract).then_inc(self.s_lo, 1)
                if q == 0 and u == 0:
                    nc.tensor.wait_ge(self.s_evac, b - 1 + CREDIT)
                nc.tensor.wait_ge(self.s_lo, h + 1 + CREDIT)
                for a in range(2):
                    k = 4 * q + 2 * u + a
                    for n, (wt, xt) in enumerate(((self.whi, xh), (self.whi, xl), (self.wlo, xh))):
                        first, last = k == 0 and n == 0, k == kt - 1 and n == 2
                        if mode == "tok":
                            for tt in range(NT):
                                mm = nc.tensor.matmul(ps[:, tt, 0:ncol], xt[:, k, tt * P:(tt + 1) * P],
                                                      wt[:, hs, a, 0:ncol], start=first, stop=last)
                        else:
                            o = 0
                            for f, wd in enumerate(widths):
                                mm = nc.tensor.matmul(ps[0:wd, f // 2, (f % 2) * SEQ:(f % 2) * SEQ + SEQ],
                                                      wt[:, hs, a, o:o + wd], xt[:, k, :],
                                                      start=first and f % 2 == 0, stop=last,
                                                      skip_group_check=True)
                                o += wd
                mm.then_inc(self.s_mm, 1)
            self.tile_const += 1
            if q == min(1, nq - 1) and prev is not None:
                prev()
        self.blk_const += 1

    def stream(self, name, groups, specs):
        L = len(specs)
        assert L % 2 == 0 or groups == 1

        def evac(j, g, tile_end, blk):
            sp = specs[j]
            par = j % 2
            ps = self.PS[:, 2 * par:2 * par + 2, :]
            if sp["mode"] == "feat":
                ps = ps.rearrange("p a (f t) -> p (a f) t", t=SEQ)
            sp["evac"](g, ps, (self.s_mm, 2 * tile_end + CREDIT))

        def group(g, first):
            for j in range(L):
                if j == 0:
                    prev = None if first else self._prev(evac, L - 1, g - 1)
                else:
                    prev = self._prev(evac, j - 1, g)
                self.block(specs[j], g, j % 2, prev)

        group(0, True)
        nt = sum((s["kt"] + 3) // 4 for s in specs)
        if groups > 1:
            with self.loop(groups - 1, name, nt, L) as i:
                group(i + 1, False)
        evac(L - 1, groups - 1, self.tile(), None)

    def _prev(self, evac, j, g):
        end = self.tile()
        return lambda: evac(j, g, end, None)

    def done_evac(self, ins):
        ins.then_inc(self.s_evac, 1)

    def constants(self):
        nc, G, V, sb = self.nc, self.G, self.V, self.sb
        self.ident = sb("ident", [P, P])
        self.ones = sb("ones", [P, P])
        self.triu = sb("triu", [P, P])
        self.negl = sb("negl", [P, P])
        self.negu = sb("negu", [P, P])
        self.sel = sb("sel", [P, RP, 16])
        self.selT = sb("selT", [16, RP, 2])
        self.m_in = sb("m_in", [P, P])
        self.m_st = sb("m_st", [P, P])
        self.m_d = sb("m_d", [P, P])
        self.m_o = sb("m_o", [P, P])
        self.m_dT = sb("m_dT", [P, P])
        self.m_ic = sb("m_ic", [P, RC])
        self.rst = sb("rst", [P, SEQ])

        def sel(dst, src, pattern, base, cm, op, fill):
            return G.seq(nc.gpsimd.affine_select(out=dst, in_=src, pattern=pattern, compare_op=op,
                                                 fill=fill, base=base, channel_multiplier=cm))
        ge, ne = ALU.is_ge, ALU.not_equal
        for t, v in ((self.ident, 0.0), (self.ones, 1.0), (self.triu, 1.0), (self.negl, 0.0),
                     (self.negu, 0.0), (self.sel, 1.0), (self.selT, 1.0), (self.m_in, 1.0),
                     (self.m_st, 1.0), (self.m_d, -1.0), (self.m_o, -1.0), (self.m_dT, -1.0),
                     (self.m_ic, 1.0), (self.rst, 1.0)):
            ap = t[:, :] if len(t.shape) == 2 else t[:, :, :]
            G.seq(nc.gpsimd.memset(ap, v))
        I, one = self.ident[:, :], [[1, P]]
        sel(I, I, [[-1, P]], 0, 1, ne, 1.0)
        up = lambda t, fill, base=0: sel(t[:, :], t[:, :], one, base, -1, ge, fill)
        up(self.triu, 0.0)
        up(self.negl, NEG)
        sel(self.negu[:, :], self.negu[:, :], [[-1, P]], 0, 1, ge, NEG)
        up(self.m_in, 0.0)
        up(self.m_st, 0.0, -1)
        up(self.m_d, 0.0, -1)
        up(self.m_o, 0.0, -1)
        sel(self.m_dT[:, :], self.m_dT[:, :], [[-1, P]], -1, 1, ge, 0.0)

        def same_block(t, n):
            for lo, cm, st in ((0, 1, -n), (n - 1, -1, n)):
                v = t[:, :].rearrange("p (j e) -> p j e", e=n)
                sel(v, v, [[st, P // n], [0, n]], lo, cm, ge, 0.0)
        same_block(self.m_in, RC)
        same_block(self.m_st, RC)
        same_block(self.m_d, 16)
        same_block(self.m_dT, 16)
        same_block(self.m_o, RC)
        V.wait(G.tok())
        V.seq(nc.vector.tensor_tensor(self.m_o[:, :], self.m_o[:, :], self.m_d[:, :], ALU.subtract))
        for t, pat, cm in ((self.sel[:, :, :], [[128, RP], [-64, 16]], 1),
                           (self.selT[:, :, :], [[-2, RP], [-1, 2]], 1)):
            if pat[0][0] == 128:
                sel(t, t, pat, 0, 1, ge, 0.0)
                sel(t, t, [[-128, RP], [64, 16]], 63, -1, ge, 0.0)
            else:
                sel(t, t, pat, 0, 1, ge, 0.0)
                sel(t, t, [[2, RP], [1, 2]], 0, -1, ge, 0.0)
        for hp in range(2):
            v = self.m_ic[hp * 64:hp * 64 + 64, :]
            sel(v, v, [[1, RC]], 0, -1, ge, 0.0)
        v = self.rst[:, :].rearrange("p (c e) -> p c e", e=RC)
        sel(v, v, [[0, NRC], [1, RC]], -1, 0, ge, 0.0)

    def params(self):
        nc, T, S, i = self.nc, self.T, self.S, self.i
        groups = [
            [("norm_mix_g", 16), ("norm_x_g", 16), ("norm_mem_g", 16), ("norm_ffn_g", 16),
             ("norm1_gain_2", 16), ("norm2_gain_2", 16), ("hgrn_lb_param_2", 16), ("hgrn_norm_gain_2", 1)],
            [("ssd_conv_w", 48), ("ssd_conv_b", 12), ("ssd_norm_g", 8), ("rwkv_w0", 8), ("rwkv_a0", 8),
             ("rwkv_k_k", 8), ("rwkv_k_a", 8), ("rwkv_r_k", 8), ("rwkv_ln_w", 8), ("rwkv_ln_b", 8)],
            [("ffn_conv_w_2", 128)],
            [("ffn_conv_w_2b", 4), ("ffn_conv_b_2", 44), ("mu", 24)],
        ]
        rows = [self.view(P * n, P) for n in range(len(groups))]
        self.col = {}
        base = 0
        cols = self.param_cols
        flat = lambda a: self.flat(a)
        for k, g in enumerate(groups):
            r = 0
            for name, n in g:
                if name == "ffn_conv_w_2":
                    src = flat(i[name]).rearrange("(n p) -> n p", p=P)[0:128, :]
                elif name == "ffn_conv_w_2b":
                    src = flat(i["ffn_conv_w_2"]).rearrange("(n p) -> n p", p=P)[128:132, :]
                elif name == "mu":
                    src = flat(i["rwkv_mu"])[0:3072].rearrange("(n p) -> n p", p=P)
                else:
                    src = flat(i[name]).rearrange("(n p) -> n p", p=P)
                t = self.load(0, rows[k][r:r + n, :], src)
                self.col[name] = cols[:, base + r:base + r + n]
                r += n
            base += r
        self.cols = cols
        self.colbase = base
        T.wait(t, self.G.tok())
        base = 0
        for k, g in enumerate(groups):
            r = sum(n for _, n in g)
            tt = T(nc.tensor.transpose(self.PS[:, k, 0:r], rows[k][0:r, :], self.ident[0:r, 0:r]))
            S.wait(tt)
            S(nc.scalar.activation(cols[:, base:base + r], self.PS[:, k, 0:r], ACT.Copy))
            base += r
        c0 = [0]
        o = 0
        for g in groups:
            for name, n in g:
                if name == "ffn_conv_w_2":
                    self.fcw = cols[:, o:o + 132].rearrange("p (j f) -> p j f", f=44)
                o += n

    def flat(self, a):
        while len(a.shape) > 1:
            names = " ".join(f"d{k}" for k in range(len(a.shape)))
            a = a.rearrange(f"{names} -> ({names})")
        return a

    def rstd(self, src, stat, junk, n, eps=EPS):
        nc, V, S = self.nc, self.V, self.S
        for tt in range(NT):
            S.seq(nc.scalar.activation(junk, src(tt), ACT.Square, accum_out=stat[:, tt:tt + 1]))
        V.wait(S.tok())
        V.seq(nc.vector.tensor_scalar(stat[:, 0:NT], stat[:, 0:NT], 1.0 / n, eps, ALU.mult, ALU.add))
        S.wait(V.tok())
        S.seq(nc.scalar.activation(stat[:, 0:NT], stat[:, 0:NT], ACT.Sqrt))
        V.wait(S.tok())
        return V.seq(nc.vector.reciprocal(stat[:, 0:NT], stat[:, 0:NT]))

    def to_feat(self, src, gain, xh, xl, n, k0=0):
        nc, T, V, S = self.nc, self.T, self.V, self.S
        for k in range(n):
            if k >= 8:
                T.wait(v_at[k - 8])
            for tt in range(NT):
                t = T(nc.tensor.transpose(self.PS[:, k % 8, tt * P:(tt + 1) * P], src(tt, k),
                                          self.ident[:, :]))
            S.wait(t)
            ps = self.PS[:, k % 8, 0:SEQ]
            s = S(nc.scalar.activation(xh[:, k0 + k, :], ps, ACT.Copy, scale=gain[:, k:k + 1]))
            V.wait(s)
            v = V(nc.vector.scalar_tensor_tensor(xl[:, k0 + k, :], ps, gain[:, k:k + 1],
                                                 xh[:, k0 + k, :].bitcast(F32), ALU.mult, ALU.subtract))
            if k == 0:
                v_at = {}
            v_at[k] = v

    def norm_to_feat(self, x, xn, stat, gain, xh, xl):
        nc, V, T = self.nc, self.V, self.T
        self.rstd(lambda tt: x[:, tt, :], stat, xn[:, 0, :], D)
        for tt in range(NT):
            V(nc.vector.tensor_scalar(xn[:, tt, :], x[:, tt, :], stat[:, tt:tt + 1], None, ALU.mult))
        T.wait(V.tok())
        self.to_feat(lambda tt, k: xn[:, tt, k * P:(k + 1) * P], gain, xh, xl, KD)


class LoopScope:

    def __init__(self, prog, n, name, tiles, blks):
        self.p, self.n, self.name, self.tiles, self.blks = prog, n, name, tiles, blks

    def __enter__(self):
        p = self.p
        self.steps = STEPS.get(self.name, (0, 0, 0, 0))
        self.start = [l.const for l in p.lanes]
        self.t0, self.b0 = p.tile_const, p.blk_const
        self.cm = p.nc.Fori(0, self.n)
        i = self.cm.__enter__()
        for l, s in zip(p.lanes, self.steps):
            l.terms.append((i, s))
        p.tile_terms.append((i, self.tiles))
        p.blk_terms.append((i, self.blks))
        return i

    def __exit__(self, *exc):
        p = self.p
        self.cm.__exit__(*exc)
        if exc[0] is not None:
            return False
        made = tuple(l.const - s for l, s in zip(p.lanes, self.start))
        if made != tuple(self.steps):
            MISMATCH[self.name] = made
        assert p.tile_const - self.t0 == self.tiles and p.blk_const - self.b0 == self.blks
        for l, s, m in zip(p.lanes, self.start, made):
            l.const = s + self.n * m
            l.terms.pop()
        p.tile_const = self.t0 + self.n * self.tiles
        p.blk_const = self.b0 + self.n * self.blks
        p.tile_terms.pop()
        p.blk_terms.pop()
        return False


MISMATCH = {}


class Model(Prog):

    def bc(self, ap, n):
        return ap.unsqueeze(2).to_broadcast([ap.shape[0], ap.shape[1], n])

    def rep(self, ap, n):
        return ap.unsqueeze(1).to_broadcast([ap.shape[0], n, ap.shape[1]])

    def spec(self, w, mode, col, evac, kt=KD, k0=0, xh=None, xl=None, widths=None):
        return dict(w=w, k0=k0, kt=kt, xh=xh if xh is not None else self.XH, xl=xl if xl is not None else self.XL,
                    mode=mode, col=col, evac=evac,
                    widths=widths or ([512] if mode == "tok" else [P] * 4))

    def ev_feat(self, dst, j, L, func=ACT.Copy):
        def evac(g, ps, ready):
            self.S.wait(ready)
            self.done_evac(self.nc.scalar.activation(dst[:, ds(4 * (g * L + j), 4), :], ps, func))
        return evac

    def ev_tok(self, dst, j, L, func=ACT.Copy):
        def evac(g, ps, ready):
            self.S.wait(ready)
            self.done_evac(self.nc.scalar.activation(dst[:, :, ds(512 * (g * L + j), 512)], ps, func))
        return evac

    def ev_add(self, x, j, L):
        def evac(g, ps, ready):
            self.V.wait(ready)
            o = x[:, :, ds(512 * (g * L + j), 512)]
            self.done_evac(self.nc.vector.tensor_tensor(o, o, ps, ALU.add))
        return evac

    def proj(self, name, w, c0, n, mode, ev, kt=KD, k0=0, xh=None, xl=None):
        L = 2 if n > 2 else n
        specs = [self.spec(w, mode, (lambda g, j=j: 512 * (g * L + j) + c0), ev(j, L), kt, k0, xh, xl)
                 for j in range(L)]
        self.stream(name, n // L, specs)

    def shift_mix(self, buf, tmp, mu, dst, p, f0, f1):
        nc, V = self.nc, self.V
        u, up, t = buf[0:p, f0:f1, 1:1 + SEQ], buf[0:p, f0:f1, 0:SEQ], tmp[0:p, f0:f1, :]
        V.seq(nc.vector.tensor_tensor(t, up, u, ALU.subtract))
        V.seq(nc.vector.tensor_tensor(t, t, self.bc(mu, SEQ), ALU.mult))
        V.seq(nc.vector.tensor_tensor(dst, u, t, ALU.add))

    def log1p_exp_negabs(self, out, x, t):
        nc, V, S = self.nc, self.V, self.S
        e, u, d = t
        V.seq(nc.vector.scalar_tensor_tensor(e, x, -1.0, x, ALU.mult, ALU.max))
        S.wait(V.tok())
        S.seq(nc.scalar.activation(e, e, ACT.Exp, scale=-1.0))
        V.wait(S.tok())
        V.seq(nc.vector.tensor_scalar(u, e, 1.0, None, ALU.add))
        S.wait(V.tok())
        S(nc.scalar.activation(out, u, ACT.Ln))
        V.seq(nc.vector.tensor_scalar(d, u, -1.0, 5e-8, ALU.add, ALU.max))
        V.seq(nc.vector.reciprocal(d, d))
        V.seq(nc.vector.tensor_tensor(d, d, e, ALU.mult))
        V.wait(S.tok())
        V.seq(nc.vector.tensor_tensor(out, out, d, ALU.mult))
        V.seq(nc.vector.tensor_scalar(u, e, -0.5, 1.0, ALU.mult, ALU.add))
        V.seq(nc.vector.tensor_tensor(u, u, e, ALU.mult))
        V.seq(nc.vector.tensor_tensor(out, out, u, ALU.max))

    def split(self, xh, xl, ps, scale=None):
        nc, V, S = self.nc, self.V, self.S
        if scale is None:
            S(nc.scalar.activation(xh, ps, ACT.Copy))
            V.wait(S.tok())
            return V(nc.vector.tensor_tensor(xl, ps, xh.bitcast(F32), ALU.subtract))
        S(nc.scalar.activation(xh, ps, ACT.Copy, scale=scale))
        V.wait(S.tok())
        return V(nc.vector.scalar_tensor_tensor(xl, ps, scale, xh.bitcast(F32), ALU.mult, ALU.subtract))

    def block1_in(self):
        nc, V, S, G, i = self.nc, self.V, self.S, self.G, self.i
        w = i["w_in"][0]
        Z = self.Z = self.view(0, NT, SSD_W)
        XBC_ = self.XBC = self.view(2048, 12, SEQ)
        RKV = self.RKV = self.view(5120, 24, SEQ)
        LO = self.LO = self.view(11264, 4, SEQ)
        DT = self.DT = self.view(12288, NT, 16)
        x, xn, stat = self.view(12320, NT, D), self.view(16416, NT, D), self.view(20512, 16)
        buf3, buf1 = self.view(20528, 4, SEQ + 3), self.view(21568, 4, SEQ + 1)
        tmp, acc = self.view(22600, 4, SEQ), self.view(23624, 4, SEQ)
        self.XTOK = i["x"][0].rearrange("(t p) d -> p t d", p=P)
        t = self.load(1, x, self.XTOK)
        G(nc.gpsimd.memset(buf3[:, :, 0:3], 0.0))
        G(nc.gpsimd.memset(buf1[:, :, 0:1], 0.0))
        S.wait(t)
        V.wait(t)
        self.T.wait(S.tok())
        self.norm_to_feat(x, xn, stat, self.col["norm_mix_g"], self.XH, self.XL)
        self.join()

        def ev_rkv(j, L):
            def evac(g, ps, ready):
                S.wait(ready, V.tok())
                self.done_evac(nc.scalar.activation(buf1[:, :, 1:1 + SEQ], ps, ACT.Copy))
                V.wait((self.s_evac, CREDIT + self.evac_count(j, L, g)))
                b = g * L + j
                self.shift_mix(buf1, tmp, self.col["mu"][:, ds(4 * b, 4)], RKV[:, ds(4 * b, 4), :], P, 0, 4)
            return evac

        def ev_xbc(j):
            def evac(g, ps, ready):
                S.wait(ready, V.tok())
                self.done_evac(nc.scalar.activation(buf3[:, :, 3:3 + SEQ], ps, ACT.Copy))
                V.wait((self.s_evac, CREDIT + self.blk_evac0 + j + 1))
                cw = self.col["ssd_conv_w"]
                for tap in range(SSD_CONV):
                    src = buf3[:, :, tap:tap + SEQ]
                    wt = self.bc(cw[:, 12 * tap + 4 * j:12 * tap + 4 * j + 4], SEQ)
                    if tap == 0:
                        V.seq(nc.vector.tensor_tensor(acc, src, wt, ALU.mult))
                    else:
                        V.seq(nc.vector.tensor_tensor(tmp, src, wt, ALU.mult))
                        V.seq(nc.vector.tensor_tensor(acc, acc, tmp, ALU.add))
                V.seq(nc.vector.tensor_tensor(acc, acc, self.bc(self.col["ssd_conv_b"][:, 4 * j:4 * j + 4], SEQ),
                                              ALU.add))
                S.wait(V.tok())
                S(nc.scalar.activation(XBC_[:, 4 * j:4 * j + 4, :], acc, ACT.Silu))
                V.wait(S.tok())
            return evac

        def ev_lora(g, ps, ready):
            S.wait(ready, V.tok())
            S.seq(nc.scalar.activation(buf1[0:LORA, 0:2, 1:1 + SEQ], ps[0:LORA, 0:2, :], ACT.Copy))
            self.done_evac(nc.scalar.activation(buf1[:, 2:4, 1:1 + SEQ], ps[:, 2:4, :], ACT.Copy))
            V.wait(S.tok(), (self.s_evac, CREDIT + self.blk_evac0 + 4))
            self.shift_mix(buf1, tmp, self.mul[0:LORA, 0:2], LO[0:LORA, 0:2, :], LORA, 0, 2)
            self.shift_mix(buf1, tmp, self.mul[:, 2:4], LO[:, 2:4, :], P, 2, 4)

        def ev_dt(g, ps, ready):
            S.wait(ready)
            self.done_evac(nc.scalar.activation(DT, ps[:, :, 0:16], ACT.Copy))

        self.blk_evac0 = self.blk_const
        self.evac_count = lambda j, L, g: self.blk_evac0 + g * L + j + 1
        self.proj("w_in_rkv", w, 2576, 6, "feat", ev_rkv)
        self.blk_evac0 = self.blk_const
        sp = [self.spec(w, "feat", (lambda g, j=j: 1024 + 512 * j), ev_xbc(j)) for j in range(3)]
        sp.append(self.spec(w, "feat", lambda g: 2576 + 3072, ev_lora, widths=[LORA, LORA, P, P]))
        sp += [self.spec(w, "tok", (lambda g, j=j: 512 * j), self.ev_tok(Z, j, 2, ACT.Silu)) for j in range(2)]
        sp.append(self.spec(w, "tok", lambda g: 2560, ev_dt, widths=[16]))
        self.stream("w_in_rest", 1, sp)
        self.join()

    def ssd(self):
        nc, T, V, S, G = self.nc, self.T, self.V, self.S, self.G
        PS, DT, XB, Z = self.PS, self.DT, self.XBC, self.Z
        o = 12320
        xs = self.view(o, NT, SSD_W)
        bm = self.view(o + 2048, NT, 256)
        xdt = self.view(o + 2560, NT, SSD_W)
        xdte = self.view(o + 4608, SSD_W)
        cbT = self.view(o + 5632, P)
        LT = self.view(o + 5760, 4, P)
        AT = self.view(o + 6272, 4, P)
        st = self.view(o + 6784, SSD_G, 512)
        y = self.view(o + 7808, NT, SSD_W)
        sm = [self.view(o + 9856 + 32 * k, NT, 16) for k in range(10)]
        junk = self.view(o + 10240, 512)
        dt, da, cs, ecs, dte, t0, t1, t2, ncs, rs = sm
        n = 0
        for c in range(NT):
            for q in range(3):
                fs = range(4 * q, min(4 * q + 4, 10))
                bank = n % 4
                n += 1
                if n > 4:
                    T.wait(hist[n - 5])
                else:
                    hist = {} if n == 1 else hist
                for k, f in enumerate(fs):
                    T(nc.tensor.transpose(PS[:, bank, k * P:(k + 1) * P], XB[:, f, c * P:(c + 1) * P],
                                          self.ident[:, :]))
                S.wait(T.tok())
                dst = xs[:, c, 512 * q:512 * q + 512] if q < 2 else bm[:, c, :]
                hist[n - 1] = S(nc.scalar.activation(dst, PS[:, bank, 0:P * len(fs)], ACT.Copy))
        A = self.view(o + 10752, 16)
        S.seq(nc.scalar.activation(A, self.alog[:, :], ACT.Exp))
        V.seq(nc.vector.tensor_tensor(DT, DT, self.rep(self.dtb[:, :], NT), ALU.add))
        self.log1p_exp_negabs(dt, DT, (t0, t1, t2))
        V.seq(nc.vector.scalar_tensor_tensor(dt, DT, 0.0, dt, ALU.max, ALU.add))
        V.seq(nc.vector.tensor_tensor(da, dt, self.rep(A, NT), ALU.mult))
        V.seq(nc.vector.tensor_scalar(da, da, -1.0, None, ALU.mult))
        T.wait(V.tok(), S.tok())
        T(nc.tensor.matmul(PS[:, 4, 0:32], self.triu[:, :], da, start=True, stop=True))
        t = T(nc.tensor.matmul(PS[:, 5, 0:32], self.ones[:, :], da, start=True, stop=True))
        V.wait(t)
        as2 = lambda b: PS[:, b, 0:32].rearrange("p (c h) -> p c h", c=NT)
        V.seq(nc.vector.tensor_copy(cs, as2(4)))
        V.seq(nc.vector.tensor_tensor(dte, as2(5), cs, ALU.subtract))
        V.seq(nc.vector.tensor_scalar(ncs, cs, -1.0, None, ALU.mult))
        S.wait(V.tok())
        S(nc.scalar.activation(ecs, cs, ACT.Exp))
        S.seq(nc.scalar.activation(dte, dte, ACT.Exp))
        hv = lambda ap: ap.rearrange("p (h e) -> p h e", e=64)
        for c in range(NT):
            V.seq(nc.vector.tensor_tensor(hv(xdt[:, c, :]), hv(xs[:, c, :]), self.bc(dt[:, c, :], 64), ALU.mult))
        V.wait(S.tok())
        V.seq(nc.vector.tensor_tensor(hv(xdte), hv(xdt[:, 0, :]), self.bc(dte[:, 0, :], 64), ALU.mult))
        T.wait(V.tok())
        for g in range(SSD_G):
            T(nc.tensor.matmul(PS[:, 6 + g, :], bm[:, 0, g * P:(g + 1) * P], xdte[:, g * 512:g * 512 + 512],
                               start=True, stop=True))
        S.wait(T.tok())
        S(nc.scalar.activation(st, PS[:, 6:8, :], ACT.Copy))
        T.wait(S.tok())
        for c in range(NT):
            for g in range(SSD_G):
                cm, bmT = XB[:, 10 + g, c * P:(c + 1) * P], XB[:, 8 + g, c * P:(c + 1) * P]
                T(nc.tensor.matmul(PS[:, 0, 0:P], bmT, cm, start=True, stop=True))
                V.wait(T.tok())
                V(nc.vector.tensor_copy(cbT, PS[:, 0, 0:P]))
                if c > 0:
                    T(nc.tensor.matmul(PS[:, 2, :], cm, st[:, g, :], start=True, stop=True))
                for q in range(2):
                    T(nc.tensor.matmul(PS[:, 4 + q, :], self.ident[:, :], self.rep(self.negl[:, :], 4),
                                       start=True, stop=False, skip_group_check=True))
                    for e in range(4):
                        h = 8 * g + 4 * q + e
                        lhs = da[:, c, h:h + 1].to_broadcast([P, P])
                        T(nc.tensor.matmul(PS[:, 4 + q, e * P:(e + 1) * P], lhs, self.triu[:, :],
                                           start=False, stop=True, skip_group_check=True))
                    S.wait(T.tok(), V.tok())
                    for e in range(4):
                        h = 8 * g + 4 * q + e
                        S(nc.scalar.activation(LT[:, e, :], PS[:, 4 + q, e * P:(e + 1) * P], ACT.Exp,
                                               bias=ncs[:, c, h:h + 1]))
                    V.wait(S.tok(), T.tok())
                    V.seq(nc.vector.tensor_tensor(AT, LT, self.rep(cbT, 4), ALU.mult))
                    T.wait(V.tok())
                    for e in range(4):
                        h = 8 * g + 4 * q + e
                        T(nc.tensor.matmul(PS[:, 1, (4 * q + e) * 64:(4 * q + e) * 64 + 64], AT[:, e, :],
                                           xdt[:, c, h * 64:h * 64 + 64], start=(q == 0 and e == 0),
                                           stop=True, skip_group_check=True))
                    V.wait(T.tok())
                yg = y[:, c, g * 512:g * 512 + 512]
                xg = xs[:, c, g * 512:g * 512 + 512]
                V.seq(nc.vector.tensor_tensor(hv(yg), hv(xg), self.bc(self.dsk[:, 8 * g:8 * g + 8], 64), ALU.mult))
                V.seq(nc.vector.tensor_tensor(yg, yg, PS[:, 1, :], ALU.add))
                if c > 0:
                    V.wait(S.tok())
                    V.seq(nc.vector.tensor_tensor(hv(junk), hv(PS[:, 2, :]),
                                                  self.bc(ecs[:, c, 8 * g:8 * g + 8], 64), ALU.mult))
                    V.seq(nc.vector.tensor_tensor(yg, yg, junk, ALU.add))
                V.seq(nc.vector.tensor_tensor(yg, yg, Z[:, c, g * 512:g * 512 + 512], ALU.mult))
                T.wait(V.tok())
        S.wait(V.tok())
        for c in range(NT):
            for g in range(SSD_G):
                S.seq(nc.scalar.activation(junk, y[:, c, g * 512:g * 512 + 512], ACT.Square,
                                           accum_out=rs[:, c, g:g + 1]))
        V.wait(S.tok())
        r = rs[:, :, 0:2]
        V.seq(nc.vector.tensor_scalar(r, r, 1.0 / 512, EPS, ALU.mult, ALU.add))
        S.wait(V.tok())
        S.seq(nc.scalar.activation(r, r, ACT.Sqrt))
        V.wait(S.tok())
        V.seq(nc.vector.reciprocal(r, r))
        for c in range(NT):
            for g in range(SSD_G):
                yg = y[:, c, g * 512:g * 512 + 512]
                V(nc.vector.tensor_scalar(yg, yg, rs[:, c, g:g + 1], None, ALU.mult))
        T.wait(V.tok())
        self.to_feat(lambda tt, k: y[:, tt, k * P:(k + 1) * P], self.col["ssd_norm_g"], self.XH, self.XL, 8)
        self.join()

    def feat_view(self, b0):
        return self.PS[:, b0:b0 + 4, :].rearrange("p a (f t) -> p (a f) t", t=SEQ)

    def head_sum(self, src, bank):
        for f in range(RP):
            self.T(self.nc.tensor.matmul(self.PS[0:16, bank, 0:SEQ], self.sel[:, f, :], src[:, f, :],
                                         start=f == 0, stop=f == RP - 1))

    def head_bcast(self, src, b0):
        v = self.feat_view(b0)
        for f in range(RP):
            for s in range(2):
                self.T(self.nc.tensor.matmul(v[64 * s:64 * s + 64, f, :],
                                             self.selT[:, f, s:s + 1].to_broadcast([16, 64]), src,
                                             start=f % 2 == 0, stop=True, skip_group_check=True))
        return v

    def rwkv(self):
        nc, T, V, S, G, i = self.nc, self.T, self.V, self.S, self.G, self.i
        PS, LO, col = self.PS, self.LO, self.col
        tt = lambda o, a, b, op: V.seq(nc.vector.tensor_tensor(o, a, b, op))
        R, K, VV = (self.RKV[:, 8 * k:8 * k + 8, :] for k in range(3))
        LW, IC, KK = self.view(12320, RP, SEQ), self.view(14368, RP, SEQ), self.view(16416, RP, SEQ)
        Q = self.view(18464, RP, SEQ)
        t1 = self.view(20512, RP, SEQ)
        w2, a2 = self.view(22560, 1024), self.view(23584, 1024)
        hs = self.view(24608, SEQ)[0:16, :]
        bs = self.view(24864, SEQ)[0:16, :]
        eend = self.view(25120, RP, NRC)
        c8 = self.view(25152, 16)
        la = self.load(2, w2[0:LORA, :], i["rwkv_w2"][0])
        la = self.load(2, a2[0:LORA, :], i["rwkv_a2"][0])
        S.seq(nc.scalar.activation(LO[0:LORA, 0, :], LO[0:LORA, 0, :], ACT.Tanh))
        S.seq(nc.scalar.activation(LO[:, 2:4, :], LO[:, 2:4, :], ACT.Sigmoid))
        T.wait(S.tok(), la)
        for n, (w, dst, b) in enumerate(((w2, LW, "rwkv_w0"), (a2, IC, "rwkv_a0"))):
            v = self.feat_view(4 * n)
            for f in range(RP):
                T(nc.tensor.matmul(v[:, f, :], w[0:LORA, f * P:(f + 1) * P], LO[0:LORA, n, :],
                                   start=f % 2 == 0, stop=True, skip_group_check=True))
            S.wait(T.tok())
            for f in range(RP):
                S(nc.scalar.activation(dst[:, f, :], v[:, f, :], ACT.Sigmoid, bias=col[b][:, f:f + 1]))
        V.wait(S.tok())
        V.seq(nc.vector.tensor_scalar(LW, LW, -0.6065306597126334, None, ALU.mult))
        tt(KK, K, self.bc(col["rwkv_k_k"], SEQ), ALU.mult)
        tt(t1, KK, KK, ALU.mult)
        T.wait(V.tok(), S.tok())
        self.head_sum(t1, 0)
        S.wait(T.tok())
        S.seq(nc.scalar.activation(hs, PS[0:16, 0, 0:SEQ], ACT.Sqrt))
        V.wait(S.tok())
        V.seq(nc.vector.tensor_scalar(hs, hs, 1e-12, None, ALU.max))
        V.seq(nc.vector.reciprocal(hs, hs))
        T.wait(V.tok())
        v = self.head_bcast(hs, 4)
        V.wait(T.tok())
        tt(KK, KK, v, ALU.mult)
        V.seq(nc.vector.tensor_scalar(t1, IC, -1.0, None, ALU.add))
        tt(t1, t1, self.bc(col["rwkv_k_a"], SEQ), ALU.mult)
        V.seq(nc.vector.scalar_tensor_tensor(K, t1, 1.0, K, ALU.add, ALU.mult))
        tt(t1, R, K, ALU.mult)
        tt(t1, t1, self.bc(col["rwkv_r_k"], SEQ), ALU.mult)
        T.wait(V.tok())
        self.head_sum(t1, 0)
        V.wait(T.tok())
        V.seq(nc.vector.tensor_copy(bs, PS[0:16, 0, 0:SEQ]))
        tt(IC, KK, IC, ALU.mult)
        for f in range(RP):
            V(nc.vector.tensor_tensor_scan(t1[:, f, :], self.rst[:, :], LW[:, f, :], 0.0, ALU.mult, ALU.add))
        V.wait(V.tok())
        tt(LW, t1, LW, ALU.subtract)
        S.wait(V.tok())
        S.seq(nc.scalar.activation(LW, LW, ACT.Exp))
        V.wait(S.tok())
        tt(Q, KK, LW, ALU.mult)
        S.wait(V.tok())
        S.seq(nc.scalar.activation(LW, t1, ACT.Exp))
        S.seq(nc.scalar.activation(t1, t1, ACT.Exp, scale=-1.0))
        V.wait(S.tok())
        tt(R, R, LW, ALU.mult)
        V.seq(nc.vector.tensor_copy(eend, LW.rearrange("p f (c e) -> p f c e", e=RC)[:, :, :, RC - 1]))
        tt(K, K, t1, ALU.mult)
        tt(IC, IC, t1, ALU.mult)
        Aa = self.view(12320, RP, SEQ)
        Qq = self.view(14368, RP, SEQ)
        sg = self.view(16416, 2, SEQ)
        bs2, eend2 = self.view(16928, SEQ)[0:16, :], self.view(17184, RP, NRC)
        V.seq(nc.vector.tensor_copy(Aa, IC))
        V.seq(nc.vector.tensor_copy(Qq, Q))
        V.seq(nc.vector.tensor_copy(sg, LO[:, 2:4, :]))
        V.seq(nc.vector.tensor_copy(bs2, bs))
        V.seq(nc.vector.tensor_copy(eend2, eend))
        self.join()
        free = [0, 1024, 2048, 3072, 4096, 11264 - 0] + []
        spots = [0, 1024, 2048, 3072, 4096] + [17216 + 1024 * k for k in range(8)]
        B = [self.view(s, RP, P) for s in spots]
        RAT, RKT = self.view(11264, RP, RC), self.view(11776, RP, RC)
        St = B[12]
        for b in (B[0], B[1], B[2], B[3], St):
            G(nc.gpsimd.memset(b, 0.0))
        for l in (T, V, S, G):
            l.wait(G.tok())

        def pair_mm(b0, pairs, n=P):
            per = 512 // n
            for f in range(RP):
                o = PS[:, b0 + f // per, (f % per) * n:(f % per) * n + n]
                for m, (a, b) in enumerate(pairs):
                    T(nc.tensor.matmul(o, a[:, f, :], b[:, f, :], start=(f % per == 0 and m == 0),
                                       stop=m == len(pairs) - 1, skip_group_check=True))
            return T.tok()

        def turn(b0, a):
            for f in range(RP):
                T(nc.tensor.transpose(PS[:, b0 + f // 4, (f % 4) * P:(f % 4) * P + P], a[:, f, :],
                                      self.ident[:, :]))
            return T.tok()

        def bd(b0):
            return PS[:, b0:b0 + 2, :].rearrange("p a (f t) -> p (a f) t", t=P)

        def cp(b):
            return PS[:, b, :].rearrange("p (f t) -> p f t", t=RC)

        m8 = lambda m: self.rep(m[:, :], RP)
        with self.loop(NRC, "rwkv_chunks") as c:
            tok = ds(c * RC, RC)
            for hp in range(2):
                r, q = slice(64 * hp, 64 * hp + 64), slice(64 * hp, 64 * hp + 64)
                V(nc.vector.tensor_copy(B[0][r, :, q], Aa[r, :, tok]))
                V(nc.vector.tensor_copy(B[2][r, :, q], Qq[r, :, tok]))
                S(nc.scalar.activation(B[1][r, :, q], K[r, :, tok], ACT.Copy))
                G(nc.gpsimd.tensor_copy(B[3][r, :, q], VV[r, :, tok]))
            T.wait(V.tok(), S.tok())
            t_a = pair_mm(0, [(B[0], B[2])])
            t_b = pair_mm(2, [(B[2], B[0])])
            t_c = pair_mm(4, [(B[0], R[:, :, tok])], RC)
            t_d = pair_mm(5, [(B[1], R[:, :, tok])], RC)
            t_e = pair_mm(6, [(B[1], B[2])])
            V.wait(t_a)
            V(nc.vector.tensor_tensor(B[4], bd(0), m8(self.m_d), ALU.mult))
            v_a = V(nc.vector.tensor_tensor(B[6], bd(0), m8(self.m_o), ALU.mult))
            V.wait(t_b)
            v_b = V(nc.vector.tensor_tensor(B[5], bd(2), m8(self.m_dT), ALU.mult))
            V.wait(t_d)
            V(nc.vector.tensor_tensor(RAT, cp(4), self.rep(self.m_ic[:, :], RP), ALU.mult))
            v_d = V(nc.vector.tensor_tensor(RKT, cp(5), self.rep(self.m_ic[:, :], RP), ALU.mult))
            V.wait(t_e)
            v_e = V(nc.vector.tensor_tensor(B[7], bd(6), m8(self.m_st), ALU.mult))
            T.wait(v_a)
            t1_ = turn(0, B[0])
            S.wait(t1_)
            s1 = S(nc.scalar.activation(B[8], bd(0), ACT.Copy))
            T.wait(v_b)
            t2_ = turn(2, B[1])
            S.wait(t2_)
            s2 = S(nc.scalar.activation(B[9], bd(2), ACT.Copy))
            T.wait(v_d, G.tok())
            t3_ = turn(4, B[3])
            S.wait(t3_)
            s3 = S(nc.scalar.activation(B[3], bd(4), ACT.Copy))
            V.wait(v_a)
            v_p = V(nc.vector.tensor_tensor(B[10], B[4], m8(self.ident), ALU.add))
            T.wait(v_e)
            t_u = pair_mm(6, [(B[5], B[4])])
            T.wait(s1)
            t_ut = pair_mm(0, [(B[4], B[5])])
            V.wait(t_u)
            v_u = V(nc.vector.tensor_copy(B[0], bd(6)))
            S.wait(t_ut)
            s_u = S(nc.scalar.activation(B[1], bd(0), ACT.Copy))
            T.wait(s_u, v_p, s2)
            t_p = pair_mm(2, [(B[1], B[10])])
            T.wait(v_u, s3)
            t_u2 = pair_mm(4, [(B[1], B[0])])
            t_u2t = pair_mm(6, [(B[0], B[1])])
            V.wait(t_p)
            v_p = V(nc.vector.tensor_tensor(B[11], bd(2), B[10], ALU.add))
            S.wait(t_u2, t_ut)
            s_u2 = S(nc.scalar.activation(B[5], bd(4), ACT.Copy))
            V.wait(t_u2t)
            v_u2t = V(nc.vector.tensor_copy(B[4], bd(6)))
            T.wait(v_u2t, v_p)
            t_p = pair_mm(2, [(B[4], B[11])])
            T.wait(s_u2)
            t_u3t = pair_mm(0, [(B[5], B[4])])
            V.wait(t_p)
            v_p = V(nc.vector.tensor_tensor(B[10], bd(2), B[11], ALU.add))
            S.wait(t_u3t)
            s_u3 = S(nc.scalar.activation(B[0], bd(0), ACT.Copy))
            T.wait(v_p, s_u3)
            t_p = pair_mm(4, [(B[0], B[10])])
            V.wait(t_p)
            v_p = V(nc.vector.tensor_tensor(B[11], bd(4), B[10], ALU.add))
            T.wait(v_p)
            t_pt = turn(6, B[11])
            S.wait(t_pt)
            s_pt = S(nc.scalar.activation(B[1], bd(6), ACT.Copy))
            T.wait(s_pt)
            t_m = pair_mm(2, [(B[6], B[1])])
            S.wait(t_m)
            s_m = S(nc.scalar.activation(B[0], bd(2), ACT.Copy))
            T.wait(s_m)
            zsrc = B[11]
            for n, (bank, dst) in enumerate(((4, B[10]), (6, B[4]), (0, B[5]))):
                t_z = pair_mm(bank, [(B[0], zsrc)])
                V.wait(t_z)
                v_z = V(nc.vector.tensor_tensor(dst, bd(bank), B[11], ALU.add))
                T.wait(v_z)
                zsrc = dst
            T.wait(S.tok())
            t_r = pair_mm(2, [(B[2], St), (B[7], B[3])])
            S.wait(t_r)
            s_r = S(nc.scalar.activation(B[4], bd(2), ACT.Copy))
            T.wait(s_r)
            t_sa = pair_mm(4, [(B[5], B[4])])
            S.wait(t_sa)
            s_sa = S(nc.scalar.activation(B[1], bd(4), ACT.Copy, scale=-1.0))
            T.wait(s_sa)
            t_y = pair_mm(6, [(St, R[:, :, tok]), (B[1], RAT), (B[3], RKT)], RC)
            t_s = pair_mm(0, [(B[8], B[1]), (B[9], B[3])])
            S.wait(t_y)
            S(nc.scalar.activation(R[:, :, tok], cp(6), ACT.Copy))
            V.wait(t_s)
            V.seq(nc.vector.tensor_tensor(St, St, bd(0), ALU.add))
            V.seq(nc.vector.tensor_tensor(St, St, eend2[:, :, ds(c, 1)].to_broadcast([P, RP, P]), ALU.mult))
            T.wait(S.tok(), V.tok())
            S.wait(V.tok(), T.tok())
            V.wait(S.tok(), T.tok())
            G.wait(T.tok())
        self.join()
        g2 = self.view(17216, 2, RW)
        GG, t1, t2 = self.view(19264, RP, SEQ), self.view(21312, RP, SEQ), self.view(23360, RP, SEQ)
        hs = self.view(17216 - 32 + 8192, SEQ)[0:16, :]
        hs = self.view(25408, SEQ)[0:16, :]
        l2 = self.load(3, g2, i["rwkv_g2"][0].rearrange("(a p) n -> p a n", p=P))
        T.wait(l2)
        v = self.feat_view(0)
        for f in range(RP):
            for k in range(2):
                T(nc.tensor.matmul(v[:, f, :], g2[:, k, f * P:(f + 1) * P], sg[:, k, :],
                                   start=(f % 2 == 0 and k == 0), stop=k == 1, skip_group_check=True))
        S.wait(T.tok())
        S(nc.scalar.activation(GG, v, ACT.Copy))
        self.head_sum(R, 4)
        V.wait(T.tok())
        V.seq(nc.vector.tensor_scalar(hs, PS[0:16, 4, 0:SEQ], 1.0 / 64, None, ALU.mult))
        T.wait(V.tok(), S.tok())
        v = self.head_bcast(hs, 0)
        V.wait(T.tok())
        tt(R, R, v, ALU.subtract)
        tt(t1, R, R, ALU.mult)
        T.wait(V.tok())
        self.head_sum(t1, 4)
        V.wait(T.tok())
        V.seq(nc.vector.tensor_scalar(hs, PS[0:16, 4, 0:SEQ], 1.0 / 64, LN_EPS, ALU.mult, ALU.add))
        S.wait(V.tok())
        S.seq(nc.scalar.activation(hs, hs, ACT.Sqrt))
        V.wait(S.tok())
        V.seq(nc.vector.reciprocal(hs, hs))
        T.wait(V.tok())
        v = self.head_bcast(hs, 0)
        v2 = self.head_bcast(bs2, 4)
        V.wait(T.tok())
        tt(R, R, v, ALU.mult)
        tt(R, R, self.bc(col["rwkv_ln_w"], SEQ), ALU.mult)
        tt(R, R, self.bc(col["rwkv_ln_b"], SEQ), ALU.add)
        tt(t1, v2, VV, ALU.mult)
        tt(R, R, t1, ALU.add)
        tt(R, R, GG, ALU.mult)
        S.wait(V.tok())
        self.split(self.XH[:, 8:16, :], self.XL[:, 8:16, :], R)
        self.join()

    def softmax_rows(self, src, pr, st):
        nc, V, S = self.nc, self.V, self.S
        V.seq(nc.vector.tensor_reduce(st[:, 0:2], src, AX.X, ALU.max))
        V.seq(nc.vector.tensor_scalar(st[:, 2:4], st[:, 0:2], -1.0, None, ALU.mult))
        S.wait(V.tok())
        for q in range(NT):
            S(nc.scalar.activation(pr[:, q, :], src[:, q, :], ACT.Exp, bias=st[:, 2 + q:3 + q],
                                   accum_out=st[:, 4 + q:5 + q]))
        V.wait(S.tok())
        V.seq(nc.vector.reciprocal(st[:, 4:6], st[:, 4:6]))
        for q in range(NT):
            V(nc.vector.tensor_scalar(pr[:, q, :], pr[:, q, :], st[:, 4 + q:5 + q], None, ALU.mult))
        return V.tok()

    def cross(self):
        nc, T, V, S, G, i = self.nc, self.T, self.V, self.S, self.G, self.i
        PS, x = self.PS, self.x
        xn, stat = self.view(0, NT, D), self.view(4096, 16)
        Qf, Kf, Vt = self.view(4112, KD, SEQ), self.view(8208, KD, SEQ), self.view(12304, NT, D)
        Qs, Vs = self.view(16400, 4, SEQ), self.view(17424, NT, XD)
        pr, pT, st = self.view(18448, NT, SEQ), self.view(18960, NT, SEQ), self.view(19472, 8)
        self.norm_to_feat(x, xn, stat, self.col["norm_x_g"], self.XH, self.XL)
        t = self.load(4, Vt, i["mem"][0].rearrange("(t p) d -> p t d", p=P))
        self.join()
        self.proj("xattn_q", i["xattn_wq"][0], 0, 4, "feat", lambda j, L: self.ev_feat(Qf, j, L))
        self.join()
        S.wait(t)
        V.wait(t)
        self.norm_to_feat(Vt, xn, stat, self.col["norm_mem_g"], self.XH, self.XL)
        self.join()
        self.proj("xattn_k", i["xattn_wk"][0], 0, 4, "feat", lambda j, L: self.ev_feat(Kf, j, L))
        self.proj("xattn_v", i["xattn_wv"][0], 0, 4, "tok", lambda j, L: self.ev_tok(Vt, j, L))
        self.join()
        with self.loop(XH_, "xattn_heads") as h:
            S(nc.scalar.activation(Qs, Qf[:, ds(4 * h, 4), :], ACT.Copy, scale=float(XD) ** -0.5))
            G(nc.gpsimd.tensor_copy(Vs, Vt[:, :, ds(XD * h, XD)]))
            T.wait(S.tok())
            sc = PS[:, 0, :].rearrange("p (q m) -> p q m", q=NT)
            for q in range(NT):
                for k in range(4):
                    T(nc.tensor.matmul(sc[:, q, :], Qs[:, k, q * P:(q + 1) * P], Kf[:, ds(4 * h + k, 1), :],
                                       start=(q == 0 and k == 0), stop=k == 3, skip_group_check=True))
            V.wait(T.tok())
            T.wait(self.softmax_rows(sc, pr, st))
            for m in range(NT):
                for q in range(NT):
                    T(nc.tensor.transpose(PS[:, 1, m * SEQ + q * P:m * SEQ + q * P + P],
                                          pr[:, q, m * P:(m + 1) * P], self.ident[:, :]))
            S.wait(T.tok())
            S(nc.scalar.activation(pT, PS[:, 1, :].rearrange("p (m q) -> p m q", m=NT), ACT.Copy))
            T.wait(S.tok(), G.tok())
            o = PS[:, 2:4, :].rearrange("p a (f t) -> p (a f) t", t=SEQ)
            for f in range(4):
                for m in range(NT):
                    T(nc.tensor.matmul(o[:, f, :], Vs[:, m, f * P:(f + 1) * P], pT[:, m, :],
                                       start=(f % 2 == 0 and m == 0), stop=m == 1, skip_group_check=True))
            S.wait(T.tok())
            self.split(self.XH[:, ds(4 * h, 4), :], self.XL[:, ds(4 * h, 4), :], o)
            T.wait(V.tok())
            S.wait(V.tok())
            G.wait(T.tok())
        self.join()
        self.proj("xattn_o", i["xattn_wo"][0], 0, 4, "tok", lambda j, L: self.ev_add(x, j, L))
        self.join()

    def ffn1(self, AH, AL, xn, tmp, sq):
        nc, V, S, i, x = self.nc, self.V, self.S, self.i, self.x
        stat = self.stat
        self.norm_to_feat(x, xn, stat, self.col["norm_ffn_g"], self.XH, self.XL)
        self.join()
        w1, w2 = i["ffn_w1"][0], i["ffn_w2"][0]

        def ev(j, L):
            def evac(g, ps, ready):
                S.wait(ready, V.tok())
                self.done_evac(nc.scalar.activation(tmp, ps, ACT.Relu))
                V.wait((self.s_evac, CREDIT + self.evac_base() + g * L + j + 1))
                V.seq(nc.vector.tensor_tensor(sq, tmp, tmp, ALU.mult))
                d = ds(4 * (g * L + j), 4)
                S.wait(V.tok())
                S(nc.scalar.activation(AH[:, d, :], sq, ACT.Copy))
                V.wait(S.tok())
                V.seq(nc.vector.tensor_tensor(AL[:, d, :], sq, AH[:, d, :].bitcast(F32), ALU.subtract))
            return evac
        for part in range(4):
            base = self.blk()
            self.evac_base = lambda: base
            self.proj(f"ffn1_up{part}", w1, 2048 * part, 4, "feat", ev)
            self.join()
            self.proj(f"ffn1_down{part}", w2, 0, 4, "tok", lambda j, L: self.ev_add(x, j, L),
                      kt=16, k0=2048 * part, xh=AH, xl=AL)
            self.join()

    def final_norm(self, x, dst, gb, junk):
        nc, V, S = self.nc, self.V, self.S
        self.rstd(lambda tt: x[:, tt, :], self.stat, junk, D)
        for tt in range(NT):
            V.seq(nc.vector.scalar_tensor_tensor(dst[:, tt, :], x[:, tt, :], self.stat[:, tt:tt + 1], gb,
                                                 ALU.mult, ALU.mult))

    def hgrn(self):
        nc, T, V, S, G, i = self.nc, self.T, self.V, self.S, self.G, self.i
        PS, x = self.PS, self.x
        w = i["w_in_2"][0]
        tt = lambda o, a, b, op: V.seq(nc.vector.tensor_tensor(o, a, b, op))
        xn = self.view(0, NT, D)
        self.norm_to_feat(x, xn, self.stat, self.col["norm1_gain_2"], self.XH, self.XL)
        self.join()
        Qa, Fa = self.view(0, GH, SEQ), self.view(2048, GH, SEQ)
        Ia, Ga = self.view(4096, NT, 1024), self.view(6144, NT, 1024)
        self.proj("w_in2_q", w, 0, 2, "feat", lambda j, L: self.ev_feat(Qa, j, L))
        self.proj("w_in2_f", w, 1024, 2, "feat", lambda j, L: self.ev_feat(Fa, j, L, ACT.Sigmoid))
        self.proj("w_in2_i", w, 2048, 2, "tok", lambda j, L: self.ev_tok(Ia, j, L))
        self.proj("w_in2_g", w, 3072, 2, "tok", lambda j, L: self.ev_tok(Ga, j, L, ACT.Silu))
        Qb, Kb, Vb = self.view(8192, GH, SEQ), self.view(10240, GH, SEQ), self.view(12288, NT, 1024)
        Fb = self.Fb = self.view(14336, NT, 8)
        self.Qb, self.Kb, self.Vb = Qb, Kb, Vb
        self.proj("w_in2_qb", w, 4096, 2, "feat", lambda j, L: self.ev_feat(Qb, j, L))
        self.proj("w_in2_kb", w, 5120, 2, "feat", lambda j, L: self.ev_feat(Kb, j, L))

        def ev_fb(g, ps, ready):
            S.wait(ready)
            self.done_evac(nc.scalar.activation(Fb, ps[:, :, 0:8], ACT.Copy))
        sp = [self.spec(w, "tok", (lambda g, j=j: 6144 + 512 * j), self.ev_tok(Vb, j, 2)) for j in range(2)]
        sp.append(self.spec(w, "tok", lambda g: 7168, ev_fb, widths=[8]))
        self.stream("w_in2_rest", 1, sp)
        self.join()
        lb = self.view(14352, 24)
        p = self.col["hgrn_lb_param_2"]
        L0, L1, LM = lb[:, 0:8], lb[:, 8:16], lb[:, 16:24]
        tt(LM, p[:, 0:8], p[:, 8:16], ALU.max)
        tt(L0, p[:, 0:8], LM, ALU.subtract)
        tt(L1, p[:, 8:16], LM, ALU.subtract)
        S.wait(V.tok())
        S.seq(nc.scalar.activation(lb[:, 0:16], lb[:, 0:16], ACT.Exp))
        V.wait(S.tok())
        tt(LM, L0, L1, ALU.add)
        V.seq(nc.vector.reciprocal(LM, LM))
        tt(L0, L0, LM, ALU.mult)
        V.seq(nc.vector.tensor_scalar(L1, L0, -1.0, 1.0, ALU.mult, ALU.add))
        Kd, Ke, Bb = self.view(14376, GH, SEQ), self.view(16424, GH, SEQ), self.view(18472, GH, SEQ)
        dce = self.view(20520, GH, NRC)
        tt(Kd, Fa, self.bc(L1, SEQ), ALU.mult)
        tt(Kd, Kd, self.bc(L0, SEQ), ALU.add)
        S.wait(V.tok())
        S.seq(nc.scalar.activation(Bb, Kd, ACT.Ln))
        V.wait(S.tok())
        V.seq(nc.vector.tensor_scalar(Kd, Kd, -1.0, 1.0, ALU.mult, ALU.add))
        for h in range(GH):
            V(nc.vector.tensor_tensor_scan(Fa[:, h, :], self.rst[:, :], Bb[:, h, :], 0.0, ALU.mult, ALU.add))
        V.wait(V.tok())
        ch = lambda a: a.rearrange("p f (c e) -> p (f c) e", e=HCH)
        b_end = ch(Fa)[:, :, HCH - 1:HCH].to_broadcast([P, GH * NRC, HCH])
        tt(ch(Ke), b_end, ch(Fa), ALU.subtract)
        S.wait(V.tok())
        S(nc.scalar.activation(Ke, Ke, ACT.Exp))
        S(nc.scalar.activation(Bb, Fa, ACT.Exp))
        S.seq(nc.scalar.activation(Fa, Fa, ACT.Exp, scale=-1.0))
        V.wait(S.tok())
        tt(Ke, Ke, Kd, ALU.mult)
        tt(Kd, Kd, Fa, ALU.mult)
        V.seq(nc.vector.scalar_tensor_tensor(Qa, Qa, float(P) ** -0.5, Bb, ALU.mult, ALU.mult))
        V.seq(nc.vector.tensor_copy(dce, Bb.rearrange("p f (c e) -> p f c e", e=HCH)[:, :, :, HCH - 1]))
        o = 2048
        QZ = self.view(o, 4, P)
        KTe, KTo = self.view(o + 512, NT, P), self.view(o + 768, NT, P)
        Kds, Kes = self.view(o + 1024, SEQ), self.view(o + 1280, SEQ)
        AT, O = self.view(o + 1536, NT, P), self.view(18472, NT, P)
        Sn = self.view(18728, 3, P)
        stt_, dcs = self.view(19112, 4), self.view(19116, NRC)
        junk = self.view(19120, P)
        self.join()
        for b in (QZ, KTe, KTo):
            G(nc.gpsimd.memset(b, 0.0))
        for l in (T, V, S, G):
            l.wait(G.tok())
        with self.loop(GH, "hgrn_heads") as h:
            hd, cols = ds(h, 1), ds(P * h, P)
            G(nc.gpsimd.tensor_copy(Kds, Kd[:, hd, :]))
            G(nc.gpsimd.tensor_copy(Kes, Ke[:, hd, :]))
            G(nc.gpsimd.tensor_copy(dcs, dce[:, hd, :]))
            qv = Qa[:, hd, :].rearrange("p o (t c e) -> p (o t) c e", t=NT, c=2)
            for c in range(2):
                S(nc.scalar.activation(QZ.rearrange("p (t c) e -> p t c e", c=2)[:, :, c, c * 64:c * 64 + 64],
                                       qv[:, :, c, :], ACT.Copy))
            T.wait(G.tok())
            for q in range(NT):
                T(nc.tensor.matmul(PS[:, 0, q * P:(q + 1) * P], Kds[:, q * P:(q + 1) * P],
                                   Qa[:, hd, q * P:(q + 1) * P], start=q == 0, stop=True,
                                   skip_group_check=True))
            t_a = T.tok()
            for q in range(NT):
                T(nc.tensor.transpose(PS[:, 1, q * P:(q + 1) * P], Kes[:, q * P:(q + 1) * P], self.ident[:, :]))
            V.wait(t_a)
            v3 = lambda b: PS[:, b, 0:SEQ].rearrange("p (q m) -> p q m", q=NT)
            V(nc.vector.tensor_tensor(AT, v3(0), self.rep(self.m_in[:, :], NT), ALU.mult))
            S.wait(T.tok())
            S(nc.scalar.activation(KTe[0:64, :, :], v3(1)[0:64], ACT.Copy))
            S(nc.scalar.activation(KTo[64:128, :, :], v3(1)[64:128], ACT.Copy))
            T.wait(S.tok())
            for n in range(3):
                T(nc.tensor.matmul(PS[:, 2, n * P:(n + 1) * P], (KTe, KTo)[n % 2][:, n // 2, :],
                                   Ia[:, n // 2, cols], start=n == 0, stop=True, skip_group_check=True))
            V.wait(T.tok())
            V.seq(nc.vector.tensor_copy(Sn[:, 0, :], PS[:, 2, 0:P]))
            for n in (1, 2):
                V.seq(nc.vector.scalar_tensor_tensor(Sn[:, n, :], Sn[:, n - 1, :], dcs[:, n:n + 1],
                                                     PS[:, 2, n * P:(n + 1) * P], ALU.mult, ALU.add))
            T.wait(V.tok())
            for q in range(NT):
                ops = [(AT[:, q, :], Ia[:, q, cols])] + [(QZ[:, n, :], Sn[:, n - 1, :])
                                                        for n in (2 * q, 2 * q + 1) if n > 0]
                for m, (a, b) in enumerate(ops):
                    T(nc.tensor.matmul(PS[:, 3, q * P:(q + 1) * P], a, b, start=(q == 0 and m == 0),
                                       stop=m == len(ops) - 1, skip_group_check=True))
            S.wait(T.tok())
            for q in range(NT):
                S.seq(nc.scalar.activation(junk, v3(3)[:, q, :], ACT.Square, accum_out=stt_[:, q:q + 1]))
            V.wait(S.tok())
            V.seq(nc.vector.tensor_scalar(stt_[:, 0:2], stt_[:, 0:2], 1.0 / P, EPS, ALU.mult, ALU.add))
            S.wait(V.tok())
            S.seq(nc.scalar.activation(stt_[:, 0:2], stt_[:, 0:2], ACT.Sqrt))
            V.wait(S.tok())
            V.seq(nc.vector.reciprocal(stt_[:, 2:4], stt_[:, 0:2]))
            for q in range(NT):
                V(nc.vector.scalar_tensor_tensor(O[:, q, :], v3(3)[:, q, :], stt_[:, 2 + q:3 + q],
                                                 Ga[:, q, cols], ALU.mult, ALU.mult))
            T.wait(V.tok())
            for q in range(NT):
                T(nc.tensor.transpose(PS[:, 4, q * P:(q + 1) * P], O[:, q, :], self.ident[:, :]))
            S.wait(T.tok())
            self.split(self.XH[:, hd, :], self.XL[:, hd, :], PS[:, 4, 0:SEQ], self.col["hgrn_norm_gain_2"][:, 0:1])
            T.wait(V.tok())
            S.wait(V.tok())
            G.wait(T.tok(), V.tok())
        self.join()

    def fox(self):
        nc, T, V, S, G = self.nc, self.T, self.V, self.S, self.G
        PS, Fb = self.PS, self.Fb
        nlf, t = self.view(0, NT, 8), [self.view(16 + 16 * k, NT, 8) for k in range(3)]
        MK, CU = self.view(64, NT, SEQ), self.view(576, NT, SEQ)
        pr, pT, st = self.view(1088, NT, SEQ), self.view(1600, NT, SEQ), self.view(2112, 8)
        Qs, Vs, nl = self.view(2120, SEQ), self.view(2376, NT, P), self.view(2632, NT)
        V.seq(nc.vector.tensor_tensor(Fb, Fb, self.rep(self.fxb[:, :], NT), ALU.add))
        self.log1p_exp_negabs(nlf, Fb, t)
        V.seq(nc.vector.tensor_scalar(t[0], Fb, 0.0, -1.0, ALU.min, ALU.mult))
        V.seq(nc.vector.tensor_tensor(nlf, nlf, t[0], ALU.add))
        G(nc.gpsimd.memset(MK, 0.0))
        G.seq(nc.gpsimd.memset(CU, 0.0))
        G.seq(nc.gpsimd.memset(MK[:, 0, P:SEQ], NEG))
        G(nc.gpsimd.tensor_copy(MK[:, 0, 0:P], self.negu[:, :]))
        G(nc.gpsimd.tensor_copy(MK[:, 1, P:SEQ], self.negu[:, :]))
        G(nc.gpsimd.tensor_copy(CU[:, 0, 0:P], self.triu[:, :]))
        G(nc.gpsimd.tensor_copy(CU[:, 0, P:SEQ], self.ones[:, :]))
        G(nc.gpsimd.tensor_copy(CU[:, 1, P:SEQ], self.triu[:, :]))
        self.join()
        with self.loop(GH, "fox_heads") as h:
            hd = ds(h, 1)
            S(nc.scalar.activation(Qs, self.Qb[:, hd, :], ACT.Copy, scale=float(P) ** -0.5))
            G(nc.gpsimd.tensor_copy(nl, nlf[:, :, hd]))
            G(nc.gpsimd.tensor_copy(Vs, self.Vb[:, :, ds(P * h, P)]))
            T.wait(S.tok(), G.tok())
            sc = PS[:, 0, :].rearrange("p (q m) -> p q m", q=NT)
            T(nc.tensor.matmul(sc, self.ident[:, :], MK, start=True, stop=False, skip_group_check=True))
            for s in range(NT):
                T(nc.tensor.matmul(sc, nl[:, s:s + 1].to_broadcast([P, P]),
                                   self.rep(CU[:, s, :], NT), start=False, stop=False, skip_group_check=True))
            for q in range(NT):
                T(nc.tensor.matmul(sc[:, q, :], Qs[:, q * P:(q + 1) * P], self.Kb[:, hd, :],
                                   start=False, stop=True, skip_group_check=True))
            V.wait(T.tok())
            T.wait(self.softmax_rows(sc, pr, st))
            for m in range(NT):
                for q in range(NT):
                    T(nc.tensor.transpose(PS[:, 1, m * SEQ + q * P:m * SEQ + q * P + P],
                                          pr[:, q, m * P:(m + 1) * P], self.ident[:, :]))
            S.wait(T.tok())
            S(nc.scalar.activation(pT, PS[:, 1, :].rearrange("p (m q) -> p m q", m=NT), ACT.Copy))
            T.wait(S.tok())
            for m in range(NT):
                T(nc.tensor.matmul(PS[:, 2, 0:SEQ], Vs[:, m, :], pT[:, m, :], start=m == 0, stop=m == 1))
            S.wait(T.tok())
            self.split(self.XH[:, ds(h + 8, 1), :], self.XL[:, ds(h + 8, 1), :], PS[:, 2, 0:SEQ])
            T.wait(V.tok())
            S.wait(V.tok())
            G.wait(T.tok())
        self.join()

    def ffn2(self, AH, AL, xn, buf, acc, tmp):
        nc, V, S, G, i, x = self.nc, self.V, self.S, self.G, self.i, self.x
        self.norm_to_feat(x, xn, self.stat, self.col["norm2_gain_2"], self.XH, self.XL)
        G(nc.gpsimd.memset(buf[:, :, 0:2], 0.0))
        self.join()
        wg, wu, wd = i["w_ffn_gate_2"][0], i["w_ffn_up_2"][0], i["w_ffn_down_2"][0]
        cw, cb = self.fcw, self.col["ffn_conv_b_2"]
        done = 0
        for part, nb in enumerate((4, 4, 3)):
            base = self.blk()

            def ev_gate(g, ps, ready):
                b = g + done
                S.wait(ready, V.tok())
                self.done_evac(nc.scalar.activation(buf[:, :, 2:2 + SEQ], ps, ACT.Copy))
                V.wait((self.s_evac, CREDIT + base + 2 * g + 1))
                for tap in range(3):
                    wt = self.bc(cw[:, tap, ds(4 * b, 4)], SEQ)
                    V.seq(nc.vector.tensor_tensor(tmp if tap else acc, buf[:, :, tap:tap + SEQ], wt, ALU.mult))
                    if tap:
                        V.seq(nc.vector.tensor_tensor(acc, acc, tmp, ALU.add))
                V.seq(nc.vector.tensor_tensor(acc, acc, self.bc(cb[:, ds(4 * b, 4)], SEQ), ALU.add))
                S.wait(V.tok())
                S(nc.scalar.activation(acc, acc, ACT.Silu))

            def ev_up(g, ps, ready):
                V.wait(ready, S.tok())
                V.seq(nc.vector.tensor_tensor(acc, acc, ps, ALU.mult))
                self.nc.vector.sem_inc(self.s_evac, 1)
                S.wait(V.tok())
                d = ds(4 * g, 4)
                S(nc.scalar.activation(AH[:, d, :], acc, ACT.Copy))
                V.wait(S.tok())
                V.seq(nc.vector.tensor_tensor(AL[:, d, :], acc, AH[:, d, :].bitcast(F32), ALU.subtract))
            c = lambda g: 512 * (g + done)
            self.stream(f"ffn2_up{part}", nb, [self.spec(wg, "feat", c, ev_gate), self.spec(wu, "feat", c, ev_up)])
            self.join()
            self.proj(f"ffn2_down{part}", wd, 0, 4, "tok", lambda j, L: self.ev_add(x, j, L),
                      kt=4 * nb, k0=512 * done, xh=AH, xl=AL)
            self.join()
            done += nb

    def run(self, stop_at=None):
        nc, ctx, i, sb = self.nc, self.ctx, self.i, self.sb
        T, V, S = self.T, self.V, self.S
        self.constants()
        self.param_cols = sb("param_cols", [P, 113 + 124 + 128 + 72])
        self.stat = sb("stat", [P, 4])
        self.mul = sb("mu_lora", [P, 4])
        self.dtb, self.alog, self.dsk, self.fxb = (sb(n, [P, m]) for n, m in
                                                   (("dt_bias", 16), ("a_log", 16), ("d_skip", 16), ("fox_bias", 8)))
        small = ExitStack()
        small.enter_context(nc.allow_non_contiguous_dma(reason="a few hundred values"))
        mu = i["rwkv_mu"][0].rearrange("(n a) -> n a", a=1)
        self.load(5, self.mul[0:LORA, 0:1], mu[3072:3072 + LORA, :])
        self.load(5, self.mul[0:LORA, 1:2], mu[3072 + LORA:3072 + 2 * LORA, :])
        for k in range(2):
            self.load(5, self.mul[:, 2 + k:3 + k], mu[3264 + k * P:3264 + (k + 1) * P, :])
        for t, n, m in ((self.dtb, "ssd_dt_bias", 16), (self.alog, "ssd_a_log", 16), (self.dsk, "ssd_d", 16),
                        (self.fxb, "fox_gate_bias_2", 8)):
            lt = self.load(5, t[:, :], i[n].to_broadcast([P, m]))
        small.close()
        self.arena_cm = self.open_arena("arena_a", 25920)
        self.params()
        for l in self.lanes:
            l.wait(lt)
        self.join()
        self.block1_in()
        if stop_at == "in":
            return
        self.ssd()
        self.rwkv()
        if stop_at == "mix":
            return
        self.arena_cm.close()
        self.x = sb("x", [P, NT, D])
        t = self.load(6, self.x[:, :, :], self.XTOK)
        cm = self.open_arena("arena_b", 21000)
        V.wait(t)
        self.proj("w_out", i["w_out"][0], 0, 4, "tok", lambda j, L: self.ev_add(self.x, j, L))
        self.join()
        if stop_at == "w_out":
            return
        self.cross()
        if stop_at == "cross":
            return
        cm.close()

        def ffn_scope():
            c = self.scope = ExitStack()
            t = [c.enter_context(nc.sbuf_tensor(f"{n}{self.ffn_no}", s, d)) for n, s, d in (
                ("act_hi", [P, 16, SEQ], F32R), ("act_lo", [P, 16, SEQ], F32R), ("xn", [P, NT, D], F32),
                ("buf", [P, 4, SEQ + 2], F32), ("acc", [P, 4, SEQ], F32), ("tmp", [P, 4, SEQ], F32))]
            self.ffn_no += 1
            return c, t
        self.ffn_no = 1
        c, (AH, AL, xn, buf, acc, tmp) = ffn_scope()
        self.ffn1(AH, AL, xn[:, :, :], tmp[:, :, :], acc[:, :, :])
        if stop_at == "ffn1":
            return
        c.close()
        cm = self.open_arena("arena_c", 21000)
        gb = self.view(4096, D)
        t = self.load(7, gb, i["final_norm_g"].rearrange("(a n) -> a n", a=1).to_broadcast([P, D]))
        V.wait(t)
        self.final_norm(self.x[:, :, :], self.x[:, :, :], gb, self.view(0, NT, D)[:, 0, :])
        self.join()
        self.hgrn()
        self.fox()
        if stop_at == "mix2":
            return
        cm.close()
        c, (AH, AL, xn, buf, acc, tmp) = ffn_scope()
        self.proj("w_out2", i["w_out_2"][0], 0, 4, "tok", lambda j, L: self.ev_add(self.x, j, L))
        self.join()
        self.ffn2(AH, AL, xn[:, :, :], buf[:, :, :], acc[:, :, :], tmp[:, :, :])
        gb = xn[:, 1, :]
        t = self.load(8, gb, i["final_norm_gain_2"].rearrange("(a n) -> a n", a=1).to_broadcast([P, D]))
        V.wait(t)
        self.final_norm(self.x[:, :, :], self.x[:, :, :], gb, xn[:, 0, :])
        nc.sync.wait_ge(*V.tok())
        s_out = self.newsem("stored")
        nc.sync.dma_start(self.out[0].rearrange("(t p) d -> p t d", p=P), self.x[:, :, :]).then_inc(s_out, 16)
        nc.sync.wait_ge(s_out, 16)
        c.close()

    def open_arena(self, name, words):
        c = self.scope = ExitStack()
        self.arena = c.enter_context(self.nc.sbuf_tensor(name, [P, words], F32))
        self.arena_words = words
        return c


NAMES = ["x", "mem", "norm_mix_g", "w_in", "ssd_conv_w", "ssd_conv_b", "ssd_dt_bias", "ssd_a_log", "ssd_d",
         "ssd_norm_g", "rwkv_mu", "rwkv_w0", "rwkv_w2", "rwkv_a0", "rwkv_a2", "rwkv_g2", "rwkv_k_k", "rwkv_k_a",
         "rwkv_r_k", "rwkv_ln_w", "rwkv_ln_b", "w_out", "norm_x_g", "norm_mem_g", "xattn_wq", "xattn_wk",
         "xattn_wv", "xattn_wo", "norm_ffn_g", "ffn_w1", "ffn_w2", "final_norm_g", "norm1_gain_2", "w_in_2",
         "hgrn_lb_param_2", "hgrn_norm_gain_2", "fox_gate_bias_2", "w_out_2", "norm2_gain_2", "w_ffn_gate_2",
         "w_ffn_up_2", "ffn_conv_w_2", "ffn_conv_b_2", "w_ffn_down_2", "final_norm_gain_2"]


def program(nc, ins, out, stop_at=None):
    with ExitStack() as ctx:
        m = Model(nc, ctx, ins, out)
        m.run(stop_at)
        m.scope.close()
        return m


def kernel(**inputs):
    import numpy as np
    import concourse.bacc as bacc
    from concourse.bass_utils import run_bass_kernel_spmd

    nc = bacc.Bacc("TRN2", target_bir_lowering=False, num_devices=1)
    arrays, ins = {}, {}
    for name in NAMES:
        a = np.ascontiguousarray(inputs[name])
        arrays["in_" + name] = a
        ins[name] = nc.dram_tensor("in_" + name, a.shape, F32, kind="ExternalInput").ap()
    out = nc.dram_tensor("out", (1, SEQ, D), F32, kind="ExternalOutput").ap()
    program(nc, ins, out)
    r = run_bass_kernel_spmd(nc, [arrays], core_ids=[0])
    return r.results[0]["out"]
```

```python
from contextlib import ExitStack

import concourse.bass as bass
from concourse import mybir

F32 = mybir.dt.float32
F32R = mybir.dt.float32r
ALU = mybir.AluOpType
ACT = mybir.ActivationFunctionType
AX = mybir.AxisListType
ds = bass.ds

P = 128
SEQ = 256
NT = SEQ // P
D = 2048
KD = D // P
EPS = 1e-6
NEG = -1e30

SSD_W, SSD_H, SSD_G, SSD_N, SSD_CONV = 1024, 16, 2, 128, 4
XBC = SSD_W + 2 * SSD_G * SSD_N
RW = 1024
RP = RW // P
RC = 64
NRC = SEQ // RC
LORA = 96
LN_EPS = 64e-5
XH_, XD = 4, 512
FF1, FF2 = 8192, 5632
GH = 8
HCH = 64

CREDIT = 64

STEPS = {
    "w_in_rkv": (0, 6, 0, 0),
    "rwkv_chunks": (232, 21, 13, 2),
    "xattn_heads": (40, 14, 10, 2),
    "ffn1_up0": (0, 4, 2, 0),
    "ffn1_up1": (0, 4, 2, 0),
    "ffn1_up2": (0, 4, 2, 0),
    "ffn1_up3": (0, 4, 2, 0),
    "hgrn_heads": (28, 20, 16, 4),
    "fox_heads": (48, 28, 20, 8),
    "ffn2_up0": (0, 8, 2, 0),
    "ffn2_up1": (0, 8, 2, 0),
    "ffn2_up2": (0, 8, 2, 0),
}


class Lane:

    def __init__(self, eng, sem, key):
        self.eng, self.sem, self.key = eng, sem, key
        self.const, self.terms = CREDIT, []

    def value(self):
        v = self.const
        for i, per in self.terms:
            v = i * per + v
        return v

    def tok(self):
        return (self.sem, self.value())

    def __call__(self, ins):
        ins.then_inc(self.sem, 1)
        self.const += 1
        return self.tok()

    def wait(self, *toks):
        for sem, v in toks:
            self.eng.wait_ge(sem, v)

    def seq(self, ins):
        t = self(ins)
        self.wait(t)
        return t


class Prog:
    def __init__(self, nc, ctx, ins, out):
        self.nc, self.ctx, self.i, self.out = nc, ctx, ins, out
        sem = lambda n: ctx.enter_context(nc.semaphore(n))
        self.newsem = sem
        self.T = Lane(nc.tensor, sem("tensor_done"), "T")
        self.V = Lane(nc.vector, sem("vector_done"), "V")
        self.S = Lane(nc.scalar, sem("scalar_done"), "S")
        self.G = Lane(nc.gpsimd, sem("gpsimd_done"), "G")
        self.lanes = [self.T, self.V, self.S, self.G]
        self.ring_full = [sem(f"ring_full{q}") for q in range(4)]
        self.s_hi, self.s_lo = sem("weights_hi"), sem("weights_lo")
        self.s_mm, self.s_evac = sem("half_multiplied"), sem("block_evacuated")
        self.tile_const, self.tile_terms = 0, []
        self.blk_const, self.blk_terms = 0, []
        self.pend, self.par0 = None, 0
        self.s_par = [sem(f"params{k}") for k in range(12)]
        self.par_n = [0] * 12
        for s, e in ((self.T.sem, nc.tensor), (self.s_mm, nc.tensor), (self.V.sem, nc.vector),
                     (self.s_lo, nc.vector), (self.S.sem, nc.scalar), (self.s_hi, nc.scalar),
                     (self.s_evac, nc.vector), (self.G.sem, nc.gpsimd)):
            e.sem_inc(s, CREDIT)
        sb = lambda n, s, d=F32: ctx.enter_context(nc.sbuf_tensor(n, s, d))
        self.sb = sb
        self.raw = sb("raw", [P, 4, 4, 512])
        self.whi = sb("whi", [P, 4, 2, 512], F32R)
        self.wlo = sb("wlo", [P, 4, 2, 512], F32R)
        self.XH = sb("XH", [P, KD, SEQ], F32R)
        self.XL = sb("XL", [P, KD, SEQ], F32R)
        self.PS = ctx.enter_context(nc.psum_tensor("PS", [P, 8, 512], F32))

    def loop(self, n, name, tiles=0, blks=0):
        return LoopScope(self, n, name, tiles, blks)

    def view(self, off, *shape):
        n = 1
        for s in shape:
            n *= s
        assert off + n <= self.arena_words, (off + n, self.arena_words)
        v = self.arena[:, off:off + n]
        if len(shape) == 2:
            v = v.rearrange("p (a b) -> p a b", a=shape[0])
        if len(shape) == 3:
            v = v.rearrange("p (a b c) -> p a b c", a=shape[0], b=shape[1])
        return v

    def join(self, *extra):
        self.flush()
        toks = [l.tok() for l in self.lanes] + [(self.s_evac, CREDIT + self.blk_const),
                                                (self.s_mm, CREDIT + 2 * self.tile_const)] + list(extra)
        for l in self.lanes:
            for t in toks:
                if t[0] is not l.sem:
                    l.wait(t)
            l.wait(l.tok())

    def load(self, k, dst, src, eng=None):
        (eng or self.nc.scalar).dma_start(dst, src).then_inc(self.s_par[k], 16)
        self.par_n[k] += 16
        return (self.s_par[k], self.par_n[k])

    def tile(self):
        v = self.tile_const
        for i, per in self.tile_terms:
            v = i * per + v
        return v

    def blk(self):
        v = self.blk_const
        for i, per in self.blk_terms:
            v = i * per + v
        return v

    def blocks(self, todo, prev=None, ahead=0, banks=2, late=None):
        nc, T, V, S = self.nc, self.T, self.V, self.S
        t0, tc, b0, par0 = self.tile(), self.tile_const, self.blk(), self.par0
        halves, nt = [], 0
        for j, (spec, g) in enumerate(todo):
            nq = (spec["kt"] + 3) // 4
            for q in range(nq):
                for u in range(2):
                    halves.append((j, spec, g, nt, q, u, q == nq - 1 and u == 1))
                nt += 1
        ends = {}

        def split(n):
            j, spec, g, tn, q, u, _ = halves[n]
            t, slot, ncol = t0 + tn, (tc + tn) % 4, sum(spec["widths"])
            if u == 0:
                k = spec["k0"] + 512 * q
                nc.sync.wait_ge(self.s_lo, 2 * t - 6 + CREDIT)
                nc.sync.dma_start(self.raw[:, slot, :, 0:ncol],
                                  spec["w"][k:k + 512, ds(spec["col"](g), ncol)]
                                  .rearrange("(a p) n -> p a n", p=P)).then_inc(self.ring_full[slot], 16)
            h, hs = 2 * t + u, (2 * (tc + tn) + u) % 4
            raw = self.raw[:, slot, 2 * u:2 * u + 2, 0:ncol]
            hi, lo = self.whi[:, hs, :, 0:ncol], self.wlo[:, hs, :, 0:ncol]
            nc.scalar.wait_ge(self.ring_full[slot], 4 * (t - slot) + 16)
            nc.scalar.wait_ge(self.s_mm, h - 3 + CREDIT)
            nc.scalar.activation(hi, raw, ACT.Copy).then_inc(self.s_hi, 1)
            nc.vector.wait_ge(self.s_hi, h + 1 + CREDIT)
            nc.vector.tensor_tensor(lo, raw, hi.bitcast(F32), ALU.subtract).then_inc(self.s_lo, 1)

        def multiply(n):
            j, spec, g, tn, q, u, last_half = halves[n]
            ncol, widths, xh, xl = sum(spec["widths"]), spec["widths"], spec["xh"], spec["xl"]
            par = (par0 + j) % banks
            ps = self.PS[:, 2 * par:2 * par + 2, :]
            h, hs = 2 * (t0 + tn) + u, (2 * (tc + tn) + u) % 4
            if q == 0 and u == 0:
                nc.tensor.wait_ge(self.s_evac, b0 + j - banks + 1 + CREDIT)
            nc.tensor.wait_ge(self.s_lo, h + 1 + CREDIT)
            for a in range(2):
                k = 4 * q + 2 * u + a
                for m, (wt, xt) in enumerate(((self.whi, xh), (self.whi, xl), (self.wlo, xh))):
                    first, last = k == 0 and m == 0, k == spec["kt"] - 1 and m == 2
                    if spec["mode"] == "tok":
                        for tt in range(NT):
                            mm = nc.tensor.matmul(ps[:, tt, 0:ncol], xt[:, k, tt * P:(tt + 1) * P],
                                                  wt[:, hs, a, 0:ncol], start=first, stop=last)
                    else:
                        o = 0
                        for f, wd in enumerate(widths):
                            mm = nc.tensor.matmul(ps[0:wd, f // 2, (f % 2) * SEQ:(f % 2) * SEQ + SEQ],
                                                  wt[:, hs, a, o:o + wd], xt[:, k, :],
                                                  start=first and f % 2 == 0, stop=last,
                                                  skip_group_check=True)
                            o += wd
            mm.then_inc(self.s_mm, 1)

        def evacuation(j):
            return self.evac_of(todo[j][0], todo[j][1], (par0 + j) % banks, t0 + ends[j], b0 + j)

        for n in range(min(ahead, len(halves))):
            split(n)
        since = 0
        for n, (j, spec, g, tn, q, u, last_half) in enumerate(halves):
            if q == 0 and u == 0:
                since = 0
            if n + ahead < len(halves):
                split(n + ahead)
            if late is not None and j == 0 and 4 * q >= late and u == 0:
                for _ in prev or ():
                    pass
                prev = None
                self.T.wait(self.V.tok(), self.S.tok())
            multiply(n)
            since += 1
            if prev is not None and since >= 2:
                prev = None if next(prev, True) else prev
            if last_half:
                for _ in prev or ():
                    pass
                ends[j] = tn + 1
                prev = evacuation(j)
            yield
        self.tile_const += nt
        self.blk_const += len(todo)
        self.par0 = (par0 + len(todo)) % banks
        return prev

    def stream(self, name, groups, specs, ahead=0, late=None):
        L = len(specs)
        assert L % 2 == 0 or groups == 1
        if late is not None:
            self.T.wait(self.V.tok(), self.S.tok())
        self.pend = yield from self.blocks([(sp, 0) for sp in specs], self.pend, ahead, late=late)
        if groups > 1:
            def left_over(g):
                return self.evac_of(specs[-1], g, (self.par0 - 1) % 2, self.tile(), self.blk() - 1)
            with self.loop(groups - 1, name, sum((sp["kt"] + 3) // 4 for sp in specs), L) as i:
                yield from self.blocks([(sp, i + 1) for sp in specs], left_over(i))
            self.pend = left_over(groups - 1)

    def evac_of(self, spec, g, par, tiles, block):
        ps = self.PS[:, 2 * par:2 * par + 2, :]
        if spec["mode"] == "feat":
            ps = ps.rearrange("p a (f t) -> p (a f) t", t=SEQ)
        return spec["evac"](g, ps, (self.s_mm, 2 * tiles + CREDIT), (self.s_evac, block + 1 + CREDIT))

    def flush(self):
        for _ in self.pend or ():
            pass
        self.pend = None

    def run_now(self, gen):
        for _ in gen:
            pass

    def together(self, *gens):
        gens = list(gens)
        while gens:
            for item in list(gens):
                gen, n = item
                for _ in range(n):
                    if next(gen, self) is self:
                        gens.remove(item)
                        break

    def done_evac(self, ins):
        ins.then_inc(self.s_evac, 1)

    def constants(self):
        nc, G, V, sb = self.nc, self.G, self.V, self.sb
        self.ident = sb("ident", [P, P])
        self.ones = sb("ones", [P, P])
        self.triu = sb("triu", [P, P])
        self.negl = sb("negl", [P, P])
        self.negu = sb("negu", [P, P])
        self.sel = sb("sel", [P, RP, 16])
        self.selT = sb("selT", [16, RP, 2])
        self.m_in = sb("m_in", [P, P])
        self.m_st = sb("m_st", [P, P])
        self.m_d = sb("m_d", [P, P])
        self.m_o = sb("m_o", [P, P])
        self.m_dT = sb("m_dT", [P, P])
        self.m_ic = sb("m_ic", [P, RC])
        self.rst = sb("rst", [P, SEQ])

        def sel(dst, src, pattern, base, cm, op, fill):
            return G.seq(nc.gpsimd.affine_select(out=dst, in_=src, pattern=pattern, compare_op=op,
                                                 fill=fill, base=base, channel_multiplier=cm))
        ge, ne = ALU.is_ge, ALU.not_equal
        for t, v in ((self.ident, 0.0), (self.ones, 1.0), (self.triu, 1.0), (self.negl, 0.0),
                     (self.negu, 0.0), (self.sel, 1.0), (self.selT, 1.0), (self.m_in, 1.0),
                     (self.m_st, 1.0), (self.m_d, -1.0), (self.m_o, -1.0), (self.m_dT, -1.0),
                     (self.m_ic, 1.0), (self.rst, 1.0)):
            ap = t[:, :] if len(t.shape) == 2 else t[:, :, :]
            G.seq(nc.gpsimd.memset(ap, v))
        I, one = self.ident[:, :], [[1, P]]
        sel(I, I, [[-1, P]], 0, 1, ne, 1.0)
        up = lambda t, fill, base=0: sel(t[:, :], t[:, :], one, base, -1, ge, fill)
        up(self.triu, 0.0)
        up(self.negl, NEG)
        sel(self.negu[:, :], self.negu[:, :], [[-1, P]], 0, 1, ge, NEG)
        up(self.m_in, 0.0)
        up(self.m_st, 0.0, -1)
        up(self.m_d, 0.0, -1)
        up(self.m_o, 0.0, -1)
        sel(self.m_dT[:, :], self.m_dT[:, :], [[-1, P]], -1, 1, ge, 0.0)

        def same_block(t, n):
            for lo, cm, st in ((0, 1, -n), (n - 1, -1, n)):
                v = t[:, :].rearrange("p (j e) -> p j e", e=n)
                sel(v, v, [[st, P // n], [0, n]], lo, cm, ge, 0.0)
        same_block(self.m_in, RC)
        same_block(self.m_st, RC)
        same_block(self.m_d, 16)
        same_block(self.m_dT, 16)
        same_block(self.m_o, RC)
        V.wait(G.tok())
        V.seq(nc.vector.tensor_tensor(self.m_o[:, :], self.m_o[:, :], self.m_d[:, :], ALU.subtract))
        for t, pat, cm in ((self.sel[:, :, :], [[128, RP], [-64, 16]], 1),
                           (self.selT[:, :, :], [[-2, RP], [-1, 2]], 1)):
            if pat[0][0] == 128:
                sel(t, t, pat, 0, 1, ge, 0.0)
                sel(t, t, [[-128, RP], [64, 16]], 63, -1, ge, 0.0)
            else:
                sel(t, t, pat, 0, 1, ge, 0.0)
                sel(t, t, [[2, RP], [1, 2]], 0, -1, ge, 0.0)
        for hp in range(2):
            v = self.m_ic[hp * 64:hp * 64 + 64, :]
            sel(v, v, [[1, RC]], 0, -1, ge, 0.0)
        v = self.rst[:, :].rearrange("p (c e) -> p c e", e=RC)
        sel(v, v, [[0, NRC], [1, RC]], -1, 0, ge, 0.0)

    def params(self):
        nc, T, S, i = self.nc, self.T, self.S, self.i
        groups = [
            [("norm_mix_g", 16), ("norm_x_g", 16), ("norm_mem_g", 16), ("norm_ffn_g", 16),
             ("norm1_gain_2", 16), ("norm2_gain_2", 16), ("hgrn_lb_param_2", 16), ("hgrn_norm_gain_2", 1)],
            [("ssd_conv_w", 48), ("ssd_conv_b", 12), ("ssd_norm_g", 8), ("rwkv_w0", 8), ("rwkv_a0", 8),
             ("rwkv_k_k", 8), ("rwkv_k_a", 8), ("rwkv_r_k", 8), ("rwkv_ln_w", 8), ("rwkv_ln_b", 8)],
            [("ffn_conv_w_2", 128)],
            [("ffn_conv_w_2b", 4), ("ffn_conv_b_2", 44), ("mu", 24)],
        ]
        rows = [self.view(P * n, P) for n in range(len(groups))]
        self.col = {}
        base = 0
        cols = self.param_cols
        flat = lambda a: self.flat(a)
        for k, g in enumerate(groups):
            r = 0
            for name, n in g:
                if name == "ffn_conv_w_2":
                    src = flat(i[name]).rearrange("(n p) -> n p", p=P)[0:128, :]
                elif name == "ffn_conv_w_2b":
                    src = flat(i["ffn_conv_w_2"]).rearrange("(n p) -> n p", p=P)[128:132, :]
                elif name == "mu":
                    src = flat(i["rwkv_mu"])[0:3072].rearrange("(n p) -> n p", p=P)
                else:
                    src = flat(i[name]).rearrange("(n p) -> n p", p=P)
                t = self.load(0, rows[k][r:r + n, :], src)
                self.col[name] = cols[:, base + r:base + r + n]
                r += n
            base += r
        self.cols = cols
        self.colbase = base
        T.wait(t, self.G.tok())
        base = 0
        for k, g in enumerate(groups):
            r = sum(n for _, n in g)
            tt = T(nc.tensor.transpose(self.PS[:, k, 0:r], rows[k][0:r, :], self.ident[0:r, 0:r]))
            S.wait(tt)
            S(nc.scalar.activation(cols[:, base:base + r], self.PS[:, k, 0:r], ACT.Copy))
            base += r
        c0 = [0]
        o = 0
        for g in groups:
            for name, n in g:
                if name == "ffn_conv_w_2":
                    self.fcw = cols[:, o:o + 132].rearrange("p (j f) -> p j f", f=44)
                o += n

    def flat(self, a):
        while len(a.shape) > 1:
            names = " ".join(f"d{k}" for k in range(len(a.shape)))
            a = a.rearrange(f"{names} -> ({names})")
        return a

    def rstd(self, src, stat, junk, n, eps=EPS):
        nc, V, S = self.nc, self.V, self.S
        for tt in range(NT):
            S.seq(nc.scalar.activation(junk, src(tt), ACT.Square, accum_out=stat[:, tt:tt + 1]))
        V.wait(S.tok())
        V.seq(nc.vector.tensor_scalar(stat[:, 0:NT], stat[:, 0:NT], 1.0 / n, eps, ALU.mult, ALU.add))
        S.wait(V.tok())
        S.seq(nc.scalar.activation(stat[:, 0:NT], stat[:, 0:NT], ACT.Sqrt))
        V.wait(S.tok())
        return V.seq(nc.vector.reciprocal(stat[:, 0:NT], stat[:, 0:NT]))

    def to_feat(self, src, gain, xh, xl, n, k0=0):
        nc, T, V, S = self.nc, self.T, self.V, self.S
        for k in range(n):
            if k >= 8:
                T.wait(v_at[k - 8])
            for tt in range(NT):
                t = T(nc.tensor.transpose(self.PS[:, k % 8, tt * P:(tt + 1) * P], src(tt, k),
                                          self.ident[:, :]))
            S.wait(t)
            ps = self.PS[:, k % 8, 0:SEQ]
            s = S(nc.scalar.activation(xh[:, k0 + k, :], ps, ACT.Copy, scale=gain[:, k:k + 1]))
            V.wait(s)
            v = V(nc.vector.scalar_tensor_tensor(xl[:, k0 + k, :], ps, gain[:, k:k + 1],
                                                 xh[:, k0 + k, :].bitcast(F32), ALU.mult, ALU.subtract))
            if k == 0:
                v_at = {}
            v_at[k] = v

    def norm_to_feat(self, x, xn, stat, gain, xh, xl):
        nc, V, T = self.nc, self.V, self.T
        self.rstd(lambda tt: x[:, tt, :], stat, xn[:, 0, :], D)
        for tt in range(NT):
            V(nc.vector.tensor_scalar(xn[:, tt, :], x[:, tt, :], stat[:, tt:tt + 1], None, ALU.mult))
        T.wait(V.tok())
        self.to_feat(lambda tt, k: xn[:, tt, k * P:(k + 1) * P], gain, xh, xl, KD)


class LoopScope:

    def __init__(self, prog, n, name, tiles, blks):
        self.p, self.n, self.name, self.tiles, self.blks = prog, n, name, tiles, blks

    def __enter__(self):
        p = self.p
        self.steps = STEPS.get(self.name, (0, 0, 0, 0))
        self.start = [l.const for l in p.lanes]
        self.t0, self.b0 = p.tile_const, p.blk_const
        self.cm = p.nc.Fori(0, self.n)
        i = self.cm.__enter__()
        for l, s in zip(p.lanes, self.steps):
            l.terms.append((i, s))
        p.tile_terms.append((i, self.tiles))
        p.blk_terms.append((i, self.blks))
        return i

    def __exit__(self, *exc):
        p = self.p
        self.cm.__exit__(*exc)
        if exc[0] is not None:
            return False
        made = tuple(l.const - s for l, s in zip(p.lanes, self.start))
        assert made == tuple(self.steps), (self.name, made)
        assert p.tile_const - self.t0 == self.tiles and p.blk_const - self.b0 == self.blks
        for l, s, m in zip(p.lanes, self.start, made):
            l.const = s + self.n * m
            l.terms.pop()
        p.tile_const = self.t0 + self.n * self.tiles
        p.blk_const = self.b0 + self.n * self.blks
        p.tile_terms.pop()
        p.blk_terms.pop()
        return False


class Model(Prog):

    def bc(self, ap, n):
        return ap.unsqueeze(2).to_broadcast([ap.shape[0], ap.shape[1], n])

    def rep(self, ap, n):
        return ap.unsqueeze(1).to_broadcast([ap.shape[0], n, ap.shape[1]])

    def spec(self, w, mode, col, evac, kt=KD, k0=0, xh=None, xl=None, widths=None):
        return dict(w=w, k0=k0, kt=kt, xh=xh if xh is not None else self.XH, xl=xl if xl is not None else self.XL,
                    mode=mode, col=col, evac=evac,
                    widths=widths or ([512] if mode == "tok" else [P] * 4))

    def ev_feat(self, dst, j, L, func=ACT.Copy):
        def evac(g, ps, ready, out):
            self.S.wait(ready)
            self.done_evac(self.nc.scalar.activation(dst[:, ds(4 * (g * L + j), 4), :], ps, func))
            yield
        return evac

    def ev_tok(self, dst, j, L, func=ACT.Copy):
        def evac(g, ps, ready, out):
            self.S.wait(ready)
            self.done_evac(self.nc.scalar.activation(dst[:, :, ds(512 * (g * L + j), 512)], ps, func))
            yield
        return evac

    def ev_add(self, x, j, L):
        def evac(g, ps, ready, out):
            self.V.wait(ready)
            o = x[:, :, ds(512 * (g * L + j), 512)]
            self.done_evac(self.nc.vector.tensor_tensor(o, o, ps, ALU.add))
            yield
        return evac

    def proj(self, name, w, c0, n, mode, ev, kt=KD, k0=0, xh=None, xl=None, late=None):
        L = 2 if n > 2 else n
        specs = [self.spec(w, mode, (lambda g, j=j: 512 * (g * L + j) + c0), ev(j, L), kt, k0, xh, xl)
                 for j in range(L)]
        self.run_now(self.stream(name, n // L, specs, late=late))

    def shift_mix(self, buf, tmp, mu, dst, p, f0, f1):
        nc, V = self.nc, self.V
        u, up, t = buf[0:p, f0:f1, 1:1 + SEQ], buf[0:p, f0:f1, 0:SEQ], tmp[0:p, f0:f1, :]
        V.seq(nc.vector.tensor_tensor(t, up, u, ALU.subtract))
        V.seq(nc.vector.tensor_tensor(t, t, self.bc(mu, SEQ), ALU.mult))
        V.seq(nc.vector.tensor_tensor(dst, u, t, ALU.add))

    def log1p_exp_negabs(self, out, x, t):
        nc, V, S = self.nc, self.V, self.S
        e, u, d = t
        V.seq(nc.vector.scalar_tensor_tensor(e, x, -1.0, x, ALU.mult, ALU.max))
        S.wait(V.tok())
        S.seq(nc.scalar.activation(e, e, ACT.Exp, scale=-1.0))
        V.wait(S.tok())
        V.seq(nc.vector.tensor_scalar(u, e, 1.0, None, ALU.add))
        S.wait(V.tok())
        S(nc.scalar.activation(out, u, ACT.Ln))
        V.seq(nc.vector.tensor_scalar(d, u, -1.0, 5e-8, ALU.add, ALU.max))
        V.seq(nc.vector.reciprocal(d, d))
        V.seq(nc.vector.tensor_tensor(d, d, e, ALU.mult))
        V.wait(S.tok())
        V.seq(nc.vector.tensor_tensor(out, out, d, ALU.mult))
        V.seq(nc.vector.tensor_scalar(u, e, -0.5, 1.0, ALU.mult, ALU.add))
        V.seq(nc.vector.tensor_tensor(u, u, e, ALU.mult))
        V.seq(nc.vector.tensor_tensor(out, out, u, ALU.max))

    def split(self, xh, xl, ps, scale=None):
        nc, V, S = self.nc, self.V, self.S
        if scale is None:
            S(nc.scalar.activation(xh, ps, ACT.Copy))
            V.wait(S.tok())
            return V(nc.vector.tensor_tensor(xl, ps, xh.bitcast(F32), ALU.subtract))
        S(nc.scalar.activation(xh, ps, ACT.Copy, scale=scale))
        V.wait(S.tok())
        return V(nc.vector.scalar_tensor_tensor(xl, ps, scale, xh.bitcast(F32), ALU.mult, ALU.subtract))

    def block1_in(self):
        nc, V, S, G, i = self.nc, self.V, self.S, self.G, self.i
        w = i["w_in"][0]
        Z = self.Z = self.view(0, NT, SSD_W)
        XBC_ = self.XBC = self.view(2048, 12, SEQ)
        RKV = self.RKV = self.view(5120, 24, SEQ)
        LO = self.LO = self.view(11264, 4, SEQ)
        DT = self.DT = self.view(12288, NT, 16)
        x, xn, stat = self.view(12320, NT, D), self.view(16416, NT, D), self.view(20512, 16)
        buf3, buf1 = self.view(20528, 4, SEQ + 3), self.view(21568, 4, SEQ + 1)
        tmp, acc = self.view(22600, 4, SEQ), self.view(23624, 4, SEQ)
        self.XTOK = i["x"][0].rearrange("(t p) d -> p t d", p=P)
        t = self.load(1, x, self.XTOK)
        G(nc.gpsimd.memset(buf3[:, :, 0:3], 0.0))
        G(nc.gpsimd.memset(buf1[:, :, 0:1], 0.0))
        S.wait(t)
        V.wait(t)
        self.T.wait(S.tok())
        self.norm_to_feat(x, xn, stat, self.col["norm_mix_g"], self.XH, self.XL)
        self.join()

        def ev_rkv(j, L):
            def evac(g, ps, ready, out):
                S.wait(ready, V.tok())
                self.done_evac(nc.scalar.activation(buf1[:, :, 1:1 + SEQ], ps, ACT.Copy))
                yield
                V.wait(out)
                b = g * L + j
                self.shift_mix(buf1, tmp, self.col["mu"][:, ds(4 * b, 4)], RKV[:, ds(4 * b, 4), :], P, 0, 4)
                yield
            return evac

        def ev_xbc(j):
            def evac(g, ps, ready, out):
                S.wait(ready, V.tok())
                self.done_evac(nc.scalar.activation(buf3[:, :, 3:3 + SEQ], ps, ACT.Copy))
                yield
                V.wait(out)
                cw = self.col["ssd_conv_w"]
                for tap in range(SSD_CONV):
                    src = buf3[:, :, tap:tap + SEQ]
                    wt = self.bc(cw[:, 12 * tap + 4 * j:12 * tap + 4 * j + 4], SEQ)
                    if tap == 0:
                        V.seq(nc.vector.tensor_tensor(acc, src, wt, ALU.mult))
                    else:
                        V.seq(nc.vector.tensor_tensor(tmp, src, wt, ALU.mult))
                        V.seq(nc.vector.tensor_tensor(acc, acc, tmp, ALU.add))
                    yield
                V.seq(nc.vector.tensor_tensor(acc, acc, self.bc(self.col["ssd_conv_b"][:, 4 * j:4 * j + 4], SEQ),
                                              ALU.add))
                yield
                S.wait(V.tok())
                S(nc.scalar.activation(XBC_[:, 4 * j:4 * j + 4, :], acc, ACT.Silu))
                V.wait(S.tok())
            return evac

        def ev_lora(g, ps, ready, out):
            S.wait(ready, V.tok())
            S.seq(nc.scalar.activation(buf1[0:LORA, 0:2, 1:1 + SEQ], ps[0:LORA, 0:2, :], ACT.Copy))
            self.done_evac(nc.scalar.activation(buf1[:, 2:4, 1:1 + SEQ], ps[:, 2:4, :], ACT.Copy))
            yield
            V.wait(S.tok(), out)
            self.shift_mix(buf1, tmp, self.mul[0:LORA, 0:2], LO[0:LORA, 0:2, :], LORA, 0, 2)
            self.shift_mix(buf1, tmp, self.mul[:, 2:4], LO[:, 2:4, :], P, 2, 4)

        def ev_dt(g, ps, ready, out):
            S.wait(ready)
            self.done_evac(nc.scalar.activation(DT, ps[:, :, 0:16], ACT.Copy))
            yield

        self.proj("w_in_rkv", w, 2576, 6, "feat", ev_rkv)
        sp = [self.spec(w, "feat", (lambda g, j=j: 1024 + 512 * j), ev_xbc(j)) for j in range(3)]
        sp.append(self.spec(w, "feat", lambda g: 2576 + 3072, ev_lora, widths=[LORA, LORA, P, P]))
        sp += [self.spec(w, "tok", (lambda g, j=j: 512 * j), self.ev_tok(Z, j, 2, ACT.Silu)) for j in range(2)]
        sp.append(self.spec(w, "tok", lambda g: 2560, ev_dt, widths=[16]))
        self.run_now(self.stream("w_in_rest", 1, sp))
        self.join()

    def ssd(self):
        nc, T, V, S, G = self.nc, self.T, self.V, self.S, self.G
        PS, DT, XB, Z = self.PS, self.DT, self.XBC, self.Z
        o = 12320
        xs = self.view(o, NT, SSD_W)
        bm = self.view(o + 2048, NT, 256)
        xdt = self.view(o + 2560, NT, SSD_W)
        xdte = self.view(o + 4608, SSD_W)
        cbT = self.view(o + 5632, P)
        LT = self.view(o + 5760, 4, P)
        AT = self.view(o + 6272, 4, P)
        st = self.view(o + 6784, SSD_G, 512)
        y = self.view(o + 7808, NT, SSD_W)
        sm = [self.view(o + 9856 + 32 * k, NT, 16) for k in range(10)]
        junk = self.view(o + 10240, 512)
        dt, da, cs, ecs, dte, t0, t1, t2, ncs, rs = sm
        n = 0
        for c in range(NT):
            for q in range(3):
                fs = range(4 * q, min(4 * q + 4, 10))
                bank = n % 4
                n += 1
                if n > 4:
                    T.wait(hist[n - 5])
                else:
                    hist = {} if n == 1 else hist
                for k, f in enumerate(fs):
                    T(nc.tensor.transpose(PS[:, bank, k * P:(k + 1) * P], XB[:, f, c * P:(c + 1) * P],
                                          self.ident[:, :]))
                S.wait(T.tok())
                dst = xs[:, c, 512 * q:512 * q + 512] if q < 2 else bm[:, c, :]
                hist[n - 1] = S(nc.scalar.activation(dst, PS[:, bank, 0:P * len(fs)], ACT.Copy))
        A = self.view(o + 10752, 16)
        S.seq(nc.scalar.activation(A, self.alog[:, :], ACT.Exp))
        V.seq(nc.vector.tensor_tensor(DT, DT, self.rep(self.dtb[:, :], NT), ALU.add))
        self.log1p_exp_negabs(dt, DT, (t0, t1, t2))
        V.seq(nc.vector.scalar_tensor_tensor(dt, DT, 0.0, dt, ALU.max, ALU.add))
        V.seq(nc.vector.tensor_tensor(da, dt, self.rep(A, NT), ALU.mult))
        V.seq(nc.vector.tensor_scalar(da, da, -1.0, None, ALU.mult))
        T.wait(V.tok(), S.tok())
        T(nc.tensor.matmul(PS[:, 4, 0:32], self.triu[:, :], da, start=True, stop=True))
        t = T(nc.tensor.matmul(PS[:, 5, 0:32], self.ones[:, :], da, start=True, stop=True))
        V.wait(t)
        as2 = lambda b: PS[:, b, 0:32].rearrange("p (c h) -> p c h", c=NT)
        V.seq(nc.vector.tensor_copy(cs, as2(4)))
        V.seq(nc.vector.tensor_tensor(dte, as2(5), cs, ALU.subtract))
        V.seq(nc.vector.tensor_scalar(ncs, cs, -1.0, None, ALU.mult))
        S.wait(V.tok())
        S(nc.scalar.activation(ecs, cs, ACT.Exp))
        S.seq(nc.scalar.activation(dte, dte, ACT.Exp))
        hv = lambda ap: ap.rearrange("p (h e) -> p h e", e=64)
        for c in range(NT):
            V.seq(nc.vector.tensor_tensor(hv(xdt[:, c, :]), hv(xs[:, c, :]), self.bc(dt[:, c, :], 64), ALU.mult))
        V.wait(S.tok())
        V.seq(nc.vector.tensor_tensor(hv(xdte), hv(xdt[:, 0, :]), self.bc(dte[:, 0, :], 64), ALU.mult))
        T.wait(V.tok())
        for g in range(SSD_G):
            T(nc.tensor.matmul(PS[:, 6 + g, :], bm[:, 0, g * P:(g + 1) * P], xdte[:, g * 512:g * 512 + 512],
                               start=True, stop=True))
        S.wait(T.tok())
        S(nc.scalar.activation(st, PS[:, 6:8, :], ACT.Copy))
        T.wait(S.tok())
        for c in range(NT):
            for g in range(SSD_G):
                cm, bmT = XB[:, 10 + g, c * P:(c + 1) * P], XB[:, 8 + g, c * P:(c + 1) * P]
                T(nc.tensor.matmul(PS[:, 0, 0:P], bmT, cm, start=True, stop=True))
                V.wait(T.tok())
                V(nc.vector.tensor_copy(cbT, PS[:, 0, 0:P]))
                if c > 0:
                    T(nc.tensor.matmul(PS[:, 2, :], cm, st[:, g, :], start=True, stop=True))
                for q in range(2):
                    T(nc.tensor.matmul(PS[:, 4 + q, :], self.ident[:, :], self.rep(self.negl[:, :], 4),
                                       start=True, stop=False, skip_group_check=True))
                    for e in range(4):
                        h = 8 * g + 4 * q + e
                        lhs = da[:, c, h:h + 1].to_broadcast([P, P])
                        T(nc.tensor.matmul(PS[:, 4 + q, e * P:(e + 1) * P], lhs, self.triu[:, :],
                                           start=False, stop=True, skip_group_check=True))
                    S.wait(T.tok(), V.tok())
                    for e in range(4):
                        h = 8 * g + 4 * q + e
                        S(nc.scalar.activation(LT[:, e, :], PS[:, 4 + q, e * P:(e + 1) * P], ACT.Exp,
                                               bias=ncs[:, c, h:h + 1]))
                    V.wait(S.tok(), T.tok())
                    V.seq(nc.vector.tensor_tensor(AT, LT, self.rep(cbT, 4), ALU.mult))
                    T.wait(V.tok())
                    for e in range(4):
                        h = 8 * g + 4 * q + e
                        T(nc.tensor.matmul(PS[:, 1, (4 * q + e) * 64:(4 * q + e) * 64 + 64], AT[:, e, :],
                                           xdt[:, c, h * 64:h * 64 + 64], start=(q == 0 and e == 0),
                                           stop=True, skip_group_check=True))
                    V.wait(T.tok())
                yg = y[:, c, g * 512:g * 512 + 512]
                xg = xs[:, c, g * 512:g * 512 + 512]
                V.seq(nc.vector.tensor_tensor(hv(yg), hv(xg), self.bc(self.dsk[:, 8 * g:8 * g + 8], 64), ALU.mult))
                V.seq(nc.vector.tensor_tensor(yg, yg, PS[:, 1, :], ALU.add))
                if c > 0:
                    V.wait(S.tok())
                    V.seq(nc.vector.tensor_tensor(hv(junk), hv(PS[:, 2, :]),
                                                  self.bc(ecs[:, c, 8 * g:8 * g + 8], 64), ALU.mult))
                    V.seq(nc.vector.tensor_tensor(yg, yg, junk, ALU.add))
                V.seq(nc.vector.tensor_tensor(yg, yg, Z[:, c, g * 512:g * 512 + 512], ALU.mult))
                T.wait(V.tok())
        S.wait(V.tok())
        for c in range(NT):
            for g in range(SSD_G):
                S.seq(nc.scalar.activation(junk, y[:, c, g * 512:g * 512 + 512], ACT.Square,
                                           accum_out=rs[:, c, g:g + 1]))
        V.wait(S.tok())
        r = rs[:, :, 0:2]
        V.seq(nc.vector.tensor_scalar(r, r, 1.0 / 512, EPS, ALU.mult, ALU.add))
        S.wait(V.tok())
        S.seq(nc.scalar.activation(r, r, ACT.Sqrt))
        V.wait(S.tok())
        V.seq(nc.vector.reciprocal(r, r))
        for c in range(NT):
            for g in range(SSD_G):
                yg = y[:, c, g * 512:g * 512 + 512]
                V(nc.vector.tensor_scalar(yg, yg, rs[:, c, g:g + 1], None, ALU.mult))
        T.wait(V.tok())
        self.to_feat(lambda tt, k: y[:, tt, k * P:(k + 1) * P], self.col["ssd_norm_g"], self.XH, self.XL, 8)
        self.join()

    def feat_view(self, b0):
        return self.PS[:, b0:b0 + 4, :].rearrange("p a (f t) -> p (a f) t", t=SEQ)

    def head_sum(self, src, bank):
        for f in range(RP):
            self.T(self.nc.tensor.matmul(self.PS[0:16, bank, 0:SEQ], self.sel[:, f, :], src[:, f, :],
                                         start=f == 0, stop=f == RP - 1))

    def head_bcast(self, src, b0):
        v = self.feat_view(b0)
        for f in range(RP):
            for s in range(2):
                self.T(self.nc.tensor.matmul(v[64 * s:64 * s + 64, f, :],
                                             self.selT[:, f, s:s + 1].to_broadcast([16, 64]), src,
                                             start=f % 2 == 0, stop=True, skip_group_check=True))
        return v

    def rwkv(self):
        nc, T, V, S, G, i = self.nc, self.T, self.V, self.S, self.G, self.i
        PS, LO, col = self.PS, self.LO, self.col
        tt = lambda o, a, b, op: V.seq(nc.vector.tensor_tensor(o, a, b, op))
        R, K, VV = (self.RKV[:, 8 * k:8 * k + 8, :] for k in range(3))
        LW, IC, KK = self.view(12320, RP, SEQ), self.view(14368, RP, SEQ), self.view(16416, RP, SEQ)
        Q = self.view(18464, RP, SEQ)
        t1 = self.view(20512, RP, SEQ)
        w2, a2 = self.view(22560, 1024), self.view(23584, 1024)
        hs = self.view(24608, SEQ)[0:16, :]
        bs = self.view(24864, SEQ)[0:16, :]
        eend = self.view(25120, RP, NRC)
        c8 = self.view(25152, 16)
        la = self.load(2, w2[0:LORA, :], i["rwkv_w2"][0])
        la = self.load(2, a2[0:LORA, :], i["rwkv_a2"][0])
        S.seq(nc.scalar.activation(LO[0:LORA, 0, :], LO[0:LORA, 0, :], ACT.Tanh))
        S.seq(nc.scalar.activation(LO[:, 2:4, :], LO[:, 2:4, :], ACT.Sigmoid))
        T.wait(S.tok(), la)
        for n, (w, dst, b) in enumerate(((w2, LW, "rwkv_w0"), (a2, IC, "rwkv_a0"))):
            v = self.feat_view(4 * n)
            for f in range(RP):
                T(nc.tensor.matmul(v[:, f, :], w[0:LORA, f * P:(f + 1) * P], LO[0:LORA, n, :],
                                   start=f % 2 == 0, stop=True, skip_group_check=True))
            S.wait(T.tok())
            for f in range(RP):
                S(nc.scalar.activation(dst[:, f, :], v[:, f, :], ACT.Sigmoid, bias=col[b][:, f:f + 1]))
        V.wait(S.tok())
        V.seq(nc.vector.tensor_scalar(LW, LW, -0.6065306597126334, None, ALU.mult))
        tt(KK, K, self.bc(col["rwkv_k_k"], SEQ), ALU.mult)
        tt(t1, KK, KK, ALU.mult)
        T.wait(V.tok(), S.tok())
        self.head_sum(t1, 0)
        S.wait(T.tok())
        S.seq(nc.scalar.activation(hs, PS[0:16, 0, 0:SEQ], ACT.Sqrt))
        V.wait(S.tok())
        V.seq(nc.vector.tensor_scalar(hs, hs, 1e-12, None, ALU.max))
        V.seq(nc.vector.reciprocal(hs, hs))
        T.wait(V.tok())
        v = self.head_bcast(hs, 4)
        V.wait(T.tok())
        tt(KK, KK, v, ALU.mult)
        V.seq(nc.vector.tensor_scalar(t1, IC, -1.0, None, ALU.add))
        tt(t1, t1, self.bc(col["rwkv_k_a"], SEQ), ALU.mult)
        V.seq(nc.vector.scalar_tensor_tensor(K, t1, 1.0, K, ALU.add, ALU.mult))
        tt(t1, R, K, ALU.mult)
        tt(t1, t1, self.bc(col["rwkv_r_k"], SEQ), ALU.mult)
        T.wait(V.tok())
        self.head_sum(t1, 0)
        V.wait(T.tok())
        V.seq(nc.vector.tensor_copy(bs, PS[0:16, 0, 0:SEQ]))
        tt(IC, KK, IC, ALU.mult)
        for f in range(RP):
            V(nc.vector.tensor_tensor_scan(t1[:, f, :], self.rst[:, :], LW[:, f, :], 0.0, ALU.mult, ALU.add))
        V.wait(V.tok())
        tt(LW, t1, LW, ALU.subtract)
        S.wait(V.tok())
        S.seq(nc.scalar.activation(LW, LW, ACT.Exp))
        V.wait(S.tok())
        tt(Q, KK, LW, ALU.mult)
        S.wait(V.tok())
        S.seq(nc.scalar.activation(LW, t1, ACT.Exp))
        S.seq(nc.scalar.activation(t1, t1, ACT.Exp, scale=-1.0))
        V.wait(S.tok())
        tt(R, R, LW, ALU.mult)
        V.seq(nc.vector.tensor_copy(eend, LW.rearrange("p f (c e) -> p f c e", e=RC)[:, :, :, RC - 1]))
        tt(K, K, t1, ALU.mult)
        tt(IC, IC, t1, ALU.mult)
        Aa = self.view(12320, RP, SEQ)
        Qq = self.view(14368, RP, SEQ)
        sg = self.view(16416, 2, SEQ)
        bs2, eend2 = self.view(16928, SEQ)[0:16, :], self.view(17184, RP, NRC)
        V.seq(nc.vector.tensor_copy(Aa, IC))
        V.seq(nc.vector.tensor_copy(Qq, Q))
        V.seq(nc.vector.tensor_copy(sg, LO[:, 2:4, :]))
        V.seq(nc.vector.tensor_copy(bs2, bs))
        V.seq(nc.vector.tensor_copy(eend2, eend))
        self.join()
        free = [0, 1024, 2048, 3072, 4096, 11264 - 0] + []
        spots = [0, 1024, 2048, 3072, 4096] + [17216 + 1024 * k for k in range(8)]
        B = [self.view(s, RP, P) for s in spots]
        RAT, RKT = self.view(11264, RP, RC), self.view(11776, RP, RC)
        St = B[12]
        for b in (B[0], B[1], B[2], B[3], St):
            G(nc.gpsimd.memset(b, 0.0))
        for l in (T, V, S, G):
            l.wait(G.tok())

        def pair_mm(b0, pairs, n=P):
            per = 512 // n
            for f in range(RP):
                o = PS[:, b0 + f // per, (f % per) * n:(f % per) * n + n]
                for m, (a, b) in enumerate(pairs):
                    T(nc.tensor.matmul(o, a[:, f, :], b[:, f, :], start=(f % per == 0 and m == 0),
                                       stop=m == len(pairs) - 1, skip_group_check=True))
            return T.tok()

        def turn(b0, a):
            for f in range(RP):
                T(nc.tensor.transpose(PS[:, b0 + f // 4, (f % 4) * P:(f % 4) * P + P], a[:, f, :],
                                      self.ident[:, :]))
            return T.tok()

        def bd(b0):
            return PS[:, b0:b0 + 2, :].rearrange("p a (f t) -> p (a f) t", t=P)

        def cp(b):
            return PS[:, b, :].rearrange("p (f t) -> p f t", t=RC)

        m8 = lambda m: self.rep(m[:, :], RP)
        with self.loop(NRC, "rwkv_chunks") as c:
            tok = ds(c * RC, RC)
            for hp in range(2):
                r, q = slice(64 * hp, 64 * hp + 64), slice(64 * hp, 64 * hp + 64)
                V(nc.vector.tensor_copy(B[0][r, :, q], Aa[r, :, tok]))
                V(nc.vector.tensor_copy(B[2][r, :, q], Qq[r, :, tok]))
                S(nc.scalar.activation(B[1][r, :, q], K[r, :, tok], ACT.Copy))
                G(nc.gpsimd.tensor_copy(B[3][r, :, q], VV[r, :, tok]))
            T.wait(V.tok(), S.tok())
            t_a = pair_mm(0, [(B[0], B[2])])
            t_b = pair_mm(2, [(B[2], B[0])])
            t_c = pair_mm(4, [(B[0], R[:, :, tok])], RC)
            t_d = pair_mm(5, [(B[1], R[:, :, tok])], RC)
            t_e = pair_mm(6, [(B[1], B[2])])
            V.wait(t_a)
            V(nc.vector.tensor_tensor(B[4], bd(0), m8(self.m_d), ALU.mult))
            v_a = V(nc.vector.tensor_tensor(B[6], bd(0), m8(self.m_o), ALU.mult))
            V.wait(t_b)
            v_b = V(nc.vector.tensor_tensor(B[5], bd(2), m8(self.m_dT), ALU.mult))
            V.wait(t_d)
            V(nc.vector.tensor_tensor(RAT, cp(4), self.rep(self.m_ic[:, :], RP), ALU.mult))
            v_d = V(nc.vector.tensor_tensor(RKT, cp(5), self.rep(self.m_ic[:, :], RP), ALU.mult))
            V.wait(t_e)
            v_e = V(nc.vector.tensor_tensor(B[7], bd(6), m8(self.m_st), ALU.mult))
            T.wait(v_a)
            t1_ = turn(0, B[0])
            S.wait(t1_)
            s1 = S(nc.scalar.activation(B[8], bd(0), ACT.Copy))
            T.wait(v_b)
            t2_ = turn(2, B[1])
            S.wait(t2_)
            s2 = S(nc.scalar.activation(B[9], bd(2), ACT.Copy))
            T.wait(v_d, G.tok())
            t3_ = turn(4, B[3])
            S.wait(t3_)
            s3 = S(nc.scalar.activation(B[3], bd(4), ACT.Copy))
            V.wait(v_a)
            v_p = V(nc.vector.tensor_tensor(B[10], B[4], m8(self.ident), ALU.add))
            T.wait(v_e)
            t_u = pair_mm(6, [(B[5], B[4])])
            T.wait(s1)
            t_ut = pair_mm(0, [(B[4], B[5])])
            V.wait(t_u)
            v_u = V(nc.vector.tensor_copy(B[0], bd(6)))
            S.wait(t_ut)
            s_u = S(nc.scalar.activation(B[1], bd(0), ACT.Copy))
            T.wait(s_u, v_p, s2)
            t_p = pair_mm(2, [(B[1], B[10])])
            T.wait(v_u, s3)
            t_u2 = pair_mm(4, [(B[1], B[0])])
            t_u2t = pair_mm(6, [(B[0], B[1])])
            V.wait(t_p)
            v_p = V(nc.vector.tensor_tensor(B[11], bd(2), B[10], ALU.add))
            S.wait(t_u2, t_ut)
            s_u2 = S(nc.scalar.activation(B[5], bd(4), ACT.Copy))
            V.wait(t_u2t)
            v_u2t = V(nc.vector.tensor_copy(B[4], bd(6)))
            T.wait(v_u2t, v_p)
            t_p = pair_mm(2, [(B[4], B[11])])
            T.wait(s_u2)
            t_u3t = pair_mm(0, [(B[5], B[4])])
            V.wait(t_p)
            v_p = V(nc.vector.tensor_tensor(B[10], bd(2), B[11], ALU.add))
            S.wait(t_u3t)
            s_u3 = S(nc.scalar.activation(B[0], bd(0), ACT.Copy))
            T.wait(v_p, s_u3)
            t_p = pair_mm(4, [(B[0], B[10])])
            V.wait(t_p)
            v_p = V(nc.vector.tensor_tensor(B[11], bd(4), B[10], ALU.add))
            T.wait(v_p)
            t_pt = turn(6, B[11])
            S.wait(t_pt)
            s_pt = S(nc.scalar.activation(B[1], bd(6), ACT.Copy))
            T.wait(s_pt)
            t_m = pair_mm(2, [(B[6], B[1])])
            S.wait(t_m)
            s_m = S(nc.scalar.activation(B[0], bd(2), ACT.Copy))
            T.wait(s_m)
            zsrc = B[11]
            for n, (bank, dst) in enumerate(((4, B[10]), (6, B[4]), (0, B[5]))):
                t_z = pair_mm(bank, [(B[0], zsrc)])
                V.wait(t_z)
                v_z = V(nc.vector.tensor_tensor(dst, bd(bank), B[11], ALU.add))
                T.wait(v_z)
                zsrc = dst
            T.wait(S.tok())
            t_r = pair_mm(2, [(B[2], St), (B[7], B[3])])
            S.wait(t_r)
            s_r = S(nc.scalar.activation(B[4], bd(2), ACT.Copy))
            T.wait(s_r)
            t_sa = pair_mm(4, [(B[5], B[4])])
            S.wait(t_sa)
            s_sa = S(nc.scalar.activation(B[1], bd(4), ACT.Copy, scale=-1.0))
            T.wait(s_sa)
            t_y = pair_mm(6, [(St, R[:, :, tok]), (B[1], RAT), (B[3], RKT)], RC)
            t_s = pair_mm(0, [(B[8], B[1]), (B[9], B[3])])
            S.wait(t_y)
            S(nc.scalar.activation(R[:, :, tok], cp(6), ACT.Copy))
            V.wait(t_s)
            V.seq(nc.vector.tensor_tensor(St, St, bd(0), ALU.add))
            V.seq(nc.vector.tensor_tensor(St, St, eend2[:, :, ds(c, 1)].to_broadcast([P, RP, P]), ALU.mult))
            T.wait(S.tok(), V.tok())
            S.wait(V.tok(), T.tok())
            V.wait(S.tok(), T.tok())
            G.wait(T.tok())
        self.join()
        g2 = self.view(17216, 2, RW)
        GG, t1, t2 = self.view(19264, RP, SEQ), self.view(21312, RP, SEQ), self.view(23360, RP, SEQ)
        hs = self.view(17216 - 32 + 8192, SEQ)[0:16, :]
        hs = self.view(25408, SEQ)[0:16, :]
        l2 = self.load(3, g2, i["rwkv_g2"][0].rearrange("(a p) n -> p a n", p=P))
        T.wait(l2)
        v = self.feat_view(0)
        for f in range(RP):
            for k in range(2):
                T(nc.tensor.matmul(v[:, f, :], g2[:, k, f * P:(f + 1) * P], sg[:, k, :],
                                   start=(f % 2 == 0 and k == 0), stop=k == 1, skip_group_check=True))
        S.wait(T.tok())
        S(nc.scalar.activation(GG, v, ACT.Copy))
        self.head_sum(R, 4)
        V.wait(T.tok())
        V.seq(nc.vector.tensor_scalar(hs, PS[0:16, 4, 0:SEQ], 1.0 / 64, None, ALU.mult))
        T.wait(V.tok(), S.tok())
        v = self.head_bcast(hs, 0)
        V.wait(T.tok())
        tt(R, R, v, ALU.subtract)
        tt(t1, R, R, ALU.mult)
        T.wait(V.tok())
        self.head_sum(t1, 4)
        V.wait(T.tok())
        V.seq(nc.vector.tensor_scalar(hs, PS[0:16, 4, 0:SEQ], 1.0 / 64, LN_EPS, ALU.mult, ALU.add))
        S.wait(V.tok())
        S.seq(nc.scalar.activation(hs, hs, ACT.Sqrt))
        V.wait(S.tok())
        V.seq(nc.vector.reciprocal(hs, hs))
        T.wait(V.tok())
        v = self.head_bcast(hs, 0)
        v2 = self.head_bcast(bs2, 4)
        V.wait(T.tok())
        tt(R, R, v, ALU.mult)
        tt(R, R, self.bc(col["rwkv_ln_w"], SEQ), ALU.mult)
        tt(R, R, self.bc(col["rwkv_ln_b"], SEQ), ALU.add)
        tt(t1, v2, VV, ALU.mult)
        tt(R, R, t1, ALU.add)
        tt(R, R, GG, ALU.mult)
        S.wait(V.tok())
        self.split(self.XH[:, 8:16, :], self.XL[:, 8:16, :], R)
        self.join()

    def softmax_rows(self, rows, st):
        nc, V, S = self.nc, self.V, self.S
        for q, (src, pr) in enumerate(rows):
            V(nc.vector.tensor_reduce(st[:, q:q + 1], src, AX.X, ALU.max))
        V.wait(V.tok())
        v = V(nc.vector.tensor_scalar(st[:, 2:4], st[:, 0:2], -1.0, None, ALU.mult))
        yield
        S.wait(v)
        for q, (src, pr) in enumerate(rows):
            s = S(nc.scalar.activation(pr, src, ACT.Exp, bias=st[:, 2 + q:3 + q], accum_out=st[:, 4 + q:5 + q]))
        yield
        V.wait(s)
        V.seq(nc.vector.reciprocal(st[:, 4:6], st[:, 4:6]))
        for q, (src, pr) in enumerate(rows):
            v = V(nc.vector.tensor_scalar(pr, pr, st[:, 4 + q:5 + q], None, ALU.mult))
        return v

    def heads(self, n, name, slots, head):
        with self.loop(n // slots, name) as i:
            self.together(*((head(slots * i + s, s), 1) for s in range(slots)))
            toks = [l.tok() for l in self.lanes]
            for l in self.lanes:
                l.wait(*toks)
        self.join()

    def cross(self):
        nc, T, V, S, G, i = self.nc, self.T, self.V, self.S, self.G, self.i
        PS, x = self.PS, self.x
        xn, stat = self.view(0, NT, D), self.view(4096, 16)
        Qf, Kf, Vt = self.view(4112, KD, SEQ), self.view(8208, KD, SEQ), self.view(12304, NT, D)
        slots = [[self.view(o + k, *sh) for k, sh in
                  ((0, (4, SEQ)), (1024, (NT, XD)), (2048, (NT, SEQ)), (2560, (NT, SEQ)), (3072, (8,)))]
                 for o in (0, 16400)]
        self.norm_to_feat(x, xn, stat, self.col["norm_x_g"], self.XH, self.XL)
        t = self.load(4, Vt, i["mem"][0].rearrange("(t p) d -> p t d", p=P))
        self.join()
        self.proj("xattn_q", i["xattn_wq"][0], 0, 4, "feat", lambda j, L: self.ev_feat(Qf, j, L))
        self.join()
        S.wait(t)
        V.wait(t)
        self.norm_to_feat(Vt, xn, stat, self.col["norm_mem_g"], self.XH, self.XL)
        self.join()
        self.proj("xattn_k", i["xattn_wk"][0], 0, 4, "feat", lambda j, L: self.ev_feat(Kf, j, L))
        self.proj("xattn_v", i["xattn_wv"][0], 0, 4, "tok", lambda j, L: self.ev_tok(Vt, j, L))
        self.join()

        def head(h, slot):
            Qs, Vs, pr, pT, st = slots[slot]
            b = 4 * slot
            s = S(nc.scalar.activation(Qs, Qf[:, ds(4 * h, 4), :], ACT.Copy, scale=float(XD) ** -0.5))
            g = G(nc.gpsimd.tensor_copy(Vs, Vt[:, :, ds(XD * h, XD)]))
            yield
            T.wait(s)
            sc = PS[:, b, :].rearrange("p (q m) -> p q m", q=NT)
            for q in range(NT):
                for k in range(4):
                    t = T(nc.tensor.matmul(sc[:, q, :], Qs[:, k, q * P:(q + 1) * P], Kf[:, ds(4 * h + k, 1), :],
                                           start=(q == 0 and k == 0), stop=k == 3, skip_group_check=True))
            V.wait(t)
            v = yield from self.softmax_rows([(sc[:, q, :], pr[:, q, :]) for q in range(NT)], st)
            yield
            T.wait(v)
            for m in range(NT):
                for q in range(NT):
                    t = T(nc.tensor.transpose(PS[:, b + 1, m * SEQ + q * P:m * SEQ + q * P + P],
                                              pr[:, q, m * P:(m + 1) * P], self.ident[:, :]))
            S.wait(t)
            s = S(nc.scalar.activation(pT, PS[:, b + 1, :].rearrange("p (m q) -> p m q", m=NT), ACT.Copy))
            yield
            T.wait(s, g)
            o = PS[:, b + 2:b + 4, :].rearrange("p a (f t) -> p (a f) t", t=SEQ)
            for f in range(4):
                for m in range(NT):
                    t = T(nc.tensor.matmul(o[:, f, :], Vs[:, m, f * P:(f + 1) * P], pT[:, m, :],
                                           start=(f % 2 == 0 and m == 0), stop=m == 1, skip_group_check=True))
            S.wait(t)
            self.split(self.XH[:, ds(4 * h, 4), :], self.XL[:, ds(4 * h, 4), :], o)
        self.heads(XH_, "xattn_heads", 2, head)
        self.proj("xattn_o", i["xattn_wo"][0], 0, 4, "tok", lambda j, L: self.ev_add(x, j, L))
        self.join()

    def ffn1(self, AH, AL, xn, tmp, sq):
        nc, V, S, i, x = self.nc, self.V, self.S, self.i, self.x
        stat = self.stat
        self.norm_to_feat(x, xn, stat, self.col["norm_ffn_g"], self.XH, self.XL)
        self.join()
        w1, w2 = i["ffn_w1"][0], i["ffn_w2"][0]

        def ev(j, L):
            def evac(g, ps, ready, out):
                S.wait(ready, V.tok())
                self.done_evac(nc.scalar.activation(tmp, ps, ACT.Relu))
                yield
                V.wait(out)
                V.seq(nc.vector.tensor_tensor(sq, tmp, tmp, ALU.mult))
                yield
                d = ds(4 * (g * L + j), 4)
                S.wait(V.tok())
                S(nc.scalar.activation(AH[:, d, :], sq, ACT.Copy))
                yield
                V.wait(S.tok())
                V.seq(nc.vector.tensor_tensor(AL[:, d, :], sq, AH[:, d, :].bitcast(F32), ALU.subtract))
            return evac
        for part in range(4):
            self.proj(f"ffn1_up{part}", w1, 2048 * part, 4, "feat", ev)
            self.proj(f"ffn1_down{part}", w2, 0, 4, "tok", lambda j, L: self.ev_add(x, j, L),
                      kt=16, k0=2048 * part, xh=AH, xl=AL, late=12)
        self.join()

    def final_norm(self, x, dst, gb, junk):
        nc, V, S = self.nc, self.V, self.S
        self.rstd(lambda tt: x[:, tt, :], self.stat, junk, D)
        for tt in range(NT):
            V.seq(nc.vector.scalar_tensor_tensor(dst[:, tt, :], x[:, tt, :], self.stat[:, tt:tt + 1], gb,
                                                 ALU.mult, ALU.mult))

    def hgrn(self):
        nc, T, V, S, G, i = self.nc, self.T, self.V, self.S, self.G, self.i
        PS, x = self.PS, self.x
        w = i["w_in_2"][0]
        tt = lambda o, a, b, op: V.seq(nc.vector.tensor_tensor(o, a, b, op))
        xn = self.view(0, NT, D)
        self.norm_to_feat(x, xn, self.stat, self.col["norm1_gain_2"], self.XH, self.XL)
        self.join()
        Qa, Fa = self.view(0, GH, SEQ), self.view(2048, GH, SEQ)
        Ia, Ga = self.view(4096, NT, 1024), self.view(6144, NT, 1024)
        self.proj("w_in2_q", w, 0, 2, "feat", lambda j, L: self.ev_feat(Qa, j, L))
        self.proj("w_in2_f", w, 1024, 2, "feat", lambda j, L: self.ev_feat(Fa, j, L, ACT.Sigmoid))
        self.proj("w_in2_i", w, 2048, 2, "tok", lambda j, L: self.ev_tok(Ia, j, L))
        self.proj("w_in2_g", w, 3072, 2, "tok", lambda j, L: self.ev_tok(Ga, j, L, ACT.Silu))
        Qb, Kb, Vb = self.view(8192, GH, SEQ), self.view(10240, GH, SEQ), self.view(12288, NT, 1024)
        Fb = self.Fb = self.view(14336, NT, 8)
        self.Qb, self.Kb, self.Vb = Qb, Kb, Vb
        self.proj("w_in2_qb", w, 4096, 2, "feat", lambda j, L: self.ev_feat(Qb, j, L))
        self.proj("w_in2_kb", w, 5120, 2, "feat", lambda j, L: self.ev_feat(Kb, j, L))

        def ev_fb(g, ps, ready, out):
            S.wait(ready)
            self.done_evac(nc.scalar.activation(Fb, ps[:, :, 0:8], ACT.Copy))
            yield
        sp = [self.spec(w, "tok", (lambda g, j=j: 6144 + 512 * j), self.ev_tok(Vb, j, 2)) for j in range(2)]
        sp.append(self.spec(w, "tok", lambda g: 7168, ev_fb, widths=[8]))
        self.run_now(self.stream("w_in2_rest", 1, sp))
        self.join()
        lb = self.view(14352, 24)
        p = self.col["hgrn_lb_param_2"]
        L0, L1, LM = lb[:, 0:8], lb[:, 8:16], lb[:, 16:24]
        tt(LM, p[:, 0:8], p[:, 8:16], ALU.max)
        tt(L0, p[:, 0:8], LM, ALU.subtract)
        tt(L1, p[:, 8:16], LM, ALU.subtract)
        S.wait(V.tok())
        S.seq(nc.scalar.activation(lb[:, 0:16], lb[:, 0:16], ACT.Exp))
        V.wait(S.tok())
        tt(LM, L0, L1, ALU.add)
        V.seq(nc.vector.reciprocal(LM, LM))
        tt(L0, L0, LM, ALU.mult)
        V.seq(nc.vector.tensor_scalar(L1, L0, -1.0, 1.0, ALU.mult, ALU.add))
        Kd, Ke, Bb = self.view(14376, GH, SEQ), self.view(16424, GH, SEQ), self.view(18472, GH, SEQ)
        dce = self.view(20520, GH, NRC)
        tt(Kd, Fa, self.bc(L1, SEQ), ALU.mult)
        tt(Kd, Kd, self.bc(L0, SEQ), ALU.add)
        S.wait(V.tok())
        S.seq(nc.scalar.activation(Bb, Kd, ACT.Ln))
        V.wait(S.tok())
        V.seq(nc.vector.tensor_scalar(Kd, Kd, -1.0, 1.0, ALU.mult, ALU.add))
        for h in range(GH):
            V(nc.vector.tensor_tensor_scan(Fa[:, h, :], self.rst[:, :], Bb[:, h, :], 0.0, ALU.mult, ALU.add))
        V.wait(V.tok())
        ch = lambda a: a.rearrange("p f (c e) -> p (f c) e", e=HCH)
        b_end = ch(Fa)[:, :, HCH - 1:HCH].to_broadcast([P, GH * NRC, HCH])
        tt(ch(Ke), b_end, ch(Fa), ALU.subtract)
        S.wait(V.tok())
        S(nc.scalar.activation(Ke, Ke, ACT.Exp))
        S(nc.scalar.activation(Bb, Fa, ACT.Exp))
        S.seq(nc.scalar.activation(Fa, Fa, ACT.Exp, scale=-1.0))
        V.wait(S.tok())
        tt(Ke, Ke, Kd, ALU.mult)
        tt(Kd, Kd, Fa, ALU.mult)
        V.seq(nc.vector.scalar_tensor_tensor(Qa, Qa, float(P) ** -0.5, Bb, ALU.mult, ALU.mult))
        V.seq(nc.vector.tensor_copy(dce, Bb.rearrange("p f (c e) -> p f c e", e=HCH)[:, :, :, HCH - 1]))
        slots = []
        for k in range(2):
            a, b, c = 2048 + 1024 * k, 18472 + 1024 * k, 20552 + 808 * k
            slots.append(dict(QZ=self.view(a, 4, P), KTe=self.view(a + 512, NT, P), KTo=self.view(a + 768, NT, P),
                              Kds=self.view(b, SEQ), Kes=self.view(b + 256, SEQ), AT=self.view(b + 512, NT, P),
                              O=self.view(b + 768, NT, P), Sn=self.view(c, 3, P), stt_=self.view(c + 384, 4),
                              dcs=self.view(c + 388, NRC), junk=self.view(c + 392, P)))
        self.join()
        for sl in slots:
            for b in ("QZ", "KTe", "KTo"):
                G(nc.gpsimd.memset(sl[b], 0.0))
        for l in (T, V, S, G):
            l.wait(G.tok())

        def head(h, slot):
            sl = slots[slot]
            QZ, KTe, KTo, Kds, Kes, AT, O, Sn, stt_, dcs, junk = (sl[n] for n in (
                "QZ", "KTe", "KTo", "Kds", "Kes", "AT", "O", "Sn", "stt_", "dcs", "junk"))
            ba, bb = 2 * slot, 2 * slot + 1
            v3 = lambda b: PS[:, b, 0:SEQ].rearrange("p (q m) -> p q m", q=NT)
            hd, cols = ds(h, 1), ds(P * h, P)
            v_k = V(nc.vector.tensor_copy(Kds, Kd[:, hd, :]))
            g_e = G(nc.gpsimd.tensor_copy(Kes, Ke[:, hd, :]))
            g_d = G(nc.gpsimd.tensor_copy(dcs, dce[:, hd, :]))
            qv = Qa[:, hd, :].rearrange("p o (t c e) -> p (o t) c e", t=NT, c=2)
            for c in range(2):
                s_q = S(nc.scalar.activation(QZ.rearrange("p (t c) e -> p t c e", c=2)[:, :, c, c * 64:c * 64 + 64],
                                             qv[:, :, c, :], ACT.Copy))
            yield
            T.wait(v_k)
            for q in range(NT):
                t_a = T(nc.tensor.matmul(PS[:, ba, q * P:(q + 1) * P], Kds[:, q * P:(q + 1) * P],
                                         Qa[:, hd, q * P:(q + 1) * P], start=q == 0, stop=True,
                                         skip_group_check=True))
            T.wait(g_e)
            for q in range(NT):
                t = T(nc.tensor.transpose(PS[:, bb, q * P:(q + 1) * P], Kes[:, q * P:(q + 1) * P], self.ident[:, :]))
            V.wait(t_a)
            v_at = V(nc.vector.tensor_tensor(AT, v3(ba), self.rep(self.m_in[:, :], NT), ALU.mult))
            S.wait(t)
            S(nc.scalar.activation(KTe[0:64, :, :], v3(bb)[0:64], ACT.Copy))
            s = S(nc.scalar.activation(KTo[64:128, :, :], v3(bb)[64:128], ACT.Copy))
            yield
            T.wait(s)
            for n in range(3):
                t = T(nc.tensor.matmul(PS[:, bb, n * P:(n + 1) * P], (KTe, KTo)[n % 2][:, n // 2, :],
                                       Ia[:, n // 2, cols], start=n == 0, stop=True, skip_group_check=True))
            V.wait(t, g_d)
            V.seq(nc.vector.tensor_copy(Sn[:, 0, :], PS[:, bb, 0:P]))
            for n in (1, 2):
                v = V.seq(nc.vector.scalar_tensor_tensor(Sn[:, n, :], Sn[:, n - 1, :], dcs[:, n:n + 1],
                                                         PS[:, bb, n * P:(n + 1) * P], ALU.mult, ALU.add))
            yield
            T.wait(v, v_at, s_q)
            for q in range(NT):
                ops = [(AT[:, q, :], Ia[:, q, cols])] + [(QZ[:, n, :], Sn[:, n - 1, :])
                                                        for n in (2 * q, 2 * q + 1) if n > 0]
                for m, (a, b) in enumerate(ops):
                    t = T(nc.tensor.matmul(PS[:, ba, q * P:(q + 1) * P], a, b, start=(q == 0 and m == 0),
                                           stop=m == len(ops) - 1, skip_group_check=True))
            yield
            S.wait(t)
            for q in range(NT):
                s = S(nc.scalar.activation(junk, v3(ba)[:, q, :], ACT.Square, accum_out=stt_[:, q:q + 1]))
                S.wait(s)
            yield
            V.wait(s)
            v = V(nc.vector.tensor_scalar(stt_[:, 0:2], stt_[:, 0:2], 1.0 / P, EPS, ALU.mult, ALU.add))
            S.wait(v)
            s = S(nc.scalar.activation(stt_[:, 0:2], stt_[:, 0:2], ACT.Sqrt))
            yield
            V.wait(s)
            V.seq(nc.vector.reciprocal(stt_[:, 2:4], stt_[:, 0:2]))
            for q in range(NT):
                v = V(nc.vector.scalar_tensor_tensor(O[:, q, :], v3(ba)[:, q, :], stt_[:, 2 + q:3 + q],
                                                     Ga[:, q, cols], ALU.mult, ALU.mult))
            yield
            T.wait(v)
            for q in range(NT):
                t = T(nc.tensor.transpose(PS[:, bb, q * P:(q + 1) * P], O[:, q, :], self.ident[:, :]))
            S.wait(t)
            self.split(self.XH[:, hd, :], self.XL[:, hd, :], PS[:, bb, 0:SEQ], self.col["hgrn_norm_gain_2"][:, 0:1])
        self.heads(GH, "hgrn_heads", 2, head)

    def fox(self):
        nc, T, V, S, G = self.nc, self.T, self.V, self.S, self.G
        PS, Fb = self.PS, self.Fb
        nlf, t = self.view(0, NT, 8), [self.view(16 + 16 * k, NT, 8) for k in range(3)]
        CU = self.view(64, SEQ)
        slots = [[self.view(320 + 1300 * k + o, *sh) for o, sh in
                  ((0, (3 * P,)), (384, (3 * P,)), (768, (8,)), (776, (SEQ,)), (1032, (NT, P)), (1288, (NT,)))]
                 for k in range(4)]
        V.seq(nc.vector.tensor_tensor(Fb, Fb, self.rep(self.fxb[:, :], NT), ALU.add))
        self.log1p_exp_negabs(nlf, Fb, t)
        V.seq(nc.vector.tensor_scalar(t[0], Fb, 0.0, -1.0, ALU.min, ALU.mult))
        V.seq(nc.vector.tensor_tensor(nlf, nlf, t[0], ALU.add))
        G(nc.gpsimd.tensor_copy(CU[:, 0:P], self.triu[:, :]))
        G(nc.gpsimd.tensor_copy(CU[:, P:SEQ], self.ones[:, :]))
        self.join()

        def head(h, slot):
            pr, pT, st, Qs, Vs, nl = slots[slot]
            ba, bb = 2 * slot, 2 * slot + 1
            hd = ds(h, 1)
            s_q = S(nc.scalar.activation(Qs, self.Qb[:, hd, :], ACT.Copy, scale=float(P) ** -0.5))
            g_n = G(nc.gpsimd.tensor_copy(nl, nlf[:, :, hd]))
            g_v = G(nc.gpsimd.tensor_copy(Vs, self.Vb[:, :, ds(P * h, P)]))
            yield
            T.wait(s_q, g_n)
            sc, first = PS[:, ba, 0:3 * P], [True]

            def add(c0, n, lhs, rhs, stop=False):
                t = T(nc.tensor.matmul(sc[:, c0:c0 + n], lhs, rhs, start=first[0], stop=stop, skip_group_check=True))
                first[0] = False
                return t
            add(0, P, self.ident[:, :], self.negu[:, :])
            add(2 * P, P, self.ident[:, :], self.negu[:, :])
            n0, n1 = (nl[:, k:k + 1].to_broadcast([P, P]) for k in range(NT))
            add(0, P, n0, self.triu[:, :])
            add(P, 2 * P, n0, CU)
            add(2 * P, P, n1, self.triu[:, :])
            add(0, P, Qs[:, 0:P], self.Kb[:, hd, 0:P], True)
            t = add(P, 2 * P, Qs[:, P:SEQ], self.Kb[:, hd, :], True)
            V.wait(t)
            v = yield from self.softmax_rows([(sc[:, 0:P], pr[:, 0:P]), (sc[:, P:3 * P], pr[:, P:3 * P])], st)
            yield
            T.wait(v)
            for k in range(3):
                t = T(nc.tensor.transpose(PS[:, bb, k * P:(k + 1) * P], pr[:, k * P:(k + 1) * P], self.ident[:, :]))
            S.wait(t)
            s = S(nc.scalar.activation(pT, PS[:, bb, 0:3 * P], ACT.Copy))
            yield
            T.wait(s, g_v)
            T(nc.tensor.matmul(PS[:, ba, 0:SEQ], Vs[:, 0, :], pT[:, 0:SEQ], start=True, stop=False,
                               skip_group_check=True))
            t = T(nc.tensor.matmul(PS[:, ba, P:SEQ], Vs[:, 1, :], pT[:, SEQ:3 * P], start=False, stop=True,
                                   skip_group_check=True))
            S.wait(t)
            self.split(self.XH[:, ds(h + 8, 1), :], self.XL[:, ds(h + 8, 1), :], PS[:, ba, 0:SEQ])
        self.heads(GH, "fox_heads", 4, head)

    def ffn2(self, AH, AL, xn, buf, acc, tmp):
        nc, V, S, G, i, x = self.nc, self.V, self.S, self.G, self.i, self.x
        self.norm_to_feat(x, xn, self.stat, self.col["norm2_gain_2"], self.XH, self.XL)
        G(nc.gpsimd.memset(buf[:, :, 0:2], 0.0))
        self.join()
        wg, wu, wd = i["w_ffn_gate_2"][0], i["w_ffn_up_2"][0], i["w_ffn_down_2"][0]
        cw, cb = self.fcw, self.col["ffn_conv_b_2"]
        done = 0
        for part, nb in enumerate((4, 4, 3)):

            def ev_gate(g, ps, ready, out):
                b = g + done
                S.wait(ready, V.tok())
                self.done_evac(nc.scalar.activation(buf[:, :, 2:2 + SEQ], ps, ACT.Copy))
                yield
                V.wait(out)
                for tap in range(3):
                    wt = self.bc(cw[:, tap, ds(4 * b, 4)], SEQ)
                    V.seq(nc.vector.tensor_tensor(tmp if tap else acc, buf[:, :, tap:tap + SEQ], wt, ALU.mult))
                    if tap:
                        V.seq(nc.vector.tensor_tensor(acc, acc, tmp, ALU.add))
                    yield
                V.seq(nc.vector.tensor_tensor(acc, acc, self.bc(cb[:, ds(4 * b, 4)], SEQ), ALU.add))
                yield
                S.wait(V.tok())
                S(nc.scalar.activation(acc, acc, ACT.Silu))

            def ev_up(g, ps, ready, out):
                V.wait(ready, S.tok())
                V.seq(nc.vector.tensor_tensor(acc, acc, ps, ALU.mult))
                self.nc.vector.sem_inc(self.s_evac, 1)
                yield
                S.wait(V.tok())
                d = ds(4 * g, 4)
                S(nc.scalar.activation(AH[:, d, :], acc, ACT.Copy))
                yield
                V.wait(S.tok())
                V.seq(nc.vector.tensor_tensor(AL[:, d, :], acc, AH[:, d, :].bitcast(F32), ALU.subtract))
            c = lambda g: 512 * (g + done)
            self.run_now(self.stream(f"ffn2_up{part}", nb, [self.spec(wg, "feat", c, ev_gate),
                                                            self.spec(wu, "feat", c, ev_up)]))
            self.proj(f"ffn2_down{part}", wd, 0, 4, "tok", lambda j, L: self.ev_add(x, j, L),
                      kt=4 * nb, k0=512 * done, xh=AH, xl=AL, late=4 * nb - 4)
            done += nb
        self.join()

    def run(self, stop_at=None):
        nc, ctx, i, sb = self.nc, self.ctx, self.i, self.sb
        T, V, S = self.T, self.V, self.S
        self.constants()
        self.param_cols = sb("param_cols", [P, 113 + 124 + 128 + 72])
        self.stat = sb("stat", [P, 4])
        self.mul = sb("mu_lora", [P, 4])
        self.dtb, self.alog, self.dsk, self.fxb = (sb(n, [P, m]) for n, m in
                                                   (("dt_bias", 16), ("a_log", 16), ("d_skip", 16), ("fox_bias", 8)))
        small = ExitStack()
        small.enter_context(nc.allow_non_contiguous_dma(reason="a few hundred values"))
        mu = i["rwkv_mu"][0].rearrange("(n a) -> n a", a=1)
        self.load(5, self.mul[0:LORA, 0:1], mu[3072:3072 + LORA, :])
        self.load(5, self.mul[0:LORA, 1:2], mu[3072 + LORA:3072 + 2 * LORA, :])
        for k in range(2):
            self.load(5, self.mul[:, 2 + k:3 + k], mu[3264 + k * P:3264 + (k + 1) * P, :])
        for t, n, m in ((self.dtb, "ssd_dt_bias", 16), (self.alog, "ssd_a_log", 16), (self.dsk, "ssd_d", 16),
                        (self.fxb, "fox_gate_bias_2", 8)):
            lt = self.load(5, t[:, :], i[n].to_broadcast([P, m]))
        small.close()
        self.arena_cm = self.open_arena("arena_a", 25920)
        self.params()
        for l in self.lanes:
            l.wait(lt)
        self.join()
        self.block1_in()
        if stop_at == "in":
            return
        self.ssd()
        self.rwkv()
        if stop_at == "mix":
            return
        self.arena_cm.close()
        self.x = sb("x", [P, NT, D])
        t = self.load(6, self.x[:, :, :], self.XTOK)
        cm = self.open_arena("arena_b", 21000)
        V.wait(t)
        self.proj("w_out", i["w_out"][0], 0, 4, "tok", lambda j, L: self.ev_add(self.x, j, L))
        self.join()
        if stop_at == "w_out":
            return
        self.cross()
        if stop_at == "cross":
            return
        cm.close()

        def ffn_scope():
            c = self.scope = ExitStack()
            t = [c.enter_context(nc.sbuf_tensor(f"{n}{self.ffn_no}", s, d)) for n, s, d in (
                ("act_hi", [P, 16, SEQ], F32R), ("act_lo", [P, 16, SEQ], F32R), ("xn", [P, NT, D], F32),
                ("buf", [P, 4, SEQ + 2], F32), ("acc", [P, 4, SEQ], F32), ("tmp", [P, 4, SEQ], F32))]
            self.ffn_no += 1
            return c, t
        self.ffn_no = 1
        c, (AH, AL, xn, buf, acc, tmp) = ffn_scope()
        self.ffn1(AH, AL, xn[:, :, :], tmp[:, :, :], acc[:, :, :])
        if stop_at == "ffn1":
            return
        c.close()
        cm = self.open_arena("arena_c", 22200)
        gb = self.view(4096, D)
        t = self.load(7, gb, i["final_norm_g"].rearrange("(a n) -> a n", a=1).to_broadcast([P, D]))
        V.wait(t)
        self.final_norm(self.x[:, :, :], self.x[:, :, :], gb, self.view(0, NT, D)[:, 0, :])
        self.join()
        self.hgrn()
        self.fox()
        if stop_at == "mix2":
            return
        cm.close()
        c, (AH, AL, xn, buf, acc, tmp) = ffn_scope()
        self.proj("w_out2", i["w_out_2"][0], 0, 4, "tok", lambda j, L: self.ev_add(self.x, j, L))
        self.join()
        self.ffn2(AH, AL, xn[:, :, :], buf[:, :, :], acc[:, :, :], tmp[:, :, :])
        gb = xn[:, 1, :]
        t = self.load(8, gb, i["final_norm_gain_2"].rearrange("(a n) -> a n", a=1).to_broadcast([P, D]))
        V.wait(t)
        self.final_norm(self.x[:, :, :], self.x[:, :, :], gb, xn[:, 0, :])
        nc.sync.wait_ge(*V.tok())
        s_out = self.newsem("stored")
        nc.sync.dma_start(self.out[0].rearrange("(t p) d -> p t d", p=P), self.x[:, :, :]).then_inc(s_out, 16)
        nc.sync.wait_ge(s_out, 16)
        c.close()

    def open_arena(self, name, words):
        c = self.scope = ExitStack()
        self.arena = c.enter_context(self.nc.sbuf_tensor(name, [P, words], F32))
        self.arena_words = words
        return c


NAMES = ["x", "mem", "norm_mix_g", "w_in", "ssd_conv_w", "ssd_conv_b", "ssd_dt_bias", "ssd_a_log", "ssd_d",
         "ssd_norm_g", "rwkv_mu", "rwkv_w0", "rwkv_w2", "rwkv_a0", "rwkv_a2", "rwkv_g2", "rwkv_k_k", "rwkv_k_a",
         "rwkv_r_k", "rwkv_ln_w", "rwkv_ln_b", "w_out", "norm_x_g", "norm_mem_g", "xattn_wq", "xattn_wk",
         "xattn_wv", "xattn_wo", "norm_ffn_g", "ffn_w1", "ffn_w2", "final_norm_g", "norm1_gain_2", "w_in_2",
         "hgrn_lb_param_2", "hgrn_norm_gain_2", "fox_gate_bias_2", "w_out_2", "norm2_gain_2", "w_ffn_gate_2",
         "w_ffn_up_2", "ffn_conv_w_2", "ffn_conv_b_2", "w_ffn_down_2", "final_norm_gain_2"]


def program(nc, ins, out, stop_at=None):
    with ExitStack() as ctx:
        m = Model(nc, ctx, ins, out)
        m.run(stop_at)
        m.scope.close()
        return m


def kernel(**inputs):
    import numpy as np
    import concourse.bacc as bacc
    from concourse.bass_utils import run_bass_kernel_spmd

    nc = bacc.Bacc("TRN2", target_bir_lowering=False, num_devices=1)
    arrays, ins = {}, {}
    for name in NAMES:
        a = np.ascontiguousarray(inputs[name])
        arrays["in_" + name] = a
        ins[name] = nc.dram_tensor("in_" + name, a.shape, F32, kind="ExternalInput").ap()
    out = nc.dram_tensor("out", (1, SEQ, D), F32, kind="ExternalOutput").ap()
    program(nc, ins, out)
    r = run_bass_kernel_spmd(nc, [arrays], core_ids=[0])
    return r.results[0]["out"]
```

```python
from contextlib import ExitStack

import concourse.bass as bass
from concourse import mybir

F32 = mybir.dt.float32
F32R = mybir.dt.float32r
ALU = mybir.AluOpType
ACT = mybir.ActivationFunctionType
AX = mybir.AxisListType
ds = bass.ds

P = 128
SEQ = 256
NT = SEQ // P
D = 2048
KD = D // P
EPS = 1e-6
NEG = -1e30

SSD_W, SSD_H, SSD_G, SSD_N, SSD_CONV = 1024, 16, 2, 128, 4
XBC = SSD_W + 2 * SSD_G * SSD_N
RW = 1024
RP = RW // P
RC = 64
NRC = SEQ // RC
LORA = 96
LN_EPS = 64e-5
XH_, XD = 4, 512
FF1, FF2 = 8192, 5632
GH = 8
HCH = 64

CREDIT = 64

STEPS = {
    "w_in_rkv": (0, 6, 0, 0),
    "rwkv_chunks": (224, 42, 28, 12),
    "xattn_heads": (40, 14, 10, 2),
    "ffn1_up0": (0, 4, 2, 0),
    "ffn1_up1": (0, 4, 2, 0),
    "ffn1_up2": (0, 4, 2, 0),
    "ffn1_up3": (0, 4, 2, 0),
    "hgrn_heads": (56, 36, 32, 8),
    "fox_heads": (48, 28, 20, 8),
    "ffn2_up0": (0, 8, 2, 0),
    "ffn2_up1": (0, 8, 2, 0),
    "ffn2_up2": (0, 8, 2, 0),
    "xattn_o": (0, 0, 4, 0),
    "ffn1_down3": (0, 0, 4, 0),
    "w_out2": (0, 0, 4, 0),
    "ffn2_down2": (0, 0, 4, 0),
}


class Lane:

    def __init__(self, eng, sem, key):
        self.eng, self.sem, self.key = eng, sem, key
        self.const, self.terms = CREDIT, []

    def value(self):
        v = self.const
        for i, per in self.terms:
            v = i * per + v
        return v

    def tok(self):
        return (self.sem, self.value())

    def __call__(self, ins):
        ins.then_inc(self.sem, 1)
        self.const += 1
        return self.tok()

    def wait(self, *toks):
        for sem, v in toks:
            self.eng.wait_ge(sem, v)

    def wait_apart(self, *toks):
        self.wait(*toks)
        self.eng.sem_inc(self.spare, 1)

    def seq(self, ins):
        t = self(ins)
        self.wait(t)
        return t


class Prog:
    def __init__(self, nc, ctx, ins, out):
        self.nc, self.ctx, self.i, self.out = nc, ctx, ins, out
        sem = lambda n: ctx.enter_context(nc.semaphore(n))
        self.newsem = sem
        self.T = Lane(nc.tensor, sem("tensor_done"), "T")
        self.V = Lane(nc.vector, sem("vector_done"), "V")
        self.S = Lane(nc.scalar, sem("scalar_done"), "S")
        self.G = Lane(nc.gpsimd, sem("gpsimd_done"), "G")
        self.S.spare, self.G.spare = sem("scalar_spare"), sem("gpsimd_spare")
        self.lanes = [self.T, self.V, self.S, self.G]
        self.ring_full = [sem(f"ring_full{q}") for q in range(4)]
        self.s_hi, self.s_lo = sem("weights_hi"), sem("weights_lo")
        self.s_mm, self.s_evac = sem("half_multiplied"), sem("block_evacuated")
        self.tile_const, self.tile_terms = 0, []
        self.blk_const, self.blk_terms = 0, []
        self.pend, self.par0 = None, 0
        self.s_par = [sem(f"params{k}") for k in range(12)]
        self.par_n = [0] * 12
        for s, e in ((self.T.sem, nc.tensor), (self.s_mm, nc.tensor), (self.V.sem, nc.vector),
                     (self.s_lo, nc.vector), (self.S.sem, nc.scalar), (self.s_hi, nc.scalar),
                     (self.s_evac, nc.vector), (self.G.sem, nc.gpsimd)):
            e.sem_inc(s, CREDIT)
        sb = lambda n, s, d=F32: ctx.enter_context(nc.sbuf_tensor(n, s, d))
        self.sb = sb
        self.raw = sb("raw", [P, 4, 4, 512])
        self.whi = sb("whi", [P, 4, 2, 512], F32R)
        self.wlo = sb("wlo", [P, 4, 2, 512], F32R)
        self.XH = sb("XH", [P, KD, SEQ], F32R)
        self.XL = sb("XL", [P, KD, SEQ], F32R)
        self.PS = ctx.enter_context(nc.psum_tensor("PS", [P, 8, 512], F32))

    def loop(self, n, name, tiles=0, blks=0):
        return LoopScope(self, n, name, tiles, blks)

    def view(self, off, *shape):
        n = 1
        for s in shape:
            n *= s
        if self.low and off < NT * D:
            assert off + n <= NT * D
            v = self.x[:, :, :].rearrange("p a b -> p (a b)")[:, off:off + n]
        else:
            off -= NT * D * self.low
            assert off + n <= self.arena_words, (off + n, self.arena_words)
            v = self.arena[:, off:off + n]
        if len(shape) == 2:
            v = v.rearrange("p (a b) -> p a b", a=shape[0])
        if len(shape) == 3:
            v = v.rearrange("p (a b c) -> p a b c", a=shape[0], b=shape[1])
        return v

    def join(self, *extra):
        self.flush()
        toks = [l.tok() for l in self.lanes] + [(self.s_evac, CREDIT + self.blk_const),
                                                (self.s_mm, CREDIT + 2 * self.tile_const)] + list(extra)
        for l in self.lanes:
            for t in toks:
                if t[0] is not l.sem:
                    l.wait(t)
            l.wait(l.tok())

    def load(self, k, dst, src, eng=None):
        (eng or self.nc.scalar).dma_start(dst, src).then_inc(self.s_par[k], 16)
        self.par_n[k] += 16
        return (self.s_par[k], self.par_n[k])

    def tile(self):
        v = self.tile_const
        for i, per in self.tile_terms:
            v = i * per + v
        return v

    def blk(self):
        v = self.blk_const
        for i, per in self.blk_terms:
            v = i * per + v
        return v

    def blocks(self, todo, prev=None, ahead=0, banks=2, late=None, feed=None):
        nc, T, V, S = self.nc, self.T, self.V, self.S
        t0, tc, b0, par0 = self.tile(), self.tile_const, self.blk(), self.par0
        halves, nt = [], 0
        for j, (spec, g) in enumerate(todo):
            nq = (spec["kt"] + 3) // 4
            for q in range(nq):
                for u in range(2):
                    halves.append((j, spec, g, nt, q, u, q == nq - 1 and u == 1))
                nt += 1
        ends = {}

        def split(n):
            j, spec, g, tn, q, u, _ = halves[n]
            t, slot, ncol = t0 + tn, (tc + tn) % 4, sum(spec["widths"])
            if u == 0:
                k = spec["k0"] + 512 * q
                nc.sync.wait_ge(self.s_lo, 2 * t - 6 + CREDIT)
                nc.sync.dma_start(self.raw[:, slot, :, 0:ncol],
                                  spec["w"][k:k + 512, ds(spec["col"](g), ncol)]
                                  .rearrange("(a p) n -> p a n", p=P)).then_inc(self.ring_full[slot], 16)
            h, hs = 2 * t + u, (2 * (tc + tn) + u) % 4
            raw = self.raw[:, slot, 2 * u:2 * u + 2, 0:ncol]
            hi, lo = self.whi[:, hs, :, 0:ncol], self.wlo[:, hs, :, 0:ncol]
            nc.scalar.wait_ge(self.ring_full[slot], 4 * (t - slot) + 16)
            nc.scalar.wait_ge(self.s_mm, h - 3 + CREDIT)
            nc.scalar.activation(hi, raw, ACT.Copy).then_inc(self.s_hi, 1)
            nc.vector.wait_ge(self.s_hi, h + 1 + CREDIT)
            nc.vector.tensor_tensor(lo, raw, hi.bitcast(F32), ALU.subtract).then_inc(self.s_lo, 1)

        def multiply(n):
            j, spec, g, tn, q, u, last_half = halves[n]
            ncol, widths, xh, xl = sum(spec["widths"]), spec["widths"], spec["xh"], spec["xl"]
            par = (par0 + j) % banks
            ps = self.PS[:, 2 * par:2 * par + 2, :]
            h, hs = 2 * (t0 + tn) + u, (2 * (tc + tn) + u) % 4
            if q == 0 and u == 0:
                nc.tensor.wait_ge(self.s_evac, b0 + j - banks + 1 + CREDIT)
            nc.tensor.wait_ge(self.s_lo, h + 1 + CREDIT)
            for a in range(2):
                k = 4 * q + 2 * u + a
                for m, (wt, xt) in enumerate(((self.whi, xh), (self.whi, xl), (self.wlo, xh))):
                    first, last = k == 0 and m == 0, k == spec["kt"] - 1 and m == 2
                    if spec["mode"] == "tok":
                        for tt in range(NT):
                            mm = nc.tensor.matmul(ps[:, tt, 0:ncol], xt[:, k, tt * P:(tt + 1) * P],
                                                  wt[:, hs, a, 0:ncol], start=first, stop=last)
                    else:
                        o = 0
                        for f, wd in enumerate(widths):
                            mm = nc.tensor.matmul(ps[0:wd, f // 2, (f % 2) * SEQ:(f % 2) * SEQ + SEQ],
                                                  wt[:, hs, a, o:o + wd], xt[:, k, :],
                                                  start=first and f % 2 == 0, stop=last,
                                                  skip_group_check=True)
                            o += wd
            mm.then_inc(self.s_mm, 1)

        def evacuation(j):
            return self.evac_of(todo[j][0], todo[j][1], (par0 + j) % banks, t0 + ends[j], b0 + j)

        for n in range(min(ahead, len(halves))):
            split(n)
        since = 0
        for n, (j, spec, g, tn, q, u, last_half) in enumerate(halves):
            if q == 0 and u == 0:
                since = 0
            if n + ahead < len(halves):
                split(n + ahead)
            if late is not None and j == 0 and 4 * q >= late and u == 0:
                for _ in prev or ():
                    pass
                prev = None
                self.T.wait(self.V.tok(), self.S.tok())
            if feed is not None and j == 0:
                gen, there = feed
                need = min(4 * q + 2 * u + 1, spec["kt"] - 1)
                while len(there) <= need + 2 and next(gen, self) is not self:
                    pass
                self.T.wait(there[need])
            multiply(n)
            since += 1
            if prev is not None and since >= 2:
                prev = None if next(prev, True) else prev
            if last_half:
                for _ in prev or ():
                    pass
                ends[j] = tn + 1
                prev = evacuation(j)
            yield
        self.tile_const += nt
        self.blk_const += len(todo)
        self.par0 = (par0 + len(todo)) % banks
        return prev

    def stream(self, name, groups, specs, ahead=0, late=None, feed=None):
        L = len(specs)
        assert L % 2 == 0 or groups == 1
        if late is not None:
            self.T.wait(self.V.tok(), self.S.tok())
        self.pend = yield from self.blocks([(sp, 0) for sp in specs], self.pend, ahead, late=late, feed=feed)
        if groups > 1:
            def left_over(g):
                return self.evac_of(specs[-1], g, (self.par0 - 1) % 2, self.tile(), self.blk() - 1)
            with self.loop(groups - 1, name, sum((sp["kt"] + 3) // 4 for sp in specs), L) as i:
                yield from self.blocks([(sp, i + 1) for sp in specs], left_over(i))
            self.pend = left_over(groups - 1)

    def evac_of(self, spec, g, par, tiles, block):
        ps = self.PS[:, 2 * par:2 * par + 2, :]
        if spec["mode"] == "feat":
            ps = ps.rearrange("p a (f t) -> p (a f) t", t=SEQ)
        return spec["evac"](g, ps, (self.s_mm, 2 * tiles + CREDIT), (self.s_evac, block + 1 + CREDIT))

    def flush(self):
        for _ in self.pend or ():
            pass
        self.pend = None

    def run_now(self, gen):
        for _ in gen:
            pass

    def together(self, *gens):
        gens = list(gens)
        while gens:
            for item in list(gens):
                gen, n = item
                for _ in range(n):
                    if next(gen, self) is self:
                        gens.remove(item)
                        break

    def done_evac(self, ins):
        ins.then_inc(self.s_evac, 1)

    def constants(self):
        nc, G, V, sb = self.nc, self.G, self.V, self.sb
        self.ident = sb("ident", [P, P])
        self.ones = sb("ones", [P, P])
        self.triu = sb("triu", [P, P])
        self.negl = sb("negl", [P, P])
        self.negu = sb("negu", [P, P])
        self.sel = sb("sel", [P, RP, 16])
        self.selT = sb("selT", [16, RP, 2])
        self.m_in = sb("m_in", [P, P])
        self.m_st = sb("m_st", [P, P])
        self.m_d = sb("m_d", [P, P])
        self.m_dT = sb("m_dT", [P, P])
        self.m_oT = sb("m_oT", [P, P])
        self.m_ic = sb("m_ic", [P, RC])
        self.rst = sb("rst", [P, SEQ])

        def sel(dst, src, pattern, base, cm, op, fill):
            return G.seq(nc.gpsimd.affine_select(out=dst, in_=src, pattern=pattern, compare_op=op,
                                                 fill=fill, base=base, channel_multiplier=cm))
        ge, ne = ALU.is_ge, ALU.not_equal
        G.seq(nc.gpsimd.memset(self.ident[:, :], 0.0))
        I, one = self.ident[:, :], [[1, P]]
        sel(I, I, [[-1, P]], 0, 1, ne, 1.0)
        yield
        for t, v in ((self.ones, 1.0), (self.triu, 1.0), (self.negl, 0.0),
                     (self.negu, 0.0), (self.sel, 1.0), (self.selT, 1.0), (self.m_in, 1.0),
                     (self.m_st, 1.0), (self.m_d, -1.0),  (self.m_dT, -1.0), (self.m_oT, -1.0),
                     (self.m_ic, 1.0), (self.rst, 1.0)):
            ap = t[:, :] if len(t.shape) == 2 else t[:, :, :]
            G.seq(nc.gpsimd.memset(ap, v))
        up = lambda t, fill, base=0: sel(t[:, :], t[:, :], one, base, -1, ge, fill)
        up(self.triu, 0.0)
        up(self.negl, NEG)
        sel(self.negu[:, :], self.negu[:, :], [[-1, P]], 0, 1, ge, NEG)
        up(self.m_in, 0.0)
        up(self.m_st, 0.0, -1)
        up(self.m_d, 0.0, -1)
        for t in (self.m_dT, self.m_oT):
            sel(t[:, :], t[:, :], [[-1, P]], -1, 1, ge, 0.0)

        def same_block(t, n):
            for lo, cm, st in ((0, 1, -n), (n - 1, -1, n)):
                v = t[:, :].rearrange("p (j e) -> p j e", e=n)
                sel(v, v, [[st, P // n], [0, n]], lo, cm, ge, 0.0)
        same_block(self.m_in, RC)
        same_block(self.m_st, RC)
        same_block(self.m_d, 16)
        same_block(self.m_dT, 16)
        same_block(self.m_oT, RC)
        G.seq(nc.gpsimd.tensor_tensor(self.m_oT[:, :], self.m_oT[:, :], self.m_dT[:, :], ALU.subtract))
        for t, pat, cm in ((self.sel[:, :, :], [[128, RP], [-64, 16]], 1),
                           (self.selT[:, :, :], [[-2, RP], [-1, 2]], 1)):
            if pat[0][0] == 128:
                sel(t, t, pat, 0, 1, ge, 0.0)
                sel(t, t, [[-128, RP], [64, 16]], 63, -1, ge, 0.0)
            else:
                sel(t, t, pat, 0, 1, ge, 0.0)
                sel(t, t, [[2, RP], [1, 2]], 0, -1, ge, 0.0)
        for hp in range(2):
            v = self.m_ic[hp * 64:hp * 64 + 64, :]
            sel(v, v, [[1, RC]], 0, -1, ge, 0.0)
        v = self.rst[:, :].rearrange("p (c e) -> p c e", e=RC)
        sel(v, v, [[0, NRC], [1, RC]], -1, 0, ge, 0.0)

    def params(self):
        groups = [
            [("norm_mix_g", 16), ("norm_x_g", 16), ("norm_mem_g", 16), ("norm_ffn_g", 16),
             ("norm1_gain_2", 16), ("norm2_gain_2", 16), ("hgrn_lb_param_2", 16), ("hgrn_norm_gain_2", 1)],
            [("ssd_conv_w", 48), ("ssd_conv_b", 12), ("ssd_norm_g", 8), ("rwkv_w0", 8), ("rwkv_a0", 8),
             ("rwkv_k_k", 8), ("rwkv_k_a", 8), ("rwkv_r_k", 8), ("rwkv_ln_w", 8), ("rwkv_ln_b", 8)],
            [("ffn_conv_w_2", 128)],
            [("ffn_conv_w_2b", 4), ("ffn_conv_b_2", 44), ("mu", 24)],
        ]
        self.par_groups = groups
        self.col, base = {}, 0
        for g in groups:
            for name, n in g:
                if name == "ffn_conv_w_2":
                    self.fcw = self.param_cols[:, base:base + 132].rearrange("p (j f) -> p j f", f=44)
                self.col[name] = self.param_cols[:, base:base + n]
                base += n

    def param_rows(self, k):
        i, r = self.i, 0
        rows = lambda a: self.flat(a).rearrange("(n p) -> n p", p=P)
        for name, n in self.par_groups[k]:
            if name == "ffn_conv_w_2":
                src = rows(i[name])[0:128, :]
            elif name == "ffn_conv_w_2b":
                src = rows(i["ffn_conv_w_2"])[128:132, :]
            elif name == "mu":
                src = self.flat(i["rwkv_mu"])[0:3072].rearrange("(n p) -> n p", p=P)
            else:
                src = rows(i[name])
            t = self.load(9 if k else 0, self.view(P * k, P)[r:r + n, :], src, self.nc.sync if k else None)
            r += n
        return t

    def param_turn(self, k, bank, t):
        nc, T, S = self.nc, self.T, self.S
        r = sum(n for _, n in self.par_groups[k])
        base = sum(n for g in self.par_groups[:k] for _, n in g)
        T.wait(t)
        t = T(nc.tensor.transpose(self.PS[:, bank, 0:r], self.view(P * k, P)[0:r, :], self.ident[0:r, 0:r]))
        S.wait(t)
        return S(nc.scalar.activation(self.param_cols[:, base:base + r], self.PS[:, bank, 0:r], ACT.Copy))

    def flat(self, a):
        while len(a.shape) > 1:
            names = " ".join(f"d{k}" for k in range(len(a.shape)))
            a = a.rearrange(f"{names} -> ({names})")
        return a

    def squares(self, x, junk):
        for tt in range(NT):
            s = self.S(self.nc.scalar.activation(junk[:, tt, :], x[:, tt, :], ACT.Square,
                                                 accum_out=self.ssq[:, tt, 0:1]))
        return s

    def rstd(self, parts):
        nc, V, S, stat = self.nc, self.V, self.S, self.stat
        if parts > 1:
            V.seq(nc.vector.tensor_reduce(stat[:, 0:NT], self.ssq[:, :, 0:parts], AX.X, ALU.add))
            src = stat[:, 0:NT]
        else:
            src = self.ssq[:, :, 0]
        S.wait(V(nc.vector.tensor_scalar(stat[:, 0:NT], src, 1.0 / D, EPS, ALU.mult, ALU.add)))
        V.wait(S(nc.scalar.activation(stat[:, 0:NT], stat[:, 0:NT], ACT.Sqrt)))
        V.seq(nc.vector.reciprocal(stat[:, 0:NT], stat[:, 0:NT]))

    def to_feat(self, src, gain, xh, xl, n, k0=0, banks=8, b0=0, there=None, ready=None):
        nc, T, V, S = self.nc, self.T, self.V, self.S
        v_at = {} if there is None else there
        for k in range(n):
            if ready is not None and k % 4 == 0:
                T.wait(ready[k // 4])
            if k >= banks:
                T.wait(v_at[k - banks])
            bank = b0 + k % banks
            for tt in range(NT):
                t = T(nc.tensor.transpose(self.PS[:, bank, tt * P:(tt + 1) * P], src(tt, k), self.ident[:, :]))
            S.wait(t)
            ps = self.PS[:, bank, 0:SEQ]
            s = S(nc.scalar.activation(xh[:, k0 + k, :], ps, ACT.Copy, scale=gain[:, k:k + 1]))
            V.wait(s)
            v_at[k] = V(nc.vector.scalar_tensor_tensor(xl[:, k0 + k, :], ps, gain[:, k:k + 1],
                                                       xh[:, k0 + k, :].bitcast(F32), ALU.mult, ALU.subtract))
            yield

    def norm_feed(self, x, xn, gain, parts):
        nc, V = self.nc, self.V
        self.rstd(parts)
        ready = []
        for q in range(4):
            for tt in range(NT):
                c = slice(512 * q, 512 * q + 512)
                v = V(nc.vector.tensor_scalar(xn[:, tt, c], x[:, tt, c], self.stat[:, tt:tt + 1], None, ALU.mult))
            ready.append(v)
        there = {}
        return self.to_feat(lambda tt, k: xn[:, tt, k * P:(k + 1) * P], gain, self.XH, self.XL, KD,
                            banks=4, b0=4, there=there, ready=ready), there


class LoopScope:

    def __init__(self, prog, n, name, tiles, blks):
        self.p, self.n, self.name, self.tiles, self.blks = prog, n, name, tiles, blks

    def __enter__(self):
        p = self.p
        self.steps = STEPS.get(self.name, (0, 0, 0, 0))
        self.start = [l.const for l in p.lanes]
        self.t0, self.b0 = p.tile_const, p.blk_const
        self.cm = p.nc.Fori(0, self.n)
        i = self.cm.__enter__()
        for l, s in zip(p.lanes, self.steps):
            l.terms.append((i, s))
        p.tile_terms.append((i, self.tiles))
        p.blk_terms.append((i, self.blks))
        return i

    def __exit__(self, *exc):
        p = self.p
        self.cm.__exit__(*exc)
        if exc[0] is not None:
            return False
        made = tuple(l.const - s for l, s in zip(p.lanes, self.start))
        assert made == tuple(self.steps), (self.name, made)
        assert p.tile_const - self.t0 == self.tiles and p.blk_const - self.b0 == self.blks
        for l, s, m in zip(p.lanes, self.start, made):
            l.const = s + self.n * m
            l.terms.pop()
        p.tile_const = self.t0 + self.n * self.tiles
        p.blk_const = self.b0 + self.n * self.blks
        p.tile_terms.pop()
        p.blk_terms.pop()
        return False


class Model(Prog):

    def bc(self, ap, n):
        return ap.unsqueeze(2).to_broadcast([ap.shape[0], ap.shape[1], n])

    def rep(self, ap, n):
        return ap.unsqueeze(1).to_broadcast([ap.shape[0], n, ap.shape[1]])

    def spec(self, w, mode, col, evac, kt=KD, k0=0, xh=None, xl=None, widths=None):
        return dict(w=w, k0=k0, kt=kt, xh=xh if xh is not None else self.XH, xl=xl if xl is not None else self.XL,
                    mode=mode, col=col, evac=evac,
                    widths=widths or ([512] if mode == "tok" else [P] * 4))

    def ev_feat(self, dst, j, L, func=ACT.Copy):
        def evac(g, ps, ready, out):
            self.S.wait(ready)
            self.done_evac(self.nc.scalar.activation(dst[:, ds(4 * (g * L + j), 4), :], ps, func))
            yield
        return evac

    def ev_tok(self, dst, j, L, func=ACT.Copy):
        def evac(g, ps, ready, out):
            self.S.wait(ready)
            self.done_evac(self.nc.scalar.activation(dst[:, :, ds(512 * (g * L + j), 512)], ps, func))
            yield
        return evac

    def ev_add(self, x, j, L, junk=None, there=()):
        def evac(g, ps, ready, out):
            self.V.wait(ready, *there)
            b = g * L + j
            o = x[:, :, ds(512 * b, 512)]
            self.done_evac(self.nc.vector.tensor_tensor(o, o, ps, ALU.add))
            yield
            if junk is not None:
                self.S.wait(out, self.S.tok())
                for tt in range(NT):
                    self.S(self.nc.scalar.activation(junk[:, tt, 0:512], x[:, tt, ds(512 * b, 512)], ACT.Square,
                                                     accum_out=self.ssq[:, tt, ds(b, 1)]))
                yield
        return evac

    def proj(self, name, w, c0, n, mode, ev, kt=KD, k0=0, xh=None, xl=None, late=None, feed=None):
        L = 2 if n > 2 else n
        specs = [self.spec(w, mode, (lambda g, j=j: 512 * (g * L + j) + c0), ev(j, L), kt, k0, xh, xl)
                 for j in range(L)]
        self.run_now(self.stream(name, n // L, specs, late=late, feed=feed))

    def shift_mix(self, buf, tmp, mu, dst, p, f0, f1):
        nc, V = self.nc, self.V
        u, up, t = buf[0:p, f0:f1, 1:1 + SEQ], buf[0:p, f0:f1, 0:SEQ], tmp[0:p, f0:f1, :]
        V.seq(nc.vector.tensor_tensor(t, up, u, ALU.subtract))
        yield
        V.seq(nc.vector.tensor_tensor(t, t, self.bc(mu, SEQ), ALU.mult))
        yield
        V.seq(nc.vector.tensor_tensor(dst, u, t, ALU.add))

    def log1p_exp_negabs(self, out, x, t):
        nc, V, S = self.nc, self.V, self.S
        e, u, d = t
        V.seq(nc.vector.scalar_tensor_tensor(e, x, -1.0, x, ALU.mult, ALU.max))
        yield
        S.wait(V.tok())
        S.seq(nc.scalar.activation(e, e, ACT.Exp, scale=-1.0))
        yield
        V.wait(S.tok())
        V.seq(nc.vector.tensor_scalar(u, e, 1.0, None, ALU.add))
        yield
        S.wait(V.tok())
        S(nc.scalar.activation(out, u, ACT.Ln))
        V.seq(nc.vector.tensor_scalar(d, u, -1.0, 5e-8, ALU.add, ALU.max))
        V.seq(nc.vector.reciprocal(d, d))
        V.seq(nc.vector.tensor_tensor(d, d, e, ALU.mult))
        yield
        V.wait(S.tok())
        V.seq(nc.vector.tensor_tensor(out, out, d, ALU.mult))
        V.seq(nc.vector.tensor_scalar(u, e, -0.5, 1.0, ALU.mult, ALU.add))
        V.seq(nc.vector.tensor_tensor(u, u, e, ALU.mult))
        V.seq(nc.vector.tensor_tensor(out, out, u, ALU.max))

    def split(self, xh, xl, ps, scale=None):
        nc, V, S = self.nc, self.V, self.S
        if scale is None:
            S(nc.scalar.activation(xh, ps, ACT.Copy))
            V.wait(S.tok())
            return V(nc.vector.tensor_tensor(xl, ps, xh.bitcast(F32), ALU.subtract))
        S(nc.scalar.activation(xh, ps, ACT.Copy, scale=scale))
        V.wait(S.tok())
        return V(nc.vector.scalar_tensor_tensor(xl, ps, scale, xh.bitcast(F32), ALU.mult, ALU.subtract))

    def block1_in(self, constants):
        nc, V, S, G, i = self.nc, self.V, self.S, self.G, self.i
        w = i["w_in"][0]
        Z = self.Z = self.view(0, NT, SSD_W)
        XBC_ = self.XBC = self.view(4096, 12, SEQ)
        RKV = self.RKV = self.view(7168, 24, SEQ)
        LO = self.LO = self.view(13312, 4, SEQ)
        DT = self.DT = self.view(14336, NT, 16)
        xn = self.view(16416, NT, D)
        buf3, buf1 = self.view(20528, 4, SEQ + 3), self.view(21568, 4, SEQ + 1)
        tmp, acc = self.view(22600, 4, SEQ), self.view(23624, 4, SEQ)
        G(nc.gpsimd.memset(buf3[:, :, 0:3], 0.0))
        G(nc.gpsimd.memset(buf1[:, :, 0:1], 0.0))
        S.wait(G.tok())
        V.wait(G.tok())
        feed = self.norm_feed(self.x_in, xn, self.col["norm_mix_g"], 1)
        self.run_now(constants)

        def first_block():
            rest = self.rest_of_params()
            for k, _ in enumerate(feed[0]):
                if k == 5:
                    next(rest)
                yield
            self.T.wait(feed[1][KD - 1])
            yield from rest

        def ev_rkv(j, L):
            def evac(g, ps, ready, out):
                S.wait(ready, V.tok())
                self.done_evac(nc.scalar.activation(buf1[:, :, 1:1 + SEQ], ps, ACT.Copy))
                yield
                V.wait(out)
                b = g * L + j
                yield from self.shift_mix(buf1, tmp, self.col["mu"][:, ds(4 * b, 4)], RKV[:, ds(4 * b, 4), :], P, 0, 4)
                yield
            return evac

        def ev_xbc(j):
            def evac(g, ps, ready, out):
                S.wait(ready, V.tok())
                self.done_evac(nc.scalar.activation(buf3[:, :, 3:3 + SEQ], ps, ACT.Copy))
                yield
                V.wait(out)
                cw = self.col["ssd_conv_w"]
                for tap in range(SSD_CONV):
                    src = buf3[:, :, tap:tap + SEQ]
                    wt = self.bc(cw[:, 12 * tap + 4 * j:12 * tap + 4 * j + 4], SEQ)
                    if tap == 0:
                        V.seq(nc.vector.tensor_tensor(acc, src, wt, ALU.mult))
                    else:
                        V.seq(nc.vector.tensor_tensor(tmp, src, wt, ALU.mult))
                        yield
                        V.seq(nc.vector.tensor_tensor(acc, acc, tmp, ALU.add))
                    yield
                V.seq(nc.vector.tensor_tensor(acc, acc, self.bc(self.col["ssd_conv_b"][:, 4 * j:4 * j + 4], SEQ),
                                              ALU.add))
                yield
                S.wait(V.tok())
                S(nc.scalar.activation(XBC_[:, 4 * j:4 * j + 4, :], acc, ACT.Silu))
                V.wait(S.tok())
            return evac

        def ev_lora(g, ps, ready, out):
            S.wait(ready, V.tok())
            S.seq(nc.scalar.activation(buf1[0:LORA, 0:2, 1:1 + SEQ], ps[0:LORA, 0:2, :], ACT.Copy))
            self.done_evac(nc.scalar.activation(buf1[:, 2:4, 1:1 + SEQ], ps[:, 2:4, :], ACT.Copy))
            yield
            V.wait(S.tok(), out)
            yield from self.shift_mix(buf1, tmp, self.mul[0:LORA, 0:2], LO[0:LORA, 0:2, :], LORA, 0, 2)
            yield from self.shift_mix(buf1, tmp, self.mul[:, 2:4], LO[:, 2:4, :], P, 2, 4)

        def ev_dt(g, ps, ready, out):
            S.wait(ready)
            self.done_evac(nc.scalar.activation(DT, ps[:, :, 0:16], ACT.Copy))
            yield

        self.proj("w_in_rkv", w, 2576, 6, "feat", ev_rkv, feed=(first_block(), feed[1]))
        sp = [self.spec(w, "feat", (lambda g, j=j: 1024 + 512 * j), ev_xbc(j)) for j in range(3)]
        sp.append(self.spec(w, "feat", lambda g: 2576 + 3072, ev_lora, widths=[LORA, LORA, P, P]))
        sp += [self.spec(w, "tok", (lambda g, j=j: 512 * j), self.ev_tok(Z, j, 2, ACT.Silu)) for j in range(2)]
        sp.append(self.spec(w, "tok", lambda g: 2560, ev_dt, widths=[16]))
        self.run_now(self.stream("w_in_rest", 1, sp))
        self.join()

    def ssd(self):
        nc, T, V, S, G = self.nc, self.T, self.V, self.S, self.G
        PS, DT, XB, Z = self.PS, self.DT, self.XBC, self.Z
        ring = self.raw[:, :, :, :].rearrange("p a b c -> p (a b c)")
        part = lambda o, a, n: ring[:, o:o + a * n].rearrange("p (a n) -> p a n", a=a)
        xs, xdt, y = part(0, NT, SSD_W), part(2048, NT, SSD_W), part(4096, NT, SSD_W)
        xdte, st = ring[:, 6144:7168], part(7168, SSD_G, 512)
        o = 18464
        bm, cbT = self.view(o, 256), self.view(o + 256, 4, P)
        L = [self.view(o + 768 + 512 * q, 4, P) for q in range(2)]
        junk = self.view(4096, 512)
        o = 25168
        sm = [self.view(o + 32 * k, NT, 16) for k in range(10)]
        A = self.view(o + 320, 16)
        dt, da, cs, ecs, dte, t0, t1, t2, ncs, rs = sm
        free, n = {}, 0
        for c in range(NT):
            for q in range(3):
                if (c, q) == (1, 2):
                    break
                fs = range(4 * q, min(4 * q + 4, 10))
                bank = n % 4
                if n >= 4:
                    T.wait(free[bank])
                for k, f in enumerate(fs):
                    t = T(nc.tensor.transpose(PS[:, bank, k * P:(k + 1) * P], XB[:, f, c * P:(c + 1) * P],
                                              self.ident[:, :]))
                S.wait(t)
                dst = xs[:, c, 512 * q:512 * q + 512] if q < 2 else bm
                free[bank] = S(nc.scalar.activation(dst, PS[:, bank, 0:P * len(fs)], ACT.Copy))
                n += 1
                yield
        free_all = S.tok()
        S.seq(nc.scalar.activation(A, self.alog[:, :], ACT.Exp))
        V.seq(nc.vector.tensor_tensor(DT, DT, self.rep(self.dtb[:, :], NT), ALU.add))
        yield from self.log1p_exp_negabs(dt, DT, (t0, t1, t2))
        V.seq(nc.vector.scalar_tensor_tensor(dt, DT, 0.0, dt, ALU.max, ALU.add))
        V.seq(nc.vector.tensor_tensor(da, dt, self.rep(A, NT), ALU.mult))
        v = V.seq(nc.vector.tensor_scalar(da, da, -1.0, None, ALU.mult))
        T.wait(v, S.tok())
        T(nc.tensor.matmul(PS[:, 0, 0:32], self.triu[:, :], da, start=True, stop=True))
        t = T(nc.tensor.matmul(PS[:, 1, 0:32], self.ones[:, :], da, start=True, stop=True))
        yield
        V.wait(t)
        as2 = lambda b: PS[:, b, 0:32].rearrange("p (c h) -> p c h", c=NT)
        V.seq(nc.vector.tensor_copy(cs, as2(0)))
        V.seq(nc.vector.tensor_tensor(dte, as2(1), cs, ALU.subtract))
        v_c = V.seq(nc.vector.tensor_scalar(ncs, cs, -1.0, None, ALU.mult))
        S.wait(v_c)
        S(nc.scalar.activation(ecs, cs, ACT.Exp))
        s_e = S(nc.scalar.activation(dte, dte, ACT.Exp))
        hv = lambda ap: ap.rearrange("p (h e) -> p h e", e=64)
        for c in range(NT):
            V(nc.vector.tensor_tensor(hv(xdt[:, c, :]), hv(xs[:, c, :]), self.bc(dt[:, c, :], 64), ALU.mult))
            G.wait(free_all)
            g_d = G(nc.gpsimd.tensor_tensor(hv(y[:, c, :]), hv(xs[:, c, :]), self.bc(self.dsk[:, :], 64), ALU.mult))
        V.wait(s_e, V.tok())
        v_x = V(nc.vector.tensor_tensor(hv(xdte), hv(xdt[:, 0, :]), self.bc(dte[:, 0, :], 64), ALU.mult))
        yield
        T.wait(v_x)
        for g in range(SSD_G):
            t = T(nc.tensor.matmul(PS[:, 2 + g, :], bm[:, g * P:(g + 1) * P], xdte[:, g * 512:g * 512 + 512],
                                   start=True, stop=True))
        S.wait(t)
        s_l = s_st = S(nc.scalar.activation(st, PS[:, 2:4, :], ACT.Copy))
        T.wait(s_st)
        yield
        cT = lambda c, g: XB[:, 10 + g, c * P:(c + 1) * P]
        for n in range(4):
            c, g = n // 2, n % 2
            t = T(nc.tensor.matmul(PS[:, 0, n * P:(n + 1) * P], XB[:, 8 + g, c * P:(c + 1) * P], cT(c, g),
                                   start=n == 0, stop=True, skip_group_check=True))
        V.wait(t)
        v_cb = V(nc.vector.tensor_copy(cbT, PS[:, 0, :].rearrange("p (n t) -> p n t", n=4)))
        T.wait(v_cb)
        s_l, v_l, y_t = [s_st, s_st], [v_cb, v_cb], [v_cb, v_cb]

        def decays(c, g, q):
            bank = (3, 0)[q]
            T.wait(s_l[q])
            T(nc.tensor.matmul(PS[:, bank, :], self.ident[:, :], self.rep(self.negl[:, :], 4),
                               start=True, stop=False, skip_group_check=True))
            for e in range(4):
                h = 8 * g + 4 * q + e
                t = T(nc.tensor.matmul(PS[:, bank, e * P:(e + 1) * P], da[:, c, h:h + 1].to_broadcast([P, P]),
                                       self.triu[:, :], start=False, stop=True, skip_group_check=True))
            S.wait(t, y_t[q])
            for e in range(4):
                h = 8 * g + 4 * q + e
                s_l[q] = S(nc.scalar.activation(L[q][:, e, :], PS[:, bank, e * P:(e + 1) * P], ACT.Exp,
                                                bias=ncs[:, c, h:h + 1]))
            V.wait(s_l[q])
            v_l[q] = V(nc.vector.tensor_tensor(L[q], L[q], self.rep(cbT[:, 2 * c + g, :], 4), ALU.mult))
        steps = [(c, g, q) for c in range(NT) for g in range(SSD_G) for q in range(2)]
        v_y = v_cb
        decays(*steps[0])
        for n, (c, g, q) in enumerate(steps):
            if n + 1 < len(steps):
                decays(*steps[n + 1])
            yield
            if q == 0:
                T.wait(v_y)
                if c > 0:
                    T(nc.tensor.matmul(PS[:, 2, :], cT(c, g), st[:, g, :], start=True, stop=True))
            T.wait(v_l[q])
            for e in range(4):
                h = 8 * g + 4 * q + e
                y_t[q] = T(nc.tensor.matmul(PS[:, 1, (4 * q + e) * 64:(4 * q + e) * 64 + 64], L[q][:, e, :],
                                            xdt[:, c, h * 64:h * 64 + 64], start=(q == 0 and e == 0),
                                            stop=True, skip_group_check=True))
            yield
            if q == 1:
                yg = y[:, c, g * 512:g * 512 + 512]
                V.wait(y_t[1], g_d)
                V.seq(nc.vector.tensor_tensor(yg, yg, PS[:, 1, :], ALU.add))
                if c > 0:
                    V.seq(nc.vector.tensor_tensor(hv(junk), hv(PS[:, 2, :]),
                                                  self.bc(ecs[:, c, 8 * g:8 * g + 8], 64), ALU.mult))
                    V.seq(nc.vector.tensor_tensor(yg, yg, junk, ALU.add))
                v_y = V.seq(nc.vector.tensor_tensor(yg, yg, Z[:, c, g * 512:g * 512 + 512], ALU.mult))
                yield
        S.wait(v_y)
        for c in range(NT):
            for g in range(SSD_G):
                S.wait(S.tok())
                s = S(nc.scalar.activation(junk, y[:, c, g * 512:g * 512 + 512], ACT.Square,
                                           accum_out=rs[:, c, g:g + 1]))
        yield
        V.wait(s)
        r = rs[:, :, 0:2]
        v = V.seq(nc.vector.tensor_scalar(r, r, 1.0 / 512, EPS, ALU.mult, ALU.add))
        S.wait(v)
        s = S(nc.scalar.activation(r, r, ACT.Sqrt))
        yield
        V.wait(s)
        V.seq(nc.vector.reciprocal(r, r))
        for c in range(NT):
            for g in range(SSD_G):
                yg = y[:, c, g * 512:g * 512 + 512]
                v = V(nc.vector.tensor_scalar(yg, yg, rs[:, c, g:g + 1], None, ALU.mult))
        yield
        T.wait(v)
        yield from self.to_feat(lambda tt, k: y[:, tt, k * P:(k + 1) * P], self.col["ssd_norm_g"], self.XH, self.XL,
                                8, banks=4)

    def feat_view(self, b0):
        return self.PS[:, b0:b0 + 4, :].rearrange("p a (f t) -> p (a f) t", t=SEQ)

    def head_sum(self, src, bank):
        for f in range(RP):
            self.T(self.nc.tensor.matmul(self.PS[0:16, bank, 0:SEQ], self.sel[:, f, :], src[:, f, :],
                                         start=f == 0, stop=f == RP - 1))

    def head_bcast(self, src, b0):
        v = self.feat_view(b0)
        for f in range(RP):
            self.T(self.nc.tensor.matmul(v[:, f, :], self.spread[:, f, :].bitcast(F32), src,
                                         start=f % 2 == 0, stop=True, skip_group_check=True))
        return v

    def rwkv_views(self):
        self.IC, self.KK, self.LW = self.view(2048, RP, SEQ), self.view(16416, RP, SEQ), self.view(14368, RP, SEQ)
        self.t1 = self.view(20512, RP, SEQ)
        self.hs, self.bs = self.view(24608, SEQ)[0:16, :], self.view(24864, SEQ)[0:16, :]
        self.eend = self.view(25120, RP, NRC)

    def rwkv_prep(self):
        nc, T, V, S, G, i = self.nc, self.T, self.V, self.S, self.G, self.i
        PS, LO, col = self.PS, self.LO, self.col
        tt = lambda o, a, b, op: V.seq(nc.vector.tensor_tensor(o, a, b, op))
        R, K, VV = (self.RKV[:, 8 * k:8 * k + 8, :] for k in range(3))
        LW, IC, KK, t1, hs, bs, eend = self.LW, self.IC, self.KK, self.t1, self.hs, self.bs, self.eend
        w2, a2 = self.view(22560, 1024), self.view(23584, 1024)
        la = self.load(2, w2[0:LORA, :], i["rwkv_w2"][0])
        la = self.load(2, a2[0:LORA, :], i["rwkv_a2"][0])
        S(nc.scalar.activation(LO[0:LORA, 0, :], LO[0:LORA, 0, :], ACT.Tanh))
        s = S(nc.scalar.activation(LO[:, 2:4, :], LO[:, 2:4, :], ACT.Sigmoid))
        room = self.XH[0:16, 8:12, :]
        V(nc.vector.tensor_copy(room.rearrange("p a (b c) -> p (a b) c", c=64),
                                self.selT[:, :, :].rearrange("p a b -> p (a b)").unsqueeze(2)
                                .to_broadcast([16, 16, 64])))
        self.spread = room.rearrange("p a (b c) -> p (a b) c", c=P)
        tt(KK, K, self.bc(col["rwkv_k_k"], SEQ), ALU.mult)
        v_kk = tt(t1, KK, KK, ALU.mult)
        yield
        T.wait(s, la)
        for n, (w, dst, b) in enumerate(((w2, LW, "rwkv_w0"), (a2, IC, "rwkv_a0"))):
            v = self.feat_view(4)
            if n:
                T.wait(s)
            for f in range(RP):
                t = T(nc.tensor.matmul(v[:, f, :], w[0:LORA, f * P:(f + 1) * P], LO[0:LORA, n, :],
                                       start=f % 2 == 0, stop=True, skip_group_check=True))
            S.wait(t)
            yield
            for f in range(RP):
                s = S(nc.scalar.activation(dst[:, f, :], v[:, f, :], ACT.Sigmoid, bias=col[b][:, f:f + 1]))
                if f % 4 == 3:
                    yield
        T.wait(v_kk, s)
        self.head_sum(t1, 4)
        t = T.tok()
        V.wait(s)
        V.seq(nc.vector.tensor_scalar(LW, LW, -0.6065306597126334, None, ALU.mult))
        yield
        S.wait(t)
        s = S(nc.scalar.activation(hs, PS[0:16, 4, 0:SEQ], ACT.Sqrt))
        V.wait(t)
        V.seq(nc.vector.tensor_scalar(t1, IC, -1.0, None, ALU.add))
        tt(t1, t1, self.bc(col["rwkv_k_a"], SEQ), ALU.mult)
        yield
        V.wait(s)
        V.seq(nc.vector.tensor_scalar(hs, hs, 1e-12, None, ALU.max))
        v = V.seq(nc.vector.reciprocal(hs, hs))
        T.wait(v)
        vb = self.head_bcast(hs, 4)
        t = T.tok()
        V.seq(nc.vector.scalar_tensor_tensor(K, t1, 1.0, K, ALU.add, ALU.mult))
        yield
        tt(t1, R, K, ALU.mult)
        v = tt(t1, t1, self.bc(col["rwkv_r_k"], SEQ), ALU.mult)
        yield
        V.wait(t)
        v_n = tt(KK, KK, vb, ALU.mult)
        yield
        T.wait(v, v_n)
        self.head_sum(t1, 4)
        t = T.tok()
        tt(IC, KK, IC, ALU.mult)
        yield
        V.wait(t)
        V.seq(nc.vector.tensor_copy(bs, PS[0:16, 4, 0:SEQ]))
        for f in range(RP):
            v = V(nc.vector.tensor_tensor_scan(t1[:, f, :], self.rst[:, :], LW[:, f, :], 0.0, ALU.mult, ALU.add))
            if f % 2:
                yield
        V.wait(v)
        v = tt(LW, t1, LW, ALU.subtract)
        S.wait(v)
        s = S(nc.scalar.activation(LW, LW, ACT.Exp))
        yield
        V.wait(s)
        v = tt(KK, KK, LW, ALU.mult)
        S.wait(v)
        s = S(nc.scalar.activation(LW, t1, ACT.Exp))
        S.wait(s)
        s2 = S(nc.scalar.activation(t1, t1, ACT.Exp, scale=-1.0))
        yield
        V.wait(s)
        tt(R, R, LW, ALU.mult)
        V(nc.vector.tensor_copy(eend, LW.rearrange("p f (c e) -> p f c e", e=RC)[:, :, :, RC - 1]))
        yield
        V.wait(s2)
        tt(K, K, t1, ALU.mult)
        yield
        tt(IC, IC, t1, ALU.mult)

    def rwkv(self):
        nc, T, V, S, G, i = self.nc, self.T, self.V, self.S, self.G, self.i
        PS, LO, col = self.PS, self.LO, self.col
        tt = lambda o, a, b, op: V.seq(nc.vector.tensor_tensor(o, a, b, op))
        R, K, VV = (self.RKV[:, 8 * k:8 * k + 8, :] for k in range(3))
        Aa, Qq, eend, bs, hs = self.IC, self.KK, self.eend, self.bs, self.hs
        ring = self.raw[:, :, :, :].rearrange("p a b c -> p (a b c)")
        spots = [0, 1024, 4096, 5120, 6144, 14368, 15392, 18464, 19488, 20512, 21536, 22560]
        A_, K_, Q_, V_, LDT, LD, LO_, LK, PT, X1, X2, St = (self.view(s, RP, P) for s in spots)
        VC, StC, RAT, RKT = (self.view(s, RP, RC) for s in (23584, 24096, 13312, 25168))
        AT_, KT_, VT_ = (ring[:, o:o + 1024].rearrange("p (f e) -> p f e", f=RP) for o in (1024, 2048, 3072))
        ZC, Z0 = (ring[:, o:o + 512].rearrange("p (f e) -> p f e", f=RP) for o in (0, 512))
        for b in (A_, K_, Q_, LD, St, StC):
            V(nc.vector.memset(b, 0.0))
        for b in (V_,):
            G(nc.gpsimd.memset(b, 0.0))
        for l in (T, V, S, G):
            l.wait(G.tok(), V.tok())
        rep4 = lambda m: self.rep(m[:, :], 4)
        tmul = lambda o, a, b: V(nc.vector.tensor_tensor(o, a, b, ALU.mult))
        halves = [(slice(64 * e, 64 * e + 64), slice(64 * e, 64 * e + 64)) for e in range(2)]

        def inputs(c, grp):
            tok, fs = ds(c * RC, RC), slice(4 * grp, 4 * grp + 4)
            for r, q in halves:
                S(nc.scalar.activation(K_[r, fs, q], K[r, fs, tok], ACT.Copy))
                V(nc.vector.tensor_copy(A_[r, fs, q], Aa[r, fs, tok]))
                V(nc.vector.tensor_copy(Q_[r, fs, q], Qq[r, fs, tok]))
                G(nc.gpsimd.tensor_copy(V_[r, fs, q], VV[r, fs, tok]))

        def chunk(c, grp, last=False):
            tok, fs, b0 = ds(c * RC, RC), slice(4 * grp, 4 * grp + 4), 4 * grp

            def mm(bank, pairs, n=P, at=0, first=True):
                for f in range(4):
                    o = PS[:, b0 + bank, at + f * n:at + f * n + n]
                    for m, (a, b) in enumerate(pairs):
                        t = T(nc.tensor.matmul(o, a[:, 4 * grp + f, :], b[:, 4 * grp + f, :],
                                               start=first and f == 0 and m == 0, stop=m == len(pairs) - 1,
                                               skip_group_check=True))
                return t

            def turn(bank, a):
                for f in range(4):
                    t = T(nc.tensor.transpose(PS[:, b0 + bank, f * P:f * P + P], a[:, 4 * grp + f, :],
                                              self.ident[:, :]))
                return t
            full = lambda bank: PS[:, b0 + bank, :].rearrange("p (f t) -> p f t", f=4)
            comp = lambda bank, at=0: PS[:, b0 + bank, at:at + 4 * RC].rearrange("p (f t) -> p f t", f=4)
            copy = lambda dst, src: S(nc.scalar.activation(dst, src, ACT.Copy))
            x = lambda b: b[:, fs, :]
            Rt = R[:, :, tok]
            t_a = mm(0, [(A_, Q_)])
            t_b = mm(1, [(Q_, A_)])
            mm(3, [(A_, Rt)], RC)
            t_d = mm(3, [(K_, Rt)], RC, 4 * RC, False)
            t_e = mm(2, [(K_, Q_)])
            V.wait(t_a)
            v_dt = tmul(x(LDT), full(0), rep4(self.m_d))
            V.wait(t_b)
            v_l = tmul(x(LD), full(1), rep4(self.m_dT))
            v_o = tmul(x(LO_), full(1), rep4(self.m_oT))
            yield
            T.wait(v_l)
            t_u = mm(0, [(LD, LDT)])
            T.wait(v_o)
            t_ut = mm(1, [(LDT, LD)])
            V.wait(v_dt)
            v_p = V(nc.vector.tensor_tensor(x(PT), x(LDT), rep4(self.ident), ALU.add))
            V.wait(t_d)
            tmul(x(RAT), comp(3), self.rep(self.m_ic[:, :], 4))
            v_r = tmul(x(RKT), comp(3, 4 * RC), self.rep(self.m_ic[:, :], 4))
            V.wait(t_e)
            v_k = tmul(x(LK), full(2), rep4(self.m_st))
            yield
            S.wait(t_u)
            s_u = copy(x(X1), full(0))
            S.wait(t_ut)
            s_ut = copy(x(X2), full(1))
            T.wait(v_r)
            t_k = turn(3, K_)
            T.wait(v_k)
            t_v = turn(2, V_)
            yield
            T.wait(s_ut, v_p)
            t_p = mm(0, [(X2, PT)])
            t_u2 = mm(1, [(X2, X1)])
            S.wait(t_k)
            s_kt = copy(x(KT_), full(3))
            S.wait(t_v)
            s_vt = copy(x(VT_), full(2))
            G.wait_apart(s_vt)
            for r, q in halves:
                g_c = G(nc.gpsimd.tensor_copy(VC[r, fs, :], VT_[r, fs, q]))
            V.wait(t_p)
            v_p = V(nc.vector.tensor_tensor(x(PT), full(0), x(PT), ALU.add))
            V.wait(t_u2)
            v_u2 = V(nc.vector.tensor_copy(x(LD), full(1)))
            yield
            T.wait(s_kt)
            t_u2t = mm(3, [(X1, X2)])
            T.wait(s_vt)
            t_at = turn(2, A_)
            S.wait(t_u2t)
            s_u2t = copy(x(LDT), full(3))
            S.wait(t_at)
            s_at = copy(x(AT_), full(2))
            yield
            T.wait(s_u2t, v_p)
            t_p = mm(0, [(LDT, PT)])
            T.wait(v_u2)
            t_u3 = mm(1, [(LD, LDT)])
            V.wait(t_p)
            v_p = V(nc.vector.tensor_tensor(x(PT), full(0), x(PT), ALU.add))
            S.wait(t_u3)
            s_u3 = copy(x(X1), full(1))
            yield
            T.wait(s_at, g_c)
            t_r = mm(2, [(Q_, StC), (LK, VC)], RC)
            T.wait(v_p, s_u3)
            t_p = mm(3, [(X1, PT)])
            V.wait(t_p)
            v_p = V(nc.vector.tensor_tensor(x(PT), full(3), x(PT), ALU.add))
            S.wait(t_r)
            s_r = copy(x(ZC), comp(2))
            if not last:
                V.wait(t_r)
                G.wait_apart(t_r)
                inputs(c + 1, grp)
            yield
            T.wait(v_p)
            t_m = mm(0, [(LO_, PT)])
            T.wait(s_r)
            t_z = mm(1, [(PT, ZC)], RC)
            S.wait(t_m)
            s_m = copy(x(X2), full(0))
            V.wait(t_z)
            v_z = V(nc.vector.tensor_copy(x(Z0), comp(1)))
            yield
            T.wait(s_m, v_z)
            zsrc = Z0
            for n, bank in enumerate((2, 3, 2)):
                t_z = mm(bank, [(X2, zsrc)], RC)
                V.wait(t_z)
                if n < 2:
                    v_z = V(nc.vector.tensor_tensor(x(ZC), comp(bank), x(Z0), ALU.add))
                else:
                    v_z = V(nc.vector.scalar_tensor_tensor(x(ZC), comp(bank), -1.0, x(Z0), ALU.mult, ALU.subtract))
                yield
                T.wait(v_z)
                zsrc = ZC
            S.wait(v_z)
            for r, q in halves:
                s_z = copy(LD[r, fs, q], ZC[r, fs, :])
            t_s = mm(0, [(AT_, ZC), (KT_, VC)], RC)
            mm_y = [(St, Rt), (LD, RAT), (VT_, RKT)]
            V.wait(t_s)
            V.seq(nc.vector.tensor_tensor(x(StC), x(StC), comp(0), ALU.add))
            v_s = V(nc.vector.tensor_tensor(x(StC), x(StC), eend[:, fs, ds(c, 1)].to_broadcast([P, 4, RC]), ALU.mult))
            T.wait(s_z)
            t_y = mm(3, mm_y, RC)
            yield
            S.wait(t_y)
            copy(R[:, fs, tok], comp(3))
            G.wait_apart(t_y, v_s)
            for r, q in halves:
                G(nc.gpsimd.tensor_copy(St[r, fs, q], StC[r, fs, :]))

        def barrier():
            toks = [l.tok() for l in self.lanes]
            for l in self.lanes:
                l.wait(*toks)
        for grp in range(2):
            inputs(0, grp)
        barrier()
        with self.loop(NRC - 1, "rwkv_chunks") as c:
            self.together((chunk(c, 0), 1), (chunk(c, 1), 1))
            barrier()
        self.together((chunk(NRC - 1, 0, True), 1), (chunk(NRC - 1, 1, True), 1))
        self.join()

    def rwkv_post(self):
        nc, T, V, S, i = self.nc, self.T, self.V, self.S, self.i
        PS, col, hs, bs = self.PS, self.col, self.hs, self.bs
        tt = lambda o, a, b, op: V.seq(nc.vector.tensor_tensor(o, a, b, op))
        R, VV = self.RKV[:, 0:8, :], self.RKV[:, 16:24, :]
        sg = self.LO[:, 2:4, :]
        GG, t1, g2 = self.view(14368, RP, SEQ), self.view(18464, RP, SEQ), self.view(20512, 2, RW)
        l2 = self.load(3, g2, i["rwkv_g2"][0].rearrange("(a p) n -> p a n", p=P))
        v4 = self.feat_view(4)
        self.head_sum(R, 4)
        t = T.tok()
        yield
        V.wait(t)
        v = V(nc.vector.tensor_scalar(hs, PS[0:16, 4, 0:SEQ], 1.0 / 64, None, ALU.mult))
        T.wait(v)
        self.head_bcast(hs, 4)
        t = T.tok()
        yield
        V.wait(t)
        v_r = tt(R, R, v4, ALU.subtract)
        v = tt(t1, R, R, ALU.mult)
        yield
        T.wait(v)
        self.head_sum(t1, 4)
        t = T.tok()
        yield
        V.wait(t)
        v = V(nc.vector.tensor_scalar(hs, PS[0:16, 4, 0:SEQ], 1.0 / 64, LN_EPS, ALU.mult, ALU.add))
        S.wait(v)
        s = S(nc.scalar.activation(hs, hs, ACT.Sqrt))
        T.wait(v)
        self.head_bcast(bs, 4)
        t = T.tok()
        yield
        V.wait(s)
        v_h = V.seq(nc.vector.reciprocal(hs, hs))
        tt(R, R, self.bc(col["rwkv_ln_w"], SEQ), ALU.mult)
        yield
        V.wait(t)
        v = tt(VV, v4, VV, ALU.mult)
        T.wait(v, v_h)
        self.head_bcast(hs, 4)
        t = T.tok()
        tt(VV, VV, self.bc(col["rwkv_ln_b"], SEQ), ALU.add)
        yield
        V.wait(t)
        v = tt(R, R, v4, ALU.mult)
        T.wait(v, l2)
        for f in range(RP):
            for k in range(2):
                t = T(nc.tensor.matmul(v4[:, f, :], g2[:, k, f * P:(f + 1) * P], sg[:, k, :],
                                       start=(f % 2 == 0 and k == 0), stop=k == 1, skip_group_check=True))
        tt(R, R, VV, ALU.add)
        yield
        V.wait(t)
        v = tt(R, R, v4, ALU.mult)
        yield
        S.wait(v)
        self.split(self.XH[:, 8:16, :], self.XL[:, 8:16, :], R)

    def softmax_rows(self, rows, st):
        nc, V, S = self.nc, self.V, self.S
        for q, (src, pr) in enumerate(rows):
            V(nc.vector.tensor_reduce(st[:, q:q + 1], src, AX.X, ALU.max))
        V.wait(V.tok())
        v = V(nc.vector.tensor_scalar(st[:, 2:4], st[:, 0:2], -1.0, None, ALU.mult))
        yield
        S.wait(v)
        for q, (src, pr) in enumerate(rows):
            s = S(nc.scalar.activation(pr, src, ACT.Exp, bias=st[:, 2 + q:3 + q], accum_out=st[:, 4 + q:5 + q]))
        yield
        V.wait(s)
        V.seq(nc.vector.reciprocal(st[:, 4:6], st[:, 4:6]))
        for q, (src, pr) in enumerate(rows):
            v = V(nc.vector.tensor_scalar(pr, pr, st[:, 4 + q:5 + q], None, ALU.mult))
        return v

    def heads(self, n, name, slots, head):
        with self.loop(n // slots, name) as i:
            self.together(*((head(slots * i + s, s), 1) for s in range(slots)))
            toks = [l.tok() for l in self.lanes]
            for l in self.lanes:
                l.wait(*toks)
        self.join()

    def cross(self):
        nc, T, V, S, G, i = self.nc, self.T, self.V, self.S, self.G, self.i
        PS, x = self.PS, self.x
        xn = self.view(0, NT, D)
        Qf, Kf, Vt = self.view(4112, KD, SEQ), self.view(8208, KD, SEQ), self.view(12304, NT, D)
        slots = [[self.view(o + k, *sh) for k, sh in
                  ((0, (4, SEQ)), (1024, (NT, XD)), (2048, (NT, SEQ)), (2560, (NT, SEQ)), (3072, (8,)))]
                 for o in (0, 16400)]
        t = self.load(4, Vt, i["mem"][0].rearrange("(t p) d -> p t d", p=P))
        feed = self.norm_feed(x, xn, self.col["norm_x_g"], 4)
        self.proj("xattn_q", i["xattn_wq"][0], 0, 4, "feat", lambda j, L: self.ev_feat(Qf, j, L), feed=feed)
        S.wait(t, S.tok())
        V.wait(self.squares(Vt, Kf.rearrange("p a b -> p (a b)").rearrange("p (a b) -> p a b", a=NT)))
        feed = self.norm_feed(Vt, Vt, self.col["norm_mem_g"], 1)
        for l in (S, V):
            l.wait((self.s_mm, CREDIT + 2 * self.tile_const))
        self.flush()
        self.proj("xattn_k", i["xattn_wk"][0], 0, 4, "feat", lambda j, L: self.ev_feat(Kf, j, L), feed=feed)
        self.proj("xattn_v", i["xattn_wv"][0], 0, 4, "tok", lambda j, L: self.ev_tok(Vt, j, L))
        self.join()

        def head(h, slot):
            Qs, Vs, pr, pT, st = slots[slot]
            b = 4 * slot
            s = S(nc.scalar.activation(Qs, Qf[:, ds(4 * h, 4), :], ACT.Copy, scale=float(XD) ** -0.5))
            g = G(nc.gpsimd.tensor_copy(Vs, Vt[:, :, ds(XD * h, XD)]))
            yield
            T.wait(s)
            sc = PS[:, b, :].rearrange("p (q m) -> p q m", q=NT)
            for q in range(NT):
                for k in range(4):
                    t = T(nc.tensor.matmul(sc[:, q, :], Qs[:, k, q * P:(q + 1) * P], Kf[:, ds(4 * h + k, 1), :],
                                           start=(q == 0 and k == 0), stop=k == 3, skip_group_check=True))
            V.wait(t)
            v = yield from self.softmax_rows([(sc[:, q, :], pr[:, q, :]) for q in range(NT)], st)
            yield
            T.wait(v)
            for m in range(NT):
                for q in range(NT):
                    t = T(nc.tensor.transpose(PS[:, b + 1, m * SEQ + q * P:m * SEQ + q * P + P],
                                              pr[:, q, m * P:(m + 1) * P], self.ident[:, :]))
            S.wait(t)
            s = S(nc.scalar.activation(pT, PS[:, b + 1, :].rearrange("p (m q) -> p m q", m=NT), ACT.Copy))
            yield
            T.wait(s, g)
            o = PS[:, b + 2:b + 4, :].rearrange("p a (f t) -> p (a f) t", t=SEQ)
            for f in range(4):
                for m in range(NT):
                    t = T(nc.tensor.matmul(o[:, f, :], Vs[:, m, f * P:(f + 1) * P], pT[:, m, :],
                                           start=(f % 2 == 0 and m == 0), stop=m == 1, skip_group_check=True))
            S.wait(t)
            self.split(self.XH[:, ds(4 * h, 4), :], self.XL[:, ds(4 * h, 4), :], o)
        self.heads(XH_, "xattn_heads", 2, head)
        self.proj("xattn_o", i["xattn_wo"][0], 0, 4, "tok", lambda j, L: self.ev_add(x, j, L, xn))
        self.join()

    def ffn1(self, AH, AL, xn, tmp, sq):
        nc, V, S, i, x = self.nc, self.V, self.S, self.i, self.x
        feed = self.norm_feed(x, xn, self.col["norm_ffn_g"], 4)
        w1, w2 = i["ffn_w1"][0], i["ffn_w2"][0]

        def ev(j, L):
            def evac(g, ps, ready, out):
                S.wait(ready, V.tok())
                self.done_evac(nc.scalar.activation(tmp, ps, ACT.Relu))
                yield
                V.wait(out)
                V.seq(nc.vector.tensor_tensor(sq, tmp, tmp, ALU.mult))
                yield
                d = ds(4 * (g * L + j), 4)
                S.wait(V.tok())
                S(nc.scalar.activation(AH[:, d, :], sq, ACT.Copy))
                yield
                V.wait(S.tok())
                V.seq(nc.vector.tensor_tensor(AL[:, d, :], sq, AH[:, d, :].bitcast(F32), ALU.subtract))
            return evac
        for part in range(4):
            self.proj(f"ffn1_up{part}", w1, 2048 * part, 4, "feat", ev, feed=feed)
            feed, junk = None, xn if part == 3 else None
            self.proj(f"ffn1_down{part}", w2, 0, 4, "tok", lambda j, L: self.ev_add(x, j, L, junk),
                      kt=16, k0=2048 * part, xh=AH, xl=AL, late=12)
        self.join()

    def final_norm(self, x, dst, gb, junk=None, store=None):
        nc, V, S = self.nc, self.V, self.S
        self.rstd(4)
        for tt in range(NT):
            v = V(nc.vector.scalar_tensor_tensor(dst[:, tt, :], x[:, tt, :], self.stat[:, tt:tt + 1], gb,
                                                 ALU.mult, ALU.mult))
            if store is not None:
                nc.sync.wait_ge(*v)
                nc.sync.dma_start(self.out[0][tt * P:(tt + 1) * P, :], dst[:, tt, :]).then_inc(store, 16)
            if junk is not None:
                S.wait(v)
                s = S(nc.scalar.activation(junk[:, tt, :], dst[:, tt, :], ACT.Square,
                                           accum_out=self.ssq[:, tt, 0:1]))
        V.wait(s if junk is not None else v)

    def hgrn(self):
        nc, T, V, S, G, i = self.nc, self.T, self.V, self.S, self.G, self.i
        PS, x = self.PS, self.x
        w = i["w_in_2"][0]
        tt = lambda o, a, b, op: V.seq(nc.vector.tensor_tensor(o, a, b, op))
        xn = self.view(0, NT, D)
        feed = self.norm_feed(x, xn, self.col["norm1_gain_2"], 1)
        Qa, Fa = self.view(0, GH, SEQ), self.view(2048, GH, SEQ)
        Ia, Ga = self.view(4096, NT, 1024), self.view(6144, NT, 1024)
        self.proj("w_in2_q", w, 0, 2, "feat", lambda j, L: self.ev_feat(Qa, j, L), feed=feed)
        self.proj("w_in2_f", w, 1024, 2, "feat", lambda j, L: self.ev_feat(Fa, j, L, ACT.Sigmoid))
        Qb, Kb, Vb = self.view(8192, GH, SEQ), self.view(10240, GH, SEQ), self.view(12288, NT, 1024)
        Fb = self.Fb = self.view(14336, NT, 8)
        self.Qb, self.Kb, self.Vb = Qb, Kb, Vb
        Kd, Ke, Bb = self.view(14376, GH, SEQ), self.view(16424, GH, SEQ), self.view(18472, GH, SEQ)
        dce = self.view(20520, GH, NRC)

        def ev_fb(g, ps, ready, out):
            S.wait(ready)
            self.done_evac(nc.scalar.activation(Fb, ps[:, :, 0:8], ACT.Copy))
            yield
        self.flush()
        V.wait((self.s_evac, CREDIT + self.blk_const))
        spec = lambda c0, mode, ev: [self.spec(w, mode, (lambda g, j=j: 512 * j + c0), ev(j, 2)) for j in range(2)]
        sp = [self.spec(w, "tok", lambda g: 7168, ev_fb, widths=[8])] + \
            spec(2048, "tok", lambda j, L: self.ev_tok(Ia, j, L)) + \
            spec(3072, "tok", lambda j, L: self.ev_tok(Ga, j, L, ACT.Silu))
        fb_there = (self.s_evac, CREDIT + self.blk_const + 1)

        def prep():
            yield from self.hgrn_prep(Qa, Fa, Kd, Ke, Bb, dce)
            yield from self.fox_prep(fb_there)
        self.together((self.stream("w_in2_rest", 1, sp, 2), 1), (prep(), 1))
        self.hgrn_heads(w, Qa, Ia, Ga, Kd, Ke, dce)

    def hgrn_prep(self, Qa, Fa, Kd, Ke, Bb, dce):
        nc, V, S = self.nc, self.V, self.S
        tt = lambda o, a, b, op: V.seq(nc.vector.tensor_tensor(o, a, b, op))
        lb = self.view(14352, 24)
        p = self.col["hgrn_lb_param_2"]
        L0, L1, LM = lb[:, 0:8], lb[:, 8:16], lb[:, 16:24]
        tt(LM, p[:, 0:8], p[:, 8:16], ALU.max)
        tt(L0, p[:, 0:8], LM, ALU.subtract)
        tt(L1, p[:, 8:16], LM, ALU.subtract)
        S.wait(V.tok())
        S.seq(nc.scalar.activation(lb[:, 0:16], lb[:, 0:16], ACT.Exp))
        V.wait(S.tok())
        tt(LM, L0, L1, ALU.add)
        V.seq(nc.vector.reciprocal(LM, LM))
        tt(L0, L0, LM, ALU.mult)
        V.seq(nc.vector.tensor_scalar(L1, L0, -1.0, 1.0, ALU.mult, ALU.add))
        tt(Kd, Fa, self.bc(L1, SEQ), ALU.mult)
        yield
        v = tt(Kd, Kd, self.bc(L0, SEQ), ALU.add)
        S.wait(v)
        s = S(nc.scalar.activation(Bb, Kd, ACT.Ln))
        yield
        V.wait(s)
        V(nc.vector.tensor_scalar(Kd, Kd, -1.0, 1.0, ALU.mult, ALU.add))
        for h in range(GH):
            v = V(nc.vector.tensor_tensor_scan(Fa[:, h, :], self.rst[:, :], Bb[:, h, :], 0.0, ALU.mult, ALU.add))
            if h % 2:
                yield
        V.wait(v)
        ch = lambda a: a.rearrange("p f (c e) -> p (f c) e", e=HCH)
        b_end = ch(Fa)[:, :, HCH - 1:HCH].to_broadcast([P, GH * NRC, HCH])
        v = tt(ch(Ke), b_end, ch(Fa), ALU.subtract)
        yield
        S.wait(v)
        S(nc.scalar.activation(Ke, Ke, ACT.Exp))
        s = S(nc.scalar.activation(Bb, Fa, ACT.Exp))
        yield
        S.wait(s)
        s2 = S(nc.scalar.activation(Fa, Fa, ACT.Exp, scale=-1.0))
        V.wait(s)
        tt(Ke, Ke, Kd, ALU.mult)
        yield
        V.wait(s2)
        tt(Kd, Kd, Fa, ALU.mult)
        yield
        V.seq(nc.vector.scalar_tensor_tensor(Qa, Qa, float(P) ** -0.5, Bb, ALU.mult, ALU.mult))
        V.seq(nc.vector.tensor_copy(dce, Bb.rearrange("p f (c e) -> p f c e", e=HCH)[:, :, :, HCH - 1]))

    def hgrn_heads(self, w, Qa, Ia, Ga, Kd, Ke, dce):
        nc, T, V, S, G = self.nc, self.T, self.V, self.S, self.G
        PS, Qb, Kb, Vb = self.PS, self.Qb, self.Kb, self.Vb
        slots = []
        for k in range(2):
            a, b, c = 2048 + 1024 * k, 18472 + 1024 * k, 20552 + 808 * k
            slots.append(dict(QZ=self.view(a, 4, P), KTe=self.view(a + 512, NT, P), KTo=self.view(a + 768, NT, P),
                              Kds=self.view(b, SEQ), Kes=self.view(b + 256, SEQ), AT=self.view(b + 512, NT, P),
                              O=self.view(b + 768, NT, P), Sn=self.view(c, 3, P), stt_=self.view(c + 384, 4),
                              dcs=self.view(c + 388, NRC), junk=self.view(c + 392, P)))
        self.join()
        for sl in slots:
            for b in ("QZ", "KTe", "KTo"):
                G(nc.gpsimd.memset(sl[b], 0.0))
        for l in (T, V, S, G):
            l.wait(G.tok())

        def head(h, slot):
            sl = slots[slot]
            QZ, KTe, KTo, Kds, Kes, AT, O, Sn, stt_, dcs, junk = (sl[n] for n in (
                "QZ", "KTe", "KTo", "Kds", "Kes", "AT", "O", "Sn", "stt_", "dcs", "junk"))
            ba, bb = 4 + 2 * slot, 5 + 2 * slot
            v3 = lambda b: PS[:, b, 0:SEQ].rearrange("p (q m) -> p q m", q=NT)
            hd, cols = ds(h, 1), ds(P * h, P)
            v_k = V(nc.vector.tensor_copy(Kds, Kd[:, hd, :]))
            g_e = G(nc.gpsimd.tensor_copy(Kes, Ke[:, hd, :]))
            g_d = G(nc.gpsimd.tensor_copy(dcs, dce[:, hd, :]))
            qv = Qa[:, hd, :].rearrange("p o (t c e) -> p (o t) c e", t=NT, c=2)
            for c in range(2):
                s_q = S(nc.scalar.activation(QZ.rearrange("p (t c) e -> p t c e", c=2)[:, :, c, c * 64:c * 64 + 64],
                                             qv[:, :, c, :], ACT.Copy))
            yield
            T.wait(v_k)
            for q in range(NT):
                t_a = T(nc.tensor.matmul(PS[:, ba, q * P:(q + 1) * P], Kds[:, q * P:(q + 1) * P],
                                         Qa[:, hd, q * P:(q + 1) * P], start=q == 0, stop=True,
                                         skip_group_check=True))
            T.wait(g_e)
            for q in range(NT):
                t = T(nc.tensor.transpose(PS[:, bb, q * P:(q + 1) * P], Kes[:, q * P:(q + 1) * P], self.ident[:, :]))
            V.wait(t_a)
            v_at = V(nc.vector.tensor_tensor(AT, v3(ba), self.rep(self.m_in[:, :], NT), ALU.mult))
            S.wait(t)
            S(nc.scalar.activation(KTe[0:64, :, :], v3(bb)[0:64], ACT.Copy))
            s = S(nc.scalar.activation(KTo[64:128, :, :], v3(bb)[64:128], ACT.Copy))
            yield
            T.wait(s)
            for n in range(3):
                t = T(nc.tensor.matmul(PS[:, bb, n * P:(n + 1) * P], (KTe, KTo)[n % 2][:, n // 2, :],
                                       Ia[:, n // 2, cols], start=n == 0, stop=True, skip_group_check=True))
            V.wait(t, g_d)
            V.seq(nc.vector.tensor_copy(Sn[:, 0, :], PS[:, bb, 0:P]))
            for n in (1, 2):
                v = V.seq(nc.vector.scalar_tensor_tensor(Sn[:, n, :], Sn[:, n - 1, :], dcs[:, n:n + 1],
                                                         PS[:, bb, n * P:(n + 1) * P], ALU.mult, ALU.add))
            yield
            T.wait(v, v_at, s_q)
            for q in range(NT):
                ops = [(AT[:, q, :], Ia[:, q, cols])] + [(QZ[:, n, :], Sn[:, n - 1, :])
                                                        for n in (2 * q, 2 * q + 1) if n > 0]
                for m, (a, b) in enumerate(ops):
                    t = T(nc.tensor.matmul(PS[:, ba, q * P:(q + 1) * P], a, b, start=(q == 0 and m == 0),
                                           stop=m == len(ops) - 1, skip_group_check=True))
            yield
            S.wait(t)
            for q in range(NT):
                s = S(nc.scalar.activation(junk, v3(ba)[:, q, :], ACT.Square, accum_out=stt_[:, q:q + 1]))
                S.wait(s)
            yield
            V.wait(s)
            v = V(nc.vector.tensor_scalar(stt_[:, 0:2], stt_[:, 0:2], 1.0 / P, EPS, ALU.mult, ALU.add))
            S.wait(v)
            s = S(nc.scalar.activation(stt_[:, 0:2], stt_[:, 0:2], ACT.Sqrt))
            yield
            V.wait(s)
            V.seq(nc.vector.reciprocal(stt_[:, 2:4], stt_[:, 0:2]))
            for q in range(NT):
                v = V(nc.vector.scalar_tensor_tensor(O[:, q, :], v3(ba)[:, q, :], stt_[:, 2 + q:3 + q],
                                                     Ga[:, q, cols], ALU.mult, ALU.mult))
            yield
            T.wait(v)
            for q in range(NT):
                t = T(nc.tensor.transpose(PS[:, bb, q * P:(q + 1) * P], O[:, q, :], self.ident[:, :]))
            S.wait_apart(t)
            S(nc.scalar.activation(Qa[:, hd, :], PS[:, bb, 0:SEQ], ACT.Copy, scale=self.col["hgrn_norm_gain_2"][:, 0:1]))

        def four_heads(i):
            for r in range(2):
                if r:
                    T.wait(V.tok(), S.tok())
                    V.wait(T.tok(), S.tok())
                    S.wait(T.tok(), V.tok())
                    G.wait(T.tok(), V.tok())
                pair = [head(4 * i + 2 * r + s, s) for s in range(2)]
                while pair:
                    for gen in list(pair):
                        if next(gen, self) is self:
                            pair.remove(gen)
                    yield
        specs = [self.spec(w, mode, (lambda g, c0=c0: 512 * g + c0), ev) for c0, mode, ev in (
            (4096, "feat", self.ev_feat(Qb, 0, 1)), (5120, "feat", self.ev_feat(Kb, 0, 1)),
            (6144, "tok", self.ev_tok(Vb, 0, 1)))]

        def three_blocks(i):
            self.par0 = 0
            T.wait((self.s_evac, CREDIT + self.blk()))
            prev = yield from self.blocks([(sp, i) for sp in specs], None, 2)
            yield from prev
        with self.loop(2, "hgrn_heads", 12, 3) as i:
            self.together((three_blocks(i), 1), (four_heads(i), 1))
            toks = [l.tok() for l in self.lanes]
            for l in self.lanes:
                l.wait(*toks)
        self.par0 = 0
        self.join()
        s = S(nc.scalar.activation(self.XH[:, 0:GH, :], Qa, ACT.Copy))
        V.wait(s)
        V(nc.vector.tensor_tensor(self.XL[:, 0:GH, :], Qa, self.XH[:, 0:GH, :].bitcast(F32), ALU.subtract))

    def fox_prep(self, there):
        nc, V, G, Fb = self.nc, self.V, self.G, self.Fb
        nlf, t = self.view(21072, NT, 8), [self.view(21088 + 16 * k, NT, 8) for k in range(3)]
        CU = self.view(21880, SEQ)
        self.nlf, self.CU = nlf, CU
        V.wait(there)
        V.seq(nc.vector.tensor_tensor(Fb, Fb, self.rep(self.fxb[:, :], NT), ALU.add))
        yield from self.log1p_exp_negabs(nlf, Fb, t)
        V.seq(nc.vector.tensor_scalar(t[0], Fb, 0.0, -1.0, ALU.min, ALU.mult))
        V.seq(nc.vector.tensor_tensor(nlf, nlf, t[0], ALU.add))
        G(nc.gpsimd.tensor_copy(CU[:, 0:P], self.triu[:, :]))
        G(nc.gpsimd.tensor_copy(CU[:, P:SEQ], self.ones[:, :]))

    def fox(self):
        nc, T, V, S, G = self.nc, self.T, self.V, self.S, self.G
        PS, nlf, CU = self.PS, self.nlf, self.CU
        slots = [[self.view(2368 + 1300 * k + o, *sh) for o, sh in
                  ((0, (3 * P,)), (384, (3 * P,)), (768, (8,)), (776, (SEQ,)), (1032, (NT, P)), (1288, (NT,)))]
                 for k in range(4)]
        def head(h, slot):
            pr, pT, st, Qs, Vs, nl = slots[slot]
            ba, bb = 2 * slot, 2 * slot + 1
            hd = ds(h, 1)
            s_q = S(nc.scalar.activation(Qs, self.Qb[:, hd, :], ACT.Copy, scale=float(P) ** -0.5))
            g_n = G(nc.gpsimd.tensor_copy(nl, nlf[:, :, hd]))
            g_v = G(nc.gpsimd.tensor_copy(Vs, self.Vb[:, :, ds(P * h, P)]))
            yield
            T.wait(s_q, g_n)
            sc, first = PS[:, ba, 0:3 * P], [True]

            def add(c0, n, lhs, rhs, stop=False):
                t = T(nc.tensor.matmul(sc[:, c0:c0 + n], lhs, rhs, start=first[0], stop=stop, skip_group_check=True))
                first[0] = False
                return t
            add(0, P, self.ident[:, :], self.negu[:, :])
            add(2 * P, P, self.ident[:, :], self.negu[:, :])
            n0, n1 = (nl[:, k:k + 1].to_broadcast([P, P]) for k in range(NT))
            add(0, P, n0, self.triu[:, :])
            add(P, 2 * P, n0, CU)
            add(2 * P, P, n1, self.triu[:, :])
            add(0, P, Qs[:, 0:P], self.Kb[:, hd, 0:P], True)
            t = add(P, 2 * P, Qs[:, P:SEQ], self.Kb[:, hd, :], True)
            V.wait(t)
            v = yield from self.softmax_rows([(sc[:, 0:P], pr[:, 0:P]), (sc[:, P:3 * P], pr[:, P:3 * P])], st)
            yield
            T.wait(v)
            for k in range(3):
                t = T(nc.tensor.transpose(PS[:, bb, k * P:(k + 1) * P], pr[:, k * P:(k + 1) * P], self.ident[:, :]))
            S.wait(t)
            s = S(nc.scalar.activation(pT, PS[:, bb, 0:3 * P], ACT.Copy))
            yield
            T.wait(s, g_v)
            T(nc.tensor.matmul(PS[:, ba, 0:SEQ], Vs[:, 0, :], pT[:, 0:SEQ], start=True, stop=False,
                               skip_group_check=True))
            t = T(nc.tensor.matmul(PS[:, ba, P:SEQ], Vs[:, 1, :], pT[:, SEQ:3 * P], start=False, stop=True,
                                   skip_group_check=True))
            S.wait(t)
            self.split(self.XH[:, ds(h + 8, 1), :], self.XL[:, ds(h + 8, 1), :], PS[:, ba, 0:SEQ])
        self.heads(GH, "fox_heads", 4, head)

    def ffn2(self, AH, AL, xn, buf, acc, tmp):
        nc, V, S, G, i, x = self.nc, self.V, self.S, self.G, self.i, self.x
        S.wait(G(nc.gpsimd.memset(buf[:, :, 0:2], 0.0)))
        V.wait(G.tok())
        feed = self.norm_feed(x, xn, self.col["norm2_gain_2"], 4)
        wg, wu, wd = i["w_ffn_gate_2"][0], i["w_ffn_up_2"][0], i["w_ffn_down_2"][0]
        cw, cb = self.fcw, self.col["ffn_conv_b_2"]
        done = 0
        for part, nb in enumerate((4, 4, 3)):

            def ev_gate(g, ps, ready, out):
                b = g + done
                S.wait(ready, V.tok())
                self.done_evac(nc.scalar.activation(buf[:, :, 2:2 + SEQ], ps, ACT.Copy))
                yield
                V.wait(out)
                for tap in range(3):
                    wt = self.bc(cw[:, tap, ds(4 * b, 4)], SEQ)
                    V.seq(nc.vector.tensor_tensor(tmp if tap else acc, buf[:, :, tap:tap + SEQ], wt, ALU.mult))
                    if tap:
                        yield
                        V.seq(nc.vector.tensor_tensor(acc, acc, tmp, ALU.add))
                    yield
                V.seq(nc.vector.tensor_tensor(acc, acc, self.bc(cb[:, ds(4 * b, 4)], SEQ), ALU.add))
                yield
                S.wait(V.tok())
                S(nc.scalar.activation(acc, acc, ACT.Silu))

            def ev_up(g, ps, ready, out):
                V.wait(ready, S.tok())
                V.seq(nc.vector.tensor_tensor(acc, acc, ps, ALU.mult))
                self.nc.vector.sem_inc(self.s_evac, 1)
                yield
                S.wait(V.tok())
                d = ds(4 * g, 4)
                S(nc.scalar.activation(AH[:, d, :], acc, ACT.Copy))
                yield
                V.wait(S.tok())
                V.seq(nc.vector.tensor_tensor(AL[:, d, :], acc, AH[:, d, :].bitcast(F32), ALU.subtract))
            c = lambda g: 512 * (g + done)
            self.run_now(self.stream(f"ffn2_up{part}", nb, [self.spec(wg, "feat", c, ev_gate),
                                                            self.spec(wu, "feat", c, ev_up)], feed=feed))
            feed, junk = None, xn if part == 2 else None
            self.proj(f"ffn2_down{part}", wd, 0, 4, "tok", lambda j, L: self.ev_add(x, j, L, junk),
                      kt=4 * nb, k0=512 * done, xh=AH, xl=AL, late=4 * nb - 4)
            done += nb
        self.join()

    def run(self, stop_at=None):
        nc, ctx, i, sb = self.nc, self.ctx, self.i, self.sb
        T, V, S = self.T, self.V, self.S
        constants = self.constants()
        next(constants)
        self.param_cols = sb("param_cols", [P, 113 + 124 + 128 + 72])
        self.stat, self.ssq = sb("stat", [P, 4]), sb("sum_of_squares", [P, NT, 4])
        self.x = sb("x", [P, NT, D])
        self.mul = sb("mu_lora", [P, 4])
        self.dtb, self.alog, self.dsk, self.fxb = (sb(n, [P, m]) for n, m in
                                                   (("dt_bias", 16), ("a_log", 16), ("d_skip", 16), ("fox_bias", 8)))
        self.low = 1
        self.arena_cm = self.open_arena("arena_a", 25920 - NT * D)
        self.x_in = self.view(12320, NT, D)
        XTOK = i["x"][0].rearrange("(t p) d -> p t d", p=P)
        for tt in range(NT):
            for h in (slice(0, 1024), slice(1024, 2048)):
                t = self.load(1, self.x_in[:, tt, h], XTOK[:, tt, h], (nc.sync, nc.scalar)[tt])
        self.params()
        p0 = self.param_rows(0)
        nc.sync.wait_ge(*t)
        S.wait(t)
        V.wait(t, self.squares(self.x_in, self.view(16416, NT, D)))
        T.wait(self.G.tok())
        S.wait(self.param_turn(0, 0, p0))
        V.wait(S.tok())

        def rest_of_params():
            rest = [self.param_rows(k) for k in (1, 2, 3)][-1]
            with nc.allow_non_contiguous_dma(reason="a few hundred values"):
                mu = i["rwkv_mu"][0].rearrange("(n a) -> n a", a=1)
                self.load(5, self.mul[0:LORA, 0:1], mu[3072:3072 + LORA, :], nc.sync)
                self.load(5, self.mul[0:LORA, 1:2], mu[3072 + LORA:3072 + 2 * LORA, :], nc.sync)
                for k in range(2):
                    self.load(5, self.mul[:, 2 + k:3 + k], mu[3264 + k * P:3264 + (k + 1) * P, :], nc.sync)
                for t, n, m in ((self.dtb, "ssd_dt_bias", 16), (self.alog, "ssd_a_log", 16), (self.dsk, "ssd_d", 16),
                                (self.fxb, "fox_gate_bias_2", 8)):
                    small = self.load(5, t[:, :], i[n].to_broadcast([P, m]), nc.sync)
            yield
            for k in (1, 2, 3):
                s = self.param_turn(k, 3 + k, rest)
            for l in (V, S, self.G):
                l.wait(s, small)
            yield
        self.rest_of_params = rest_of_params
        self.block1_in(constants)
        if stop_at == "in":
            return
        self.rwkv_views()
        self.together((self.ssd(), 1), (self.rwkv_prep(), 1))
        self.join()
        self.rwkv()
        if stop_at == "mix":
            return
        x = self.x
        x_there = []
        for l in self.lanes:
            nc.sync.wait_ge(*l.tok())
        xh, xl = self.XH, self.XL
        specs = lambda k0, junk: [self.spec(i["w_out"][0], "tok", (lambda g, j=j: 512 * j), self.ev_add(x, j, 4, junk, x_there),
                                            8, k0, xh[:, k0 // P:k0 // P + 8, :], xl[:, k0 // P:k0 // P + 8, :])
                                  for j in range(4)]

        def post():
            for n, _ in enumerate(self.rwkv_post()):
                if n == 1:
                    x_there.append(self.load(6, x[:, :, :], XTOK, nc.sync))
                yield
        self.together((self.stream("w_out_ssd", 1, specs(0, None), 2), 1), (post(), 1))
        T.wait(V.tok(), S.tok())
        self.run_now(self.stream("w_out_rwkv", 1, specs(1024, self.view(16416, NT, D))))
        self.join()
        self.low = 0
        self.arena_cm.close()
        cm = self.open_arena("arena_b", 22200)
        if stop_at == "w_out":
            return
        self.cross()
        if stop_at == "cross":
            return
        cm.close()

        def ffn_scope():
            c = self.scope = ExitStack()
            t = [c.enter_context(nc.sbuf_tensor(f"{n}{self.ffn_no}", s, d)) for n, s, d in (
                ("act_hi", [P, 16, SEQ], F32R), ("act_lo", [P, 16, SEQ], F32R), ("xn", [P, NT, D], F32),
                ("buf", [P, 4, SEQ + 2], F32), ("acc", [P, 4, SEQ], F32), ("tmp", [P, 4, SEQ], F32),
                ("final_gain", [P, D], F32))]
            self.ffn_no += 1
            return c, t
        self.ffn_no = 1
        c, (AH, AL, xn, buf, acc, tmp, gb) = ffn_scope()
        gain = lambda n: i[n].rearrange("(a n) -> a n", a=1).to_broadcast([P, D])
        t = self.load(7, gb[:, :], gain("final_norm_g"))
        self.ffn1(AH, AL, xn[:, :, :], tmp[:, :, :], acc[:, :, :])
        if stop_at == "ffn1":
            return
        V.wait(t)
        self.final_norm(self.x[:, :, :], self.x[:, :, :], gb[:, :], xn[:, :, :])
        c.close()
        cm = self.open_arena("arena_c", 22200)
        self.hgrn()
        self.fox()
        if stop_at == "mix2":
            return
        cm.close()
        c, (AH, AL, xn, buf, acc, tmp, gb) = ffn_scope()
        t = self.load(8, gb[:, :], gain("final_norm_gain_2"))
        self.proj("w_out2", i["w_out_2"][0], 0, 4, "tok", lambda j, L: self.ev_add(self.x, j, L, xn))
        self.join()
        self.ffn2(AH, AL, xn[:, :, :], buf[:, :, :], acc[:, :, :], tmp[:, :, :])
        V.wait(t)
        s_out = self.newsem("stored")
        self.final_norm(self.x[:, :, :], self.x[:, :, :], gb[:, :], store=s_out)
        nc.sync.wait_ge(s_out, 16 * NT)
        c.close()

    def open_arena(self, name, words):
        c = self.scope = ExitStack()
        self.arena = c.enter_context(self.nc.sbuf_tensor(name, [P, words], F32))
        self.arena_words = words
        return c


NAMES = ["x", "mem", "norm_mix_g", "w_in", "ssd_conv_w", "ssd_conv_b", "ssd_dt_bias", "ssd_a_log", "ssd_d",
         "ssd_norm_g", "rwkv_mu", "rwkv_w0", "rwkv_w2", "rwkv_a0", "rwkv_a2", "rwkv_g2", "rwkv_k_k", "rwkv_k_a",
         "rwkv_r_k", "rwkv_ln_w", "rwkv_ln_b", "w_out", "norm_x_g", "norm_mem_g", "xattn_wq", "xattn_wk",
         "xattn_wv", "xattn_wo", "norm_ffn_g", "ffn_w1", "ffn_w2", "final_norm_g", "norm1_gain_2", "w_in_2",
         "hgrn_lb_param_2", "hgrn_norm_gain_2", "fox_gate_bias_2", "w_out_2", "norm2_gain_2", "w_ffn_gate_2",
         "w_ffn_up_2", "ffn_conv_w_2", "ffn_conv_b_2", "w_ffn_down_2", "final_norm_gain_2"]


def program(nc, ins, out, stop_at=None):
    with ExitStack() as ctx:
        m = Model(nc, ctx, ins, out)
        m.run(stop_at)
        m.scope.close()
        return m


def kernel(**inputs):
    import numpy as np
    import concourse.bacc as bacc
    from concourse.bass_utils import run_bass_kernel_spmd

    nc = bacc.Bacc("TRN2", target_bir_lowering=False, num_devices=1)
    arrays, ins = {}, {}
    for name in NAMES:
        a = np.ascontiguousarray(inputs[name])
        arrays["in_" + name] = a
        ins[name] = nc.dram_tensor("in_" + name, a.shape, F32, kind="ExternalInput").ap()
    out = nc.dram_tensor("out", (1, SEQ, D), F32, kind="ExternalOutput").ap()
    program(nc, ins, out)
    r = run_bass_kernel_spmd(nc, [arrays], core_ids=[0])
    return r.results[0]["out"]
```
